# Optimizing a Trainium2 kernel written in Bass

```python
import jax, jax.numpy as jnp
from jax import lax
import numpy as np
import math

D_MODEL = 1024
BATCH = 1
SEQ = 512
DEPTH = 1

SSD_HEADS = 8
SSD_HEAD_DIM = 64
SSD_D = SSD_HEADS * SSD_HEAD_DIM
SSD_GROUPS = 2
SSD_STATE = 128
SSD_CONV = 4
SSD_CHUNK = 128
SSD_CONV_DIM = SSD_D + 2 * SSD_GROUPS * SSD_STATE
SSD_COLS = SSD_D + SSD_CONV_DIM + SSD_HEADS

RWKV_HEADS = 8
RWKV_HEAD_DIM = 64
RWKV_D = RWKV_HEADS * RWKV_HEAD_DIM
DECAY_LORA = 64
AAA_LORA = 64
GATE_LORA = 128
RWKV_COLS = 3 * RWKV_D + DECAY_LORA + AAA_LORA + GATE_LORA
RWKV_GN_EPS = 64e-5

D_MIX = SSD_D + RWKV_D
D_IN = SSD_COLS + RWKV_COLS

D_FF = 2816
FFN_CONV = 3
NORM_EPS = 1e-6


def _rms_norm(x, g):
    xf = x.astype(jnp.float32)
    y = xf * lax.rsqrt(jnp.mean(xf * xf, axis=-1, keepdims=True) + NORM_EPS)
    return (y * g.astype(jnp.float32)).astype(x.dtype)

def _causal_dwconv(x, w, b):
    K, C = w.shape
    y = lax.conv_general_dilated(
        x, w[:, None, :].astype(x.dtype), window_strides=(1,), padding=[(K - 1, 0)],
        dimension_numbers=("NWC", "WIO", "NWC"), feature_group_count=C)
    return y + b.astype(x.dtype)

def _token_shift(x):
    return jnp.pad(x, ((0, 0), (1, 0), (0, 0)))[:, :-1]

def _segsum(a):
    cs = jnp.cumsum(a, axis=-1)
    diff = cs[..., :, None] - cs[..., None, :]
    L = a.shape[-1]
    mask = jnp.tril(jnp.ones((L, L), dtype=bool))
    return jnp.where(mask, diff, -jnp.inf)

def _ssd_chunked(xh, dt, A, Bg, Cg):
    b, T, h, p = xh.shape
    g, n = Bg.shape[2], Bg.shape[3]
    c, L = T // SSD_CHUNK, SSD_CHUNK
    Bh = jnp.repeat(Bg, h // g, axis=2).reshape(b, c, L, h, n)
    Ch = jnp.repeat(Cg, h // g, axis=2).reshape(b, c, L, h, n)
    X = (xh * dt[..., None]).reshape(b, c, L, h, p)
    a = (dt * A).reshape(b, c, L, h).transpose(0, 3, 1, 2)
    a_cs = jnp.cumsum(a, axis=-1)
    decay_in = jnp.exp(_segsum(a))
    scores = jnp.einsum("bclhn,bcshn->bhcls", Ch, Bh)
    y_diag = jnp.einsum("bhcls,bcshp->bclhp", scores * decay_in, X)
    decay_states = jnp.exp(a_cs[..., -1:] - a_cs)
    states = jnp.einsum("bclhn,bhcl,bclhp->bchpn", Bh, decay_states, X)
    chunk_decay = jnp.pad(a_cs[..., -1], ((0, 0), (0, 0), (1, 0)))
    decay_chunk = jnp.exp(_segsum(chunk_decay))
    states_p = jnp.concatenate([jnp.zeros_like(states[:, :1]), states], axis=1)
    states_in = jnp.einsum("bhzc,bchpn->bzhpn", decay_chunk, states_p)[:, :-1]
    y_off = jnp.einsum("bclhn,bchpn,bhcl->bclhp", Ch, states_in, jnp.exp(a_cs))
    return (y_diag + y_off).reshape(b, T, h, p)

def _ssd_mixer(p, conv_w, conv_b, dt_bias, a_log, d_skip, norm_g):
    b, T, _ = p.shape
    z, xbc, dt = jnp.split(p, [SSD_D, SSD_D + SSD_CONV_DIM], axis=-1)
    xbc = jax.nn.silu(_causal_dwconv(xbc, conv_w.astype(jnp.float32), conv_b.astype(jnp.float32)))
    xs, Bm, Cm = jnp.split(xbc, [SSD_D, SSD_D + SSD_GROUPS * SSD_STATE], axis=-1)
    xh = xs.reshape(b, T, SSD_HEADS, SSD_HEAD_DIM)
    Bm = Bm.reshape(b, T, SSD_GROUPS, SSD_STATE)
    Cm = Cm.reshape(b, T, SSD_GROUPS, SSD_STATE)
    dt = jax.nn.softplus(dt + dt_bias.astype(jnp.float32))
    A = -jnp.exp(a_log.astype(jnp.float32))
    y = _ssd_chunked(xh, dt, A, Bm, Cm) + d_skip.astype(jnp.float32)[:, None] * xh
    y = y.reshape(b, T, SSD_D) * jax.nn.silu(z)
    y = y.reshape(b, T, SSD_GROUPS, SSD_D // SSD_GROUPS)
    y = y * lax.rsqrt(jnp.mean(y * y, axis=-1, keepdims=True) + NORM_EPS)
    return y.reshape(b, T, SSD_D) * norm_g.astype(jnp.float32)

def _rwkv7_scan(r, w, k, v, za, zb):
    b, T, h, n = r.shape

    def step(S, inp):
        r_t, w_t, k_t, v_t, a_t, b_t = inp
        sa = jnp.einsum("bhij,bhj->bhi", S, a_t)
        S = S * w_t[:, :, None, :] + sa[..., None] * b_t[:, :, None, :] + v_t[..., None] * k_t[:, :, None, :]
        return S, jnp.einsum("bhij,bhj->bhi", S, r_t)

    xs = tuple(jnp.moveaxis(t, 1, 0) for t in (r, w, k, v, za, zb))
    S0 = jnp.zeros((b, h, n, n), dtype=r.dtype)
    _, ys = lax.scan(step, S0, xs)
    return jnp.moveaxis(ys, 0, 1)

def _rwkv7_mixer(p, mu, w0, w2, a0, a2, g2, k_k, k_a, r_k, ln_w, ln_b):
    b, T, _ = p.shape
    f32 = lambda t: t.astype(jnp.float32)
    p = p + (_token_shift(p) - p) * f32(mu)
    i1 = RWKV_D
    i2 = i1 + DECAY_LORA
    i3 = i2 + RWKV_D
    i4 = i3 + RWKV_D
    i5 = i4 + AAA_LORA
    r, w_lo, k, v, a_lo, g_lo = jnp.split(p, [i1, i2, i3, i4, i5], axis=-1)
    w_log = -jax.nn.softplus(-(f32(w0) + jnp.tanh(w_lo) @ f32(w2))) - 0.5
    decay = jnp.exp(-jnp.exp(w_log))
    a = jax.nn.sigmoid(f32(a0) + a_lo @ f32(a2))
    g = jax.nn.sigmoid(g_lo) @ f32(g2)
    heads = lambda t: t.reshape(b, T, RWKV_HEADS, RWKV_HEAD_DIM)
    kk = heads(k * f32(k_k))
    kk = kk / jnp.maximum(jnp.sqrt(jnp.sum(kk * kk, axis=-1, keepdims=True)), 1e-12)
    k = k * (1.0 + (a - 1.0) * f32(k_a))
    rh, kh, vh, ah = heads(r), heads(k), heads(v), heads(a)
    y = _rwkv7_scan(rh, heads(decay), kh, vh, -kk, kk * ah)
    mean = jnp.mean(y, axis=-1, keepdims=True)
    var = jnp.mean(jnp.square(y - mean), axis=-1, keepdims=True)
    y = ((y - mean) * lax.rsqrt(var + RWKV_GN_EPS)).reshape(b, T, RWKV_D) * f32(ln_w) + f32(ln_b)
    bonus = jnp.sum(rh * kh * f32(r_k), axis=-1, keepdims=True) * vh
    return (y + bonus.reshape(b, T, RWKV_D)) * g

def first_inputs(seed: int = 0) -> dict:
    key = jax.random.key(seed)
    ks = jax.random.split(key, 32)
    nrm = lambda k, shape, s: jax.random.normal(k, shape, jnp.float32) * s
    L = DEPTH
    dt = jnp.exp(jax.random.uniform(ks[5], (L, SSD_HEADS), jnp.float32) * (np.log(0.1) - np.log(0.001)) + np.log(0.001))
    dt = jnp.clip(dt, 1e-4)
    return {
        "x": nrm(ks[0], (BATCH, SEQ, D_MODEL), 1.0),
        "pre_mix_norm": 1.0 + nrm(ks[1], (L, D_MODEL), 0.05),
        "w_in": nrm(ks[2], (L, D_MODEL, D_IN), D_MODEL ** -0.5),
        "ssd_conv_w": nrm(ks[3], (L, SSD_CONV, SSD_CONV_DIM), SSD_CONV ** -0.5),
        "ssd_conv_b": nrm(ks[4], (L, SSD_CONV_DIM), 0.02),
        "ssd_dt_bias": dt + jnp.log(-jnp.expm1(-dt)),
        "ssd_a_log": jnp.log(jax.random.uniform(ks[6], (L, SSD_HEADS), jnp.float32, 1.0, 16.0)),
        "ssd_d": 1.0 + nrm(ks[7], (L, SSD_HEADS), 0.1),
        "ssd_norm": 1.0 + nrm(ks[8], (L, SSD_D), 0.05),
        "rwkv_mu": jax.random.uniform(ks[9], (L, RWKV_COLS), jnp.float32),
        "rwkv_w0": jax.random.uniform(ks[10], (L, RWKV_D), jnp.float32, -6.0, 1.0),
        "rwkv_w2": nrm(ks[11], (L, DECAY_LORA, RWKV_D), 0.1 * DECAY_LORA ** -0.5),
        "rwkv_a0": nrm(ks[12], (L, RWKV_D), 0.1),
        "rwkv_a2": nrm(ks[13], (L, AAA_LORA, RWKV_D), 0.5 * AAA_LORA ** -0.5),
        "rwkv_g2": nrm(ks[14], (L, GATE_LORA, RWKV_D), GATE_LORA ** -0.5),
        "rwkv_k_k": 0.85 + nrm(ks[15], (L, RWKV_D), 0.05),
        "rwkv_k_a": 1.0 + nrm(ks[16], (L, RWKV_D), 0.05),
        "rwkv_r_k": nrm(ks[17], (L, RWKV_HEADS, RWKV_HEAD_DIM), 0.1),
        "rwkv_ln_w": 1.0 + nrm(ks[18], (L, RWKV_D), 0.05),
        "rwkv_ln_b": nrm(ks[19], (L, RWKV_D), 0.02),
        "w_out": nrm(ks[20], (L, D_MIX, D_MODEL), D_MIX ** -0.5),
        "post_mix_norm": 1.0 + nrm(ks[21], (L, D_MODEL), 0.05),
        "pre_ffn_norm": 1.0 + nrm(ks[22], (L, D_MODEL), 0.05),
        "ffn_w_up": nrm(ks[23], (L, D_MODEL, 2 * D_FF), D_MODEL ** -0.5),
        "ffn_conv_w": nrm(ks[24], (L, FFN_CONV, 2 * D_FF), FFN_CONV ** -0.5),
        "ffn_conv_b": nrm(ks[25], (L, 2 * D_FF), 0.02),
        "ffn_w_down": nrm(ks[26], (L, D_FF, D_MODEL), D_FF ** -0.5),
        "post_ffn_norm": 1.0 + nrm(ks[27], (L, D_MODEL), 0.05),
    }

def first_block(x, pre_mix_norm, w_in, ssd_conv_w, ssd_conv_b, ssd_dt_bias, ssd_a_log, ssd_d, ssd_norm,
              rwkv_mu, rwkv_w0, rwkv_w2, rwkv_a0, rwkv_a2, rwkv_g2, rwkv_k_k, rwkv_k_a, rwkv_r_k,
              rwkv_ln_w, rwkv_ln_b, w_out, post_mix_norm, pre_ffn_norm, ffn_w_up, ffn_conv_w,
              ffn_conv_b, ffn_w_down, post_ffn_norm):
    h = x
    for l in range(DEPTH):
        xn = _rms_norm(h, pre_mix_norm[l])
        proj = (xn @ w_in[l]).astype(jnp.float32)
        p_ssd, p_rwkv = jnp.split(proj, [SSD_COLS], axis=-1)
        y_ssd = _ssd_mixer(p_ssd, ssd_conv_w[l], ssd_conv_b[l], ssd_dt_bias[l], ssd_a_log[l],
                           ssd_d[l], ssd_norm[l])
        y_rwkv = _rwkv7_mixer(p_rwkv, rwkv_mu[l], rwkv_w0[l], rwkv_w2[l], rwkv_a0[l], rwkv_a2[l],
                              rwkv_g2[l], rwkv_k_k[l], rwkv_k_a[l], rwkv_r_k[l], rwkv_ln_w[l], rwkv_ln_b[l])
        mix = jnp.concatenate([y_ssd, y_rwkv], axis=-1).astype(h.dtype) @ w_out[l]
        h = h + _rms_norm(mix, post_mix_norm[l])
        hn = _rms_norm(h, pre_ffn_norm[l])
        u = _causal_dwconv(hn @ ffn_w_up[l], ffn_conv_w[l], ffn_conv_b[l])
        gate, val = jnp.split(u, 2, axis=-1)
        f = (jax.nn.silu(gate) * val) @ ffn_w_down[l]
        h = h + _rms_norm(f, post_ffn_norm[l])
    return h


D_BRANCH = 512
N_BRANCHES = 3
EPS = 1e-6
GMLP_CHUNK = 128
GMLP_GROUPS = 4
GMLP_GDIM = D_BRANCH // GMLP_GROUPS
GLA_HEADS = 4
GLA_DK = D_BRANCH // 2 // GLA_HEADS
GLA_DV = D_BRANCH // GLA_HEADS
GLA_GATE_RANK = 16
GLA_GATE_TAU = 16.0
GLA_CHUNK = 64
DSA_HEADS = 4
DSA_HDIM = D_BRANCH // DSA_HEADS
DSA_IDX_HEADS = 4
DSA_IDX_DIM = 64
DSA_QBLOCK = 128
DSA_TOPK_MAX = 256
N_BUCKETS = 32
MAX_DISTANCE = 128
N_GROUPS = 4
EXPERTS_PER_GROUP = 4
N_EXPERTS = N_GROUPS * EXPERTS_PER_GROUP
D_EXPERT = 256
TOPK_IN_GROUP = 2

IN_SIZES = (
    D_BRANCH, D_BRANCH,
    GLA_HEADS * GLA_DK, GLA_HEADS * GLA_DK,
    GLA_HEADS * GLA_DV, GLA_HEADS * GLA_DV,
    GLA_GATE_RANK,
    DSA_HEADS * DSA_HDIM, DSA_HEADS * DSA_HDIM, DSA_HEADS * DSA_HDIM,
    DSA_IDX_HEADS * DSA_IDX_DIM, DSA_IDX_DIM, DSA_IDX_HEADS,
    N_BRANCHES * D_MODEL,
)
N_IN = sum(IN_SIZES)


def rms_norm(x, g):
    xf = x.astype(jnp.float32)
    y = xf * lax.rsqrt(jnp.mean(xf * xf, axis=-1, keepdims=True) + EPS)
    return (y * g.astype(jnp.float32)).astype(x.dtype)

def layer_norm(x, g, b):
    xf = x.astype(jnp.float32)
    mu = jnp.mean(xf, axis=-1, keepdims=True)
    var = jnp.mean(jnp.square(xf - mu), axis=-1, keepdims=True)
    y = (xf - mu) * lax.rsqrt(var + EPS)
    return (y * g.astype(jnp.float32) + b.astype(jnp.float32)).astype(x.dtype)

def t5_bucket(rel):
    n = jnp.maximum(rel, 0)
    max_exact = N_BUCKETS // 2
    large = max_exact + (
        jnp.log(jnp.maximum(n, max_exact).astype(jnp.float32) / max_exact)
        / math.log(MAX_DISTANCE / max_exact) * (N_BUCKETS - max_exact)
    ).astype(jnp.int32)
    large = jnp.minimum(large, N_BUCKETS - 1)
    return jnp.where(n < max_exact, n, large)

def gmlp_branch(u, v, ln_g, ln_b, w_s, b_s):
    bsz, s, _ = v.shape
    v = layer_norm(v, ln_g, ln_b)
    vc = v.reshape(bsz, s // GMLP_CHUNK, GMLP_CHUNK, GMLP_GROUPS, GMLP_GDIM)
    causal = jnp.tril(jnp.ones((GMLP_CHUNK, GMLP_CHUNK), dtype=bool))
    w = jnp.where(causal[None], w_s, jnp.zeros_like(w_s))
    mixed = jnp.einsum('gts,bcsgd->bctgd', w, vc) + b_s.T[:, :, None]
    return u * mixed.reshape(bsz, s, D_BRANCH)

def gla_scan(q, k, v, g):
    bsz, s, h, _ = q.shape
    out_dtype = v.dtype
    q = q.astype(jnp.float32) * (GLA_DK ** -0.5)

    def to_chunks(t):
        t = t.astype(jnp.float32)
        return t.reshape(bsz, s // GLA_CHUNK, GLA_CHUNK, h, t.shape[-1]).transpose(1, 0, 3, 2, 4)

    causal = jnp.tril(jnp.ones((GLA_CHUNK, GLA_CHUNK), dtype=bool))[None, None, :, :, None]

    def step(state, inp):
        qc, kc, vc, gc = inp
        b = jnp.cumsum(gc, axis=2)
        b_last = b[:, :, -1:, :]
        o_inter = jnp.einsum('bhtd,bhde->bhte', qc * jnp.exp(b), state)
        diff = b[:, :, :, None, :] - b[:, :, None, :, :]
        decay = jnp.where(causal, jnp.exp(jnp.minimum(diff, 0.0)), 0.0)
        attn = jnp.einsum('bhtd,bhsd,bhtsd->bhts', qc, kc, decay)
        o = o_inter + jnp.einsum('bhts,bhse->bhte', attn, vc)
        new_state = (jnp.exp(b_last[:, :, 0, :])[..., None] * state
                     + jnp.einsum('bhsd,bhse->bhde', kc * jnp.exp(b_last - b), vc))
        return new_state, o

    state0 = jnp.zeros((bsz, h, GLA_DK, GLA_DV), jnp.float32)
    _, o = lax.scan(step, state0, (to_chunks(q), to_chunks(k), to_chunks(v), to_chunks(g)))
    return o.transpose(1, 0, 3, 2, 4).reshape(bsz, s, h, GLA_DV).astype(out_dtype)

def dsa_attention(q, k, v, iq, ik, iw, rel_bias):
    bsz, s, h, hd = q.shape
    n_blocks = s // DSA_QBLOCK
    topk = min(DSA_TOPK_MAX, s // 4)
    key_pos = jnp.arange(s, dtype=jnp.int32)
    gather = jax.vmap(lambda arr, idx: arr[idx])

    def block(i):
        start = i * DSA_QBLOCK
        qb = lax.dynamic_slice_in_dim(q, start, DSA_QBLOCK, axis=1)
        iqb = lax.dynamic_slice_in_dim(iq, start, DSA_QBLOCK, axis=1)
        iwb = lax.dynamic_slice_in_dim(iw, start, DSA_QBLOCK, axis=1)
        qpos = start + jnp.arange(DSA_QBLOCK, dtype=jnp.int32)
        raw = jnp.einsum('bthd,bsd->bths', iqb, ik)
        score = jnp.einsum('bths,bth->bts', jax.nn.relu(raw), iwb).astype(jnp.float32)
        admissible = key_pos[None, :] <= qpos[:, None]
        score = jnp.where(admissible[None], score, -jnp.inf)
        _, top_idx = lax.top_k(score, topk)
        valid = top_idx <= qpos[None, :, None]
        kg = gather(k, top_idx)
        vg = gather(v, top_idx)
        logits = jnp.einsum('bthd,btkhd->btkh', qb, kg).astype(jnp.float32) * (hd ** -0.5)
        bias = rel_bias[t5_bucket(qpos[None, :, None] - top_idx)].astype(jnp.float32)
        logits = jnp.where(valid[..., None], logits + bias, -1e30)
        p = jax.nn.softmax(logits, axis=2).astype(v.dtype)
        return jnp.einsum('btkh,btkhd->bthd', p, vg)

    out = lax.map(block, jnp.arange(n_blocks))
    return out.transpose(1, 0, 2, 3, 4).reshape(bsz, s, h * hd)

def hybrid_mixer(h, w_in, gmlp_ln_g, gmlp_ln_b, gmlp_w_s, gmlp_b_s, gla_w_gate2, gla_b_gate,
                 gla_norm_g, dsa_qnorm_g, dsa_knorm_g, rel_bias, w_branch, b_branch_gate, w_out):
    bsz, s, _ = h.shape
    proj = h @ w_in
    splits = np.cumsum(IN_SIZES)[:-1].tolist()
    (a_u, a_v, g_q, g_k, g_v, g_r, g_a, d_q, d_k, d_v, d_iq, d_ik, d_iw, gates) = jnp.split(
        proj, splits, axis=-1)

    y_a = gmlp_branch(jax.nn.gelu(a_u), jax.nn.gelu(a_v), gmlp_ln_g, gmlp_ln_b, gmlp_w_s, gmlp_b_s)

    log_alpha = jax.nn.log_sigmoid((g_a @ gla_w_gate2 + gla_b_gate).astype(jnp.float32)) / GLA_GATE_TAU
    o_b = gla_scan(g_q.reshape(bsz, s, GLA_HEADS, GLA_DK), g_k.reshape(bsz, s, GLA_HEADS, GLA_DK),
                   g_v.reshape(bsz, s, GLA_HEADS, GLA_DV),
                   log_alpha.reshape(bsz, s, GLA_HEADS, GLA_DK))
    o_b = rms_norm(o_b, gla_norm_g) * jax.nn.silu(g_r.reshape(bsz, s, GLA_HEADS, GLA_DV))
    y_b = o_b.reshape(bsz, s, D_BRANCH)

    q = rms_norm(d_q.reshape(bsz, s, DSA_HEADS, DSA_HDIM), dsa_qnorm_g)
    k = rms_norm(d_k.reshape(bsz, s, DSA_HEADS, DSA_HDIM), dsa_knorm_g)
    y_c = dsa_attention(q, k, d_v.reshape(bsz, s, DSA_HEADS, DSA_HDIM),
                        d_iq.reshape(bsz, s, DSA_IDX_HEADS, DSA_IDX_DIM), d_ik, d_iw, rel_bias)

    ys = jnp.stack([y_a, y_b.astype(y_a.dtype), y_c.astype(y_a.dtype)], axis=0)
    up = jnp.einsum('nbse,ned->bsnd', ys, w_branch)
    gate = jax.nn.sigmoid(gates.reshape(bsz, s, N_BRANCHES, D_MODEL) + b_branch_gate)
    merged = jnp.sum(gate * up, axis=2)
    return (merged @ w_out).astype(h.dtype)

def hier_moe(h, w_group, b_group, w_router, b_router, w_exp_gate, w_exp_up, w_exp_down):
    bsz, s, d = h.shape
    hf = h.reshape(-1, d)
    grp_prob = jax.nn.softmax((hf @ w_group + b_group).astype(jnp.float32), axis=-1)
    p_g, g_idx = lax.top_k(grp_prob, 1)
    g_onehot = jax.nn.one_hot(g_idx[:, 0], N_GROUPS, dtype=jnp.float32)
    exp_logits = (hf @ w_router + b_router).astype(jnp.float32).reshape(-1, N_GROUPS, EXPERTS_PER_GROUP)
    sel_logits = jnp.einsum('tge,tg->te', exp_logits, g_onehot)
    top_vals, e_idx = lax.top_k(sel_logits, TOPK_IN_GROUP)
    weights = p_g * jax.nn.softmax(top_vals, axis=-1)
    eid = g_idx * EXPERTS_PER_GROUP + e_idx
    combine = jnp.einsum('tk,tke->te', weights,
                         jax.nn.one_hot(eid, N_EXPERTS, dtype=jnp.float32)).astype(hf.dtype)
    y = jnp.zeros_like(hf)
    for gi in range(N_GROUPS):
        sl = slice(gi * EXPERTS_PER_GROUP, (gi + 1) * EXPERTS_PER_GROUP)
        hg = jnp.einsum('td,edf->etf', hf, w_exp_gate[sl])
        hu = jnp.einsum('td,edf->etf', hf, w_exp_up[sl])
        act = jax.nn.silu(hg) * hu * combine[:, sl].T[:, :, None]
        y = y + jnp.einsum('etf,efd->td', act, w_exp_down[sl]).astype(hf.dtype)
    return y.reshape(bsz, s, d)

def second_inputs(seed: int = 0) -> dict:
    key = jax.random.key(seed)
    ks = jax.random.split(key, 28)
    L = DEPTH

    def nrm(k, shape, scale):
        return jax.random.normal(k, shape, jnp.float32) * scale

    return {
        "x": nrm(ks[0], (BATCH, SEQ, D_MODEL), 1.0),
        "c": nrm(ks[1], (BATCH, D_MODEL), 1.0),
        "w_mod": nrm(ks[2], (L, D_MODEL, 6 * D_MODEL), 0.5 * D_MODEL ** -0.5),
        "b_mod": nrm(ks[3], (L, 6 * D_MODEL), 0.02),
        "g_norm1": 1.0 + nrm(ks[4], (L, D_MODEL), 0.1),
        "g_norm2": 1.0 + nrm(ks[5], (L, D_MODEL), 0.1),
        "w_in": nrm(ks[6], (L, D_MODEL, N_IN), D_MODEL ** -0.5),
        "gmlp_ln_g": 1.0 + nrm(ks[7], (L, D_BRANCH), 0.1),
        "gmlp_ln_b": nrm(ks[8], (L, D_BRANCH), 0.02),
        "gmlp_w_s": nrm(ks[9], (L, GMLP_GROUPS, GMLP_CHUNK, GMLP_CHUNK), GMLP_CHUNK ** -0.5),
        "gmlp_b_s": 1.0 + nrm(ks[10], (L, GMLP_GROUPS, GMLP_CHUNK), 0.1),
        "gla_w_gate2": nrm(ks[11], (L, GLA_GATE_RANK, GLA_HEADS * GLA_DK), GLA_GATE_RANK ** -0.5),
        "gla_b_gate": nrm(ks[12], (L, GLA_HEADS * GLA_DK), 0.1),
        "gla_norm_g": 1.0 + nrm(ks[13], (L, GLA_DV), 0.1),
        "dsa_qnorm_g": 1.0 + nrm(ks[14], (L, DSA_HDIM), 0.1),
        "dsa_knorm_g": 1.0 + nrm(ks[15], (L, DSA_HDIM), 0.1),
        "rel_bias": nrm(ks[16], (N_BUCKETS, DSA_HEADS), 0.5),
        "w_branch": nrm(ks[17], (L, N_BRANCHES, D_BRANCH, D_MODEL), D_BRANCH ** -0.5),
        "b_branch_gate": nrm(ks[18], (L, N_BRANCHES, D_MODEL), 0.1),
        "w_out": nrm(ks[19], (L, D_MODEL, D_MODEL), D_MODEL ** -0.5),
        "w_group": nrm(ks[20], (L, D_MODEL, N_GROUPS), D_MODEL ** -0.5),
        "b_group": nrm(ks[21], (L, N_GROUPS), 0.01),
        "w_router": nrm(ks[22], (L, D_MODEL, N_EXPERTS), D_MODEL ** -0.5),
        "b_router": nrm(ks[23], (L, N_EXPERTS), 0.01),
        "w_exp_gate": nrm(ks[24], (L, N_EXPERTS, D_MODEL, D_EXPERT), D_MODEL ** -0.5),
        "w_exp_up": nrm(ks[25], (L, N_EXPERTS, D_MODEL, D_EXPERT), D_MODEL ** -0.5),
        "w_exp_down": nrm(ks[26], (L, N_EXPERTS, D_EXPERT, D_MODEL), D_EXPERT ** -0.5),
    }

def second_block(x, c, w_mod, b_mod, g_norm1, g_norm2, w_in, gmlp_ln_g, gmlp_ln_b, gmlp_w_s, gmlp_b_s,
              gla_w_gate2, gla_b_gate, gla_norm_g, dsa_qnorm_g, dsa_knorm_g, rel_bias, w_branch,
              b_branch_gate, w_out, w_group, b_group, w_router, b_router, w_exp_gate, w_exp_up,
              w_exp_down):
    c_act = jax.nn.silu(c)
    for l in range(DEPTH):
        mod = c_act @ w_mod[l] + b_mod[l]
        sh1, sc1, gt1, sh2, sc2, gt2 = [m[:, None, :] for m in jnp.split(mod, 6, axis=-1)]
        h = rms_norm(x, g_norm1[l]) * (1.0 + sc1) + sh1
        mix = hybrid_mixer(h, w_in[l], gmlp_ln_g[l], gmlp_ln_b[l], gmlp_w_s[l], gmlp_b_s[l],
                           gla_w_gate2[l], gla_b_gate[l], gla_norm_g[l], dsa_qnorm_g[l],
                           dsa_knorm_g[l], rel_bias, w_branch[l], b_branch_gate[l], w_out[l])
        x = (x + gt1 * mix).astype(x.dtype)
        h2 = rms_norm(x, g_norm2[l]) * (1.0 + sc2) + sh2
        ffn = hier_moe(h2, w_group[l], b_group[l], w_router[l], b_router[l],
                       w_exp_gate[l], w_exp_up[l], w_exp_down[l])
        x = (x + gt2 * ffn).astype(x.dtype)
    return x


def setup_inputs(seed=0):
    out = dict(first_inputs(seed))
    for name, value in second_inputs(seed + 1).items():
        if name != "x":
            out[name + "_2"] = value
    return out


def reference(
    x, pre_mix_norm, w_in, ssd_conv_w, ssd_conv_b, ssd_dt_bias, ssd_a_log, ssd_d, ssd_norm,
    rwkv_mu, rwkv_w0, rwkv_w2, rwkv_a0, rwkv_a2, rwkv_g2, rwkv_k_k, rwkv_k_a, rwkv_r_k,
    rwkv_ln_w, rwkv_ln_b, w_out, post_mix_norm, pre_ffn_norm, ffn_w_up, ffn_conv_w, ffn_conv_b,
    ffn_w_down, post_ffn_norm, c_2, w_mod_2, b_mod_2, g_norm1_2, g_norm2_2, w_in_2, gmlp_ln_g_2,
    gmlp_ln_b_2, gmlp_w_s_2, gmlp_b_s_2, gla_w_gate2_2, gla_b_gate_2, gla_norm_g_2,
    dsa_qnorm_g_2, dsa_knorm_g_2, rel_bias_2, w_branch_2, b_branch_gate_2, w_out_2, w_group_2,
    b_group_2, w_router_2, b_router_2, w_exp_gate_2, w_exp_up_2, w_exp_down_2,
):
    x = first_block(
        x, pre_mix_norm, w_in, ssd_conv_w, ssd_conv_b, ssd_dt_bias, ssd_a_log, ssd_d, ssd_norm,
        rwkv_mu, rwkv_w0, rwkv_w2, rwkv_a0, rwkv_a2, rwkv_g2, rwkv_k_k, rwkv_k_a, rwkv_r_k,
        rwkv_ln_w, rwkv_ln_b, w_out, post_mix_norm, pre_ffn_norm, ffn_w_up, ffn_conv_w,
        ffn_conv_b, ffn_w_down, post_ffn_norm,
    )
    return second_block(
        x, c_2, w_mod_2, b_mod_2, g_norm1_2, g_norm2_2, w_in_2, gmlp_ln_g_2, gmlp_ln_b_2,
        gmlp_w_s_2, gmlp_b_s_2, gla_w_gate2_2, gla_b_gate_2, gla_norm_g_2, dsa_qnorm_g_2,
        dsa_knorm_g_2, rel_bias_2, w_branch_2, b_branch_gate_2, w_out_2, w_group_2, b_group_2,
        w_router_2, b_router_2, w_exp_gate_2, w_exp_up_2, w_exp_down_2,
    )


_drawn_inputs = setup_inputs


def setup_inputs(seed=0):
    import zlib

    import numpy as np

    out = dict(_drawn_inputs(seed))
    spreads = {}
    factors = {'ssd_conv_b': 2.832,
     'rwkv_w2': 8.0,
     'rwkv_a0': 3.484,
     'rwkv_k_k': 3.451,
     'rwkv_ln_w': 3.072,
     'rwkv_ln_b': 6.892,
     'ffn_conv_b': 3.131,
     'b_mod_2': 4.463,
     'g_norm1_2': 3.131,
     'g_norm2_2': 3.572,
     'gmlp_ln_g_2': 8.0,
     'gmlp_ln_b_2': 27.74,
     'gmlp_b_s_2': 7.537,
     'gla_w_gate2_2': 4.394,
     'gla_b_gate_2': 8.0,
     'gla_norm_g_2': 8.0,
     'dsa_qnorm_g_2': 8.0,
     'dsa_knorm_g_2': 8.0,
     'rel_bias_2': 7.124,
     'b_branch_gate_2': 8.0,
     'b_group_2': 33.08,
     'b_router_2': 37.333}
    for name, (base, spread) in spreads.items():
        noise = np.random.default_rng([zlib.crc32(name.encode()), seed]).standard_normal(out[name].shape)
        drawn = base * np.exp(spread * noise) if base else spread * noise
        out[name] = __import__('jax').numpy.asarray(drawn.astype(out[name].dtype))
    for name, factor in factors.items():
        out[name] = (out[name] * factor).astype(out[name].dtype)
    return out
```

```python
from contextlib import ExitStack

import numpy as np
import concourse.bass as bass
from concourse import mybir

F32 = mybir.dt.float32
ALU = mybir.AluOpType
ACT = mybir.ActivationFunctionType
AX = mybir.AxisListType

T = 512
P = 128
NT = T // P
D = 1024
KT = D // P
UNIT = 2048
RING = 3
PADW = 516
D_FF = 2816
NF = D_FF // 256
NE = 16
N_MOD = 6 * D // 256
CH = 64
NC = T // CH
EXP_HALF = 0.6065306597126334
LOG1P_TERMS = 7

XS, BM, CM, DT, WA, GL, RR, KK_, VV, ZZ, N_PROJ = 0, 4, 6, 8, 9, 10, 11, 15, 19, 23, 28
AU, AV, GQ, GK, GV, GR, MISC, DQ, DK, DV, IQ, IK = 0, 4, 8, 10, 12, 16, 20, 21, 25, 29, 33, 35


def layout(sizes):
    at, out = 0, {}
    for name, width in sizes:
        out[name] = (at, width)
        at += width
    return out, at


CONSTS, N_CONST = layout(
    [("ident", P), ("ones", P), ("blk64", P), ("flip", P), ("strict64", P), ("incl64", P), ("incl128", P),
     ("level0t", P)] + [(f"level{k}", P) for k in range(7)] +
    [("carry64", T), ("carry128", T), ("sel16", NE * P), ("bucket", 2 * T), ("neg128", P)])
SMALL, N_SMALL = layout(
    [("g_pre_mix", KT), ("g_post_mix", KT), ("g_pre_ffn", KT), ("g_post_ffn", KT),
     ("conv_w", 4 * 8), ("conv_b", 8), ("dt_bias", 1), ("a_log", 1), ("d_skip", 4), ("ssd_norm", 4),
     ("mu", 14), ("w0", 4), ("a0", 4), ("k_k", 4), ("k_a", 4), ("r_k", 4), ("ln_w", 4), ("ln_b", 4),
     ("c", KT), ("b_mod", 48), ("g1", KT), ("g2", KT), ("gmlp_g", 4), ("gmlp_b", 4),
     ("b_gate", 2), ("gla_g", 1), ("q_g", 1), ("k_g", 1), ("b_branch", 24),
     ("b_route", 20), ("rel_bias", 4), ("ffn_conv", 16 * NF)])
MATS, N_MATS = layout(
    [("wa2", T), ("g2m", T), ("gate2", 256), ("w_s", 4 * P), ("b_s", T), ("w_route", KT * 20)])
C0, S0, M0 = 0, N_CONST, N_CONST + N_SMALL
N_FIX = N_CONST + N_SMALL + N_MATS


def build(nc, units, fixed, x, skew, out, dbg=None, stop=99):
    ctx = ExitStack()
    with ctx:
        ring = ctx.enter_context(nc.sbuf_tensor("weight_ring", [P, RING, UNIT], F32))
        fix = ctx.enter_context(nc.sbuf_tensor("fixed_data", [P, N_FIX], F32))
        res = ctx.enter_context(nc.sbuf_tensor("residual", [P, KT, T], F32))
        xn = ctx.enter_context(nc.sbuf_tensor("normed", [P, KT, T], F32))
        tiny = ctx.enter_context(nc.sbuf_tensor("tiny", [P, 1024], F32))
        n_arena = 28200
        arena = ctx.enter_context(nc.sbuf_tensor("arena", [P, n_arena], F32))
        ps = ctx.enter_context(nc.psum_tensor("psum", [P, 8, T], F32))

        sems = {}

        def sem(name):
            if name not in sems:
                sems[name] = ctx.enter_context(nc.semaphore(name))
            return sems[name]

        def C(name, rows=P, a=0, b=None):
            o, w = CONSTS[name]
            return fix[0:rows, C0 + o + a:C0 + o + (w if b is None else b)]

        def S(name, j=0, n=1, rows=P):
            o, _ = SMALL[name]
            return fix[0:rows, S0 + o + j:S0 + o + j + n]

        def M(name, r0=0, r1=P, a=0, b=None):
            o, w = MATS[name]
            return fix[r0:r1, M0 + o + a:M0 + o + (w if b is None else b)]

        def A(off, n=T, r0=0, r1=P):
            assert off + n <= n_arena, (off, n, n_arena)
            return arena[r0:r1, off:off + n]

        def four(ap):
            return ap.rearrange("p (a b) -> p a b", a=4)

        def rep4(ap):
            return ap.unsqueeze(1).to_broadcast([ap.shape[0], 4, ap.shape[1]])

        full = [sem(f"bank{b}_full") for b in range(8)]
        free = [sem(f"bank{b}_free") for b in range(8)]
        used = [0] * 8
        place = {}

        def bank_of(what, k=0):
            return place[what, k][0]

        def filled(eng, what, k=0, it=None):
            b, n, per = place[what, k]
            eng.wait_ge(full[b], n + 1 if it is None else it * per + (n + 1))

        def emptied(eng, what, k=0, it=None):
            b, n, per = place[what, k]
            eng.wait_ge(free[b], n + 1 if it is None else it * per + (n + 1))

        def freed(what, k=0):
            return free[place[what, k][0]]

        class Chain:

            def __init__(self, eng, name):
                self.eng, self.sem, self.n, self.it, self.per = eng, sem(name), 0, None, 0

            def link(self, ins):
                self.n += 1
                ins.then_inc(self.sem, 1)
                self.eng.wait_ge(self.sem, self.n if self.it is None else self.it * self.per + self.n)

            def enter(self, it, per):
                self.it, self.per, self.at = it, per, self.n

            def leave(self, times):
                assert self.n - self.at == self.per, (self.n - self.at, self.per)
                self.n = self.at + self.per * times
                self.it = None

        PROJ = 0
        YM = N_PROJ * PADW
        WK = YM + 8 * T

        def proj(t, r0=0, r1=P, shift=0):
            return A(PROJ + t * PADW + 3 - shift, T, r0, r1)

        def ym(t, r0=0, r1=P):
            return A(YM + t * T, T, r0, r1)

        XT = PROJ
        SQ = WK
        s_XD, s_XS2, s_BT, s_SI, s_GT, s_HB, s_CE, s_TC = [
            WK + o for o in (0, 2048, 4096, 5120, -1024, 6656, 7680, 8704)]
        def ew(i, r0=0, r1=P):
            return A(WK + i * T, T, r0, r1)

        e_W, e_P, e_INV, e_B, e_KK, e_AT, e_BH, e_KH, e_BP, e_KP = range(10)

        def tm(i):
            return A(WK + 5120 + i * T).rearrange("p (t c) -> p t c", t=NT)

        t_A, t_BP, t_KP, t_V = range(4)
        h_buf = [[A(WK + 7168 + i * T) for i in range(4)] + [proj(ZZ + 1), proj(ZZ + 2)], [ew(i) for i in (e_W, e_P, e_INV, e_B, e_KK, e_KP)]]
        m_AT, m_LV, m_X, m_Z, m_U, m_AW = range(6)
        gt_all = xn[0:CH, :, :].rearrange("p a b -> p (a b)").rearrange("p (c h i) -> p c h i", c=NC, h=8)
        h_all = A(PROJ, 4096, 0, CH).rearrange("p (c h i) -> p c h i", c=NC, h=8)
        TW = PROJ + DT * PADW
        SG = PROJ + ZZ * PADW

        F_UB, F_CB, F_ACT, F_ACC, F_CMB = 0, 2064, 4112, 6160, 10256

        def act_buf(b, i):
            return A(F_ACT + (2 * b + i) * T)

        def at(j, m, k):
            return m * j + k if isinstance(j, int) else j[0] * (2 * m) + (m * j[1] + k)

        def p2(t, r0=0, r1=P):
            return A(t * T, T, r0, r1)

        W2 = 36 * T
        g_VT, g_WS, g_SQ = W2, W2 + 2048, W2 + 2560
        l_B, l_E, l_QK, l_AT, l_KT, l_ST, l_VT = [
            o for o in (W2, W2 + 1024, W2 + 2048, W2 + 3072, W2 + 5120, W2 + 6144, W2 + 6912)]
        d_VT, d_MA, d_SC, d_RL, d_LG, d_PT, d_BR = [
            W2 + o for o in (0, 2048, 3328, 3840, 4864, 5888, 6912)]
        d_HK = GQ * T
        MG = W2
        s_SG2 = W2 + 4096
        OUT = 0

        v_tmp = tiny[:, 0:T]
        v_rs = tiny[:, T:2 * T]

        sm_o = [0]
        smalls = ctx.enter_context(nc.sbuf_tensor("smalls", [P, 560], F32))

        def small(n, rows=P):
            o = sm_o[0]
            sm_o[0] += n
            assert sm_o[0] <= 560
            return smalls[0:rows, o:o + n]

        dec3 = small(96)
        expA = small(1)
        one_ka = small(4)
        pls = small(16, CH)
        csil = small(KT)
        c_last = small(32)
        mod = small(48)
        gmod = small(KT)
        qg = small(1)
        iw = small(16)
        top8 = small(8)
        nmax = small(4)
        rsum = small(4)
        rinv = small(4)
        rt_l, rt_c = small(80), small(64)
        rt_w = [small(16) for _ in range(5)]
        rt_s = [small(4) for _ in range(9)]

        block = ctx.enter_context(nc.Block())
        PSB = [ps[:, b, :] for b in range(8)]


        @block.tensor
        def _(pe):
            unit = [0]

            def mm(o, l, r, start=True, stop=True):
                return nc.tensor.matmul(o, l, r, start=start, stop=stop)

            def tr(o, i):
                k = i.shape[0]
                return nc.tensor.transpose(o, i, C("ident", k, 0, k))

            def open_(what, k, b, it=None, per=0):
                if used[b]:
                    pe.wait_ge(free[b], used[b] if it is None else it * per + used[b])
                place[what, k] = (b, used[b], per)
                used[b] += 1
                return PSB[b]

            def close(last, what, k=0):
                last.then_inc(full[place[what, k][0]], 1)

            def take(it=None, per=0):
                u = unit[0]
                unit[0] += 1
                v = 16 * (u // RING + 1)
                pe.wait_ge(sem(f"weights{u % RING}_loaded"), v if it is None else it * (16 * per // RING) + v)
                return ring[:, u % RING, :]

            def norm_sum(what, srcs, ones, ready, b=4):
                o = open_(what, 0, b)
                for k, src in enumerate(srcs):
                    pe.wait_ge(*ready(k))
                    last = mm(o, ones, src, k == 0, k == len(srcs) - 1)
                close(last, what)

            def tile_1024(w, j, rhs, o, first):
                for k in range(KT):
                    last = mm(o, w[:, k, j * P:(j + 1) * P], rhs(k), k == 0, k == KT - 1)
                    if first and k == 0:
                        last.then_inc(sem("weights_used"), 1)
                return last

            def project(what, n_units, rhs, t0=0, b0=0, nb=4):
                for _ in range(n_units):
                    w = take().rearrange("p (k c) -> p k c", k=KT)
                    for j in range(2):
                        o = open_(what, t0, b0 + t0 % nb)
                        close(tile_1024(w, j, rhs, o, j == 0), what, t0)
                        t0 += 1

            def modulation(n, i0):
                pe.wait_ge(sem("csil_ready"), 1)
                for i in range(i0, i0 + n):
                    w = take().rearrange("p (k c) -> p k c", k=KT)
                    for j in range(2):
                        o = PSB[7][:, 2 * i + j:2 * i + j + 1]
                        last = tile_1024(w, j, lambda k: csil[:, k:k + 1], o, j == 0)
                if i0 + n == N_MOD:
                    close(last, "mod")

            pe.wait_ge(sem("fixed_loaded"), 16)
            pe.wait_ge(sem("x_loaded"), 16)
            for k in range(KT):
                o = open_("x", k, k % 4)
                for t in range(NT):
                    last = tr(o[:, t * P:(t + 1) * P], A(XT + t * D + k * P, P))
                close(last, "x", k)
            norm_sum("sum_pre_mix", [A(SQ + k * T) for k in range(KT)], C("ones"), lambda k: (sem("sq_pre_mix"), k + 1))
            pe.wait_ge(sem("xn_ready"), KT)
            project("proj", 14, lambda k: xn[:, k, :])

            pe.wait_ge(sem("dt_ready"), 1)
            o = open_("dec3", 0, 4)
            for i in range(3):
                for t in range(NT):
                    last = tr(o[:, (i * NT + t) * 8:(i * NT + t + 1) * 8], ym([0, 1, 2][i], 0, 8)[:, t * P:(t + 1) * P])
            close(last, "dec3")
            pe.wait_ge(sem("xbc_ready"), 8)
            for t in range(NT):
                o = open_("xs_tm", t, t)
                for k in range(4):
                    last = tr(o[:, k * P:(k + 1) * P], proj(XS + k)[:, t * P:(t + 1) * P])
                close(last, "xs_tm", t)
            for i in range(2):
                o = open_("b_tm", i, 5 + i)
                for t in range(2):
                    for g in range(2):
                        last = tr(o[:, (t * 2 + g) * P:(t * 2 + g + 1) * P],
                                  proj(BM + g)[:, (2 * i + t) * P:(2 * i + t + 1) * P])
                close(last, "b_tm", i)
            for g in range(2):
                o = open_("scores", g, 5 + g)
                for t in range(NT):
                    c = slice(t * P, (t + 1) * P)
                    last = mm(o[:, c], proj(BM + g)[:, c], proj(CM + g)[:, c])
                close(last, "scores", g)
            emptied(pe, "b_tm", 1)
            pe.wait_ge(sem("xs2_ready"), NT)
            for t in range(3):
                o = open_("state", t, t)
                for g in range(2):
                    last = mm(o[:, g * 256:(g + 1) * 256], A(s_BT, 1024)[:, (t * 2 + g) * P:(t * 2 + g + 1) * P],
                              A(s_XS2, 2048)[:, t * T + g * 256:t * T + (g + 1) * 256])
                close(last, "state", t)

            def cs_row(h):
                close(mm(open_("cs_row", h, 5 + h % 2), C("sel16", 8, h * P, (h + 1) * P), ym(1, 0, 8)), "cs_row", h)

            o = open_("chunk_decay", 0, 7)
            for h in range(8):
                last = mm(o[:, h * NT:(h + 1) * NT], C("sel16", 8, h * P, (h + 1) * P), ym(1, 0, 8)[:, P - 1::P])
            close(last, "chunk_decay")
            cs_row(0)
            cs_row(1)
            for h in range(8):
                m, e = h // 2, h % 2
                if e == 0:
                    o = open_("ssd_y", m, m)
                pe.wait_ge(sem("mt_ready"), h + 1)
                rows = o[e * CH:(e + 1) * CH, :]
                for t in range(NT):
                    c = slice(t * P, (t + 1) * P)
                    last = mm(rows[:, c], A(s_XD, 2048)[:, t * T + h * CH:t * T + (h + 1) * CH],
                              A(s_HB + (h % 2) * T)[:, c], True, t == 0)
                    if t:
                        last = mm(rows[:, c], A(s_SI + (t - 1) * T)[:, h * CH:(h + 1) * CH],
                                  A(s_CE + (h % 2) * T)[:, c], False, True)
                if e:
                    close(last, "ssd_y", m)
                else:
                    last.then_inc(sem("ssd_head_used"), 1)
                if h + 2 < 8:
                    cs_row(h + 2)
            for g in range(2):
                norm_sum(f"sum_ssd{g}", [A(s_XD + (2 * g + i) * T) for i in range(2)], C("ones"),
                         lambda i: (sem("sq_ssd"), 2 * g + i + 1))

            open_("mod", 0, 7)
            for m in range(4):
                c = slice(m * P, (m + 1) * P)
                pe.wait_ge(sem("tanh_ready"), 1)
                close(mm(open_("w_low", m, 0), M("wa2", 0, CH)[:, c], A(TW, T, 0, CH)), "w_low", m)
                close(mm(open_("a_low", m, 1), M("wa2", CH, P)[:, c], proj(WA, CH, P)), "a_low", m)
                norm_sum(f"sum_kk{m}", [ew(e_BP)], C("blk64"), lambda _: (sem("sq_kk"), m + 1))
                norm_sum(f"sum_bonus{m}", [ew(e_BP)], C("blk64"), lambda _: (sem("bonus_in"), m + 1), 5)
                modulation(6, 6 * m)
                pe.wait_ge(sem("pair_ready"), m + 1)
                o = open_("last_decay", m, 0)
                for e in range(2):
                    r = slice(e * CH, (e + 1) * CH)
                    last = mm(o[0:CH, e * NC:(e + 1) * NC], C("ident")[:, r], ew(e_P)[:, CH - 1::CH])
                close(last, "last_decay", m)
                for i, src in enumerate((ew(e_AT), ew(e_BP), ew(e_KP), proj(VV + m))):
                    o = open_(("tm", m), i, 1 + i)
                    for t in range(NT):
                        last = tr(o[:, t * P:(t + 1) * P], src[:, t * P:(t + 1) * P])
                    close(last, ("tm", m), i)

                def gram(what, e, b, l, r):
                    o = open_((what, m), e, b)
                    rows = slice(e * CH, (e + 1) * CH)
                    for t in range(NT):
                        c = slice(t * P, (t + 1) * P)
                        last = mm(o[:, c], l[rows, c], r[rows, c])
                    close(last, (what, m), e)

                def units4(what, e, b, l, r):
                    o = open_((what, m), e, b)
                    for t in range(NT):
                        c = slice(t * P, (t + 1) * P)
                        last = mm(o[:, c], l[:, c], r[:, c])
                    close(last, (what, m), e)

                for e in range(2):
                    gram("abT", e, 5 + e, ew(e_BH), ew(e_AT))
                for e in range(2):
                    gram("ab", e, 1 + e, ew(e_AT), ew(e_BH))
                for lv in range(1, 6):
                    for e in range(2):
                        hb = h_buf[e]
                        pe.wait_ge(sem(f"level{e}_ready"), 5 * m + lv)
                        units4(f"U{lv}", e, 3 * e, hb[m_LV], hb[m_X])
                    for e in range(2):
                        hb = h_buf[e]
                        emptied(pe, (f"U{lv}", m), e)
                        units4(f"ZU{lv}", e, 3 * e + 1, hb[m_U], hb[m_Z])
                        if lv < 5:
                            units4(f"XU{lv}", e, 3 * e + 2, hb[m_Z], hb[m_U])
                for e in range(2):
                    gram("akT", e, 3 * e, ew(e_KH), ew(e_AT))
                    gram("rbT", e, 3 * e + 1, ew(e_BH), proj(RR + m))
                    gram("rkT", e, 3 * e + 2, ew(e_KH), proj(RR + m))
                for e in range(2):
                    hb, r = h_buf[e], slice(e * CH, (e + 1) * CH)
                    emptied(pe, ("akT", m), e)
                    o = open_(("wv", m), e, 3 * e)
                    for t in range(NT):
                        last = mm(o[:, t * CH:(t + 1) * CH], hb[m_X][:, t * P:(t + 1) * P], tm(t_V)[:, t, r])
                    close(last, ("wv", m), e)
                for e in range(2):
                    hb = h_buf[e]
                    emptied(pe, ("wv", m), e)
                    units4("aw", e, 3 * e, hb[m_Z], hb[m_U])
                for e in range(2):
                    hb, r = h_buf[e], slice(e * CH, (e + 1) * CH)
                    emptied(pe, ("rkT", m), e)
                    emptied(pe, ("aw", m), e)
                    o = open_(("ry", m), e, 3 * e + 1)
                    for t in range(NT):
                        c = slice(t * P, (t + 1) * P)
                        mm(o[:, c], hb[m_AW][:, c], hb[m_AT][:, c], True, False)
                        mm(o[CH:P, c], tm(t_V)[:, t, r], hb[m_LV][:, c], False, True)
                        last = mm(o[0:CH, c], C("ident")[:, r], proj(RR + m)[:, c], False, True)
                    close(last, ("ry", m), e)
                    b = ((0, 2, 3, 5), (6, 0, 2, 3))[e]
                    for i in range(2):
                        q = slice(i * CH, (i + 1) * CH)
                        a = four(hb[m_AW])
                        og = open_(("gt", m), 2 * e + i, b[i])
                        for t in range(NT):
                            last = mm(og[0:CH, t * CH:(t + 1) * CH], a[q, t, 0:CH], tm(t_BP)[q, t, r])
                        close(last, ("gt", m), 2 * e + i)
                    for i in range(2):
                        q = slice(i * CH, (i + 1) * CH)
                        oh = open_(("hh", m), 2 * e + i, b[2 + i])
                        for t in range(NT):
                            c = slice(t * CH, (t + 1) * CH)
                            mm(oh[0:CH, c], tm(t_BP)[q, t, r], a[q, t, CH:P], True, False)
                            last = mm(oh[0:CH, c], tm(t_KP)[q, t, r], tm(t_V)[q, t, r], False, True)
                        close(last, ("hh", m), 2 * e + i)
            for i in range(4):
                emptied(pe, ("hh", 3), i)
            for cn in range(1, NC - 1):
                if cn > 1:
                    emptied(pe, ("s", cn - 1))
                o = open_(("s", cn), 0, 0)
                for h in range(8):
                    last = mm(o[0:CH, h * CH:(h + 1) * CH], gt_all[:, cn, h, :], h_all[:, cn - 1, h, :])
                close(last, ("s", cn))
            emptied(pe, ("s", NC - 2))
            for m in range(4):
                o = open_("rwkv_y", m, 1 + m % 2)
                for e in range(2):
                    rows = o[e * CH:(e + 1) * CH, :]
                    ry = proj((RR, KK_)[e] + m)
                    mm(rows, C("ident")[:, CH:P], ry, True, False)
                    for cn in range(1, NC):
                        c = slice(cn * CH, (cn + 1) * CH)
                        last = mm(rows[:, c], h_all[:, cn - 1, 2 * m + e, :], ry[0:CH, c], False, cn == NC - 1)
                close(last, "rwkv_y", m)
                norm_sum(f"sum_y{m}", [ew(0)], C("blk64"), lambda _: (freed("rwkv_y", m), place["rwkv_y", m][1] + 1), 3)
                norm_sum(f"sum_y2{m}", [ew(2)], C("blk64"), lambda _: (sem("sq_y"), m + 1), 4)
                pe.wait_ge(sem("sg_ready"), 1)
                close(mm(open_("gate", m, 5), M("g2m", a=m * P, b=(m + 1) * P), A(SG)), "gate", m)
            if stop <= 2:
                return
            pe.wait_ge(sem("ssd_out_ready"), 4)
            for m in range(4):
                emptied(pe, "gate", m)
            project("mix", 4, lambda k: ym(k))


            def sums(what, names, ready):
                norm_sum(what, names, C("ones"), lambda k: (sem(ready), k + 1))

            sq8 = [A(SQ + k * T) for k in range(KT)]
            sums("sum_post_mix", sq8, "sq_post_mix")
            sums("sum_pre_ffn", sq8, "sq_pre_ffn")
            pe.wait_ge(sem("ffn_in_ready"), KT)

            def up(kind, phase, sub, it=None):
                for u in range(2):
                    w = take(it, 6).rearrange("p (k c) -> p k c", k=KT)
                    for j in range(2):
                        k = (phase, sub, 2 * u + j)
                        o = open_(kind + "_up", k, 2 * u + j, it, 2)
                        close(tile_1024(w, j, lambda k: xn[:, k, :], o, j == 0), kind + "_up", k)

            def down(kind, phase, j, it=None):
                w = take(it, 6).rearrange("p (k c) -> p k c", k=2)
                sub = j % 2 if isinstance(j, int) else j[1] % 2
                pe.wait_ge(sem(kind + "_act_ready"), at(j, 2, 2))
                for m in range(KT):
                    k = (phase, sub, m)
                    o = open_(kind + "_down", k, 4 + m % 4, it, 4)
                    first = mm(o, w[:, 0, m * P:(m + 1) * P], act_buf(sub, 0), True, False)
                    if m == 0:
                        first.then_inc(sem("weights_used"), 1)
                    close(mm(o, w[:, 1, m * P:(m + 1) * P], act_buf(sub, 1), False, True), kind + "_down", k)

            def gated(kind, n):
                times = (n - 1) // 2
                with pe.Fori(0, times) as it:
                    up(kind, "loop", 1, it)
                    down(kind, "loop", (it, 0), it)
                    up(kind, "loop", 0, it)
                    down(kind, "loop", (it, 1), it)
                for b in range(8):
                    used[b] += (2 if b < 4 else 4) * (times - 1)
                unit[0] += 6 * (times - 1)
                if n % 2 == 0:
                    up(kind, "last", 1)
                    down(kind, "last", n - 2)
                down(kind, "last", n - 1)

            up("ffn", "first", 0)
            gated("ffn", NF)
            sq8b = [A(F_CMB + k * T) for k in range(KT)]
            sums("sum_post_ffn", sq8b, "sq_post_ffn")
            sums("sum_1", sq8b, "sq_1")
            if stop <= 3:
                return
            h = lambda k: xn[:, k, :]
            pe.wait_ge(sem("h_ready"), KT)
            for i in range(2):
                close(mm(open_("bias_row", i, 4 + i)[0:4, :], S("rel_bias", 0, 4), C("bucket", P, i * T, (i + 1) * T)),
                      "bias_row", i)
            project("p2", 4, h)
            o = open_("w_s", 0, 6)
            for g in range(4):
                last = tr(o[:, g * P:(g + 1) * P], M("w_s")[:, g * P:(g + 1) * P])
            close(last, "w_s")
            project("p2", 3, h, 8)
            norm_sum("gmlp_mean", [p2(AV + k) for k in range(4)], C("ones"), lambda k: (free[bank_of("p2", AV + k)], place["p2", AV + k][1] + 1))
            project("p2", 2, h, 14)
            sums("gmlp_var", [A(g_SQ + k * T) for k in range(4)], "sq_gmlp")
            project("p2", 2, h, 18)
            pe.wait_ge(sem("gmlp_v_ready"), 4)
            for t in range(NT):
                o = open_("gmlp_vt", t, 4 + t)
                for k in range(4):
                    last = tr(o[:, k * P:(k + 1) * P], p2(AV + k)[:, t * P:(t + 1) * P])
                close(last, "gmlp_vt", t)
            emptied(pe, "w_s")
            for t in range(NT):
                emptied(pe, "gmlp_vt", t)
            for g in range(4):
                o = open_("mixed", g, 4 + g)
                for t in range(NT):
                    c = slice(t * P, (t + 1) * P)
                    mm(o[:, c], A(g_VT, 2048)[:, t * T + g * P:t * T + (g + 1) * P], A(g_WS)[:, g * P:(g + 1) * P], True, False)
                    last = mm(o[:, c], C("ones"), M("b_s")[:, g * P:(g + 1) * P], False, True)
                close(last, "mixed", g)
            emptied(pe, "p2", MISC)
            for m in range(2):
                close(mm(open_("forget", m, 4 + m), M("gate2")[:, m * P:(m + 1) * P], p2(MISC)), "forget", m)
            project("p2", 7, h, 22)
            for t in range(NT):
                o = open_("gla_vt", t, 4 + t)
                for k in range(4):
                    last = tr(o[:, k * P:(k + 1) * P], p2(GV + k)[:, t * P:(t + 1) * P])
                close(last, "gla_vt", t)
            for lv in range(8):
                for m in range(2):
                    pe.wait_ge(sem("level_ready"), 2 * lv + m + 1)
                    for e in range(2):
                        r = slice(e * CH, (e + 1) * CH)
                        o = open_(("attn", lv), 2 * m + e, 2 * m + e)
                        for t in range(NT):
                            c = slice(t * P, (t + 1) * P)
                            if lv:
                                l = rr = A(l_QK + m * T)
                            else:
                                l, rr = p2(GK + m), p2(GQ + m)
                            last = mm(o[:, c], l[r, c], rr[r, c])
                        close(last, ("attn", lv), 2 * m + e)
            pe.wait_ge(sem("khat_ready"), 2)
            for m in range(2):
                o = open_("khat", m, 4 + m)
                for t in range(NT):
                    last = tr(o[:, t * P:(t + 1) * P], A(l_QK + m * T)[:, t * P:(t + 1) * P])
                close(last, "khat", m)
            for m in range(2):
                emptied(pe, "khat", m)
                o = open_("gla_state", m, 6 + m)
                for t in range(3):
                    for e in range(2):
                        last = mm(o[e * CH:(e + 1) * CH, t * P:(t + 1) * P],
                                  A(l_KT + m * T)[:, t * P + e * CH:t * P + (e + 1) * CH],
                                  A(l_VT, 2048)[:, t * T + (2 * m + e) * P:t * T + (2 * m + e + 1) * P])
                close(last, "gla_state", m)
            pe.wait_ge(sem("gla_states_ready"), 2)
            for hh in range(4):
                emptied(pe, ("attn", 7), hh)
                m, r = hh // 2, slice((hh % 2) * CH, (hh % 2 + 1) * CH)
                o = open_("gla_o", hh, hh)
                for t in range(NT):
                    c = slice(t * P, (t + 1) * P)
                    last = mm(o[:, c], A(l_VT, 2048)[:, t * T + hh * P:t * T + (hh + 1) * P],
                              A(l_AT + hh * T)[:, c], True, t == 0)
                    if t:
                        last = mm(o[:, c], A(l_ST + m * 384)[r, (t - 1) * P:t * P], A(l_E + m * T)[r, c], False, True)
                close(last, "gla_o", hh)
            for hh in range(4):
                norm_sum(f"sum_gla{hh}", [A(l_QK + (hh % 2) * T)], C("ones"), lambda _: (sem("sq_gla"), hh + 1), 4 + hh % 2)
            for i in range(8):
                norm_sum(f"sum_qk{i}", [A(l_QK + (i % 2) * T)], C("ones"), lambda _: (sem("sq_qk"), i + 1), 4 + i % 2)
            o = open_("iw", 0, 6)
            for t in range(NT):
                last = tr(o[:, t * P:(t + 1) * P], p2(MISC)[:, t * P:(t + 1) * P])
            close(last, "iw")
            pe.wait_ge(sem("gla_out_ready"), 4)
            for t in range(NT):
                o = open_("dsa_vt", t, t)
                for k in range(4):
                    last = tr(o[:, k * P:(k + 1) * P], p2(DV + k)[:, t * P:(t + 1) * P])
                close(last, "dsa_vt", t)
            for t in range(1, NT):
                n = (t + 1) * P
                for hh in range(4):
                    r = slice((hh % 2) * CH, (hh % 2 + 1) * CH)
                    close(mm(open_(("index", t), hh, 4 + hh)[:, 0:n], p2(IQ + hh // 2)[r, t * P:(t + 1) * P],
                             p2(IK)[r, 0:n]), ("index", t), hh)
            pe.wait_ge(sem("bias_loaded"), 16)
            pe.wait_ge(sem("qk_ready"), 8)

            def logits(hh, t):
                n = (t + 1) * P
                o = open_(("logits", hh), t, 4 + t % 2)
                mm(o[:, 0:n], p2(DQ + hh)[:, t * P:(t + 1) * P], p2(DK + hh)[:, 0:n], True, False)
                close(mm(o[:, 0:n], C("flip"), A(d_HK + hh * 896 + 384 - t * P, n), False, True), ("logits", hh), t)

            def attend(hh, t):
                i = 4 * hh + t
                pe.wait_ge(sem("probs_ready"), i + 1)
                o = open_("pt", i, 6 + i % 2)
                for j in range(t + 1):
                    last = tr(o[:, j * P:(j + 1) * P], A(d_LG + (i % 2) * T)[:, j * P:(j + 1) * P])
                close(last, "pt", i)

            def values(hh, t):
                i = 4 * hh + t
                emptied(pe, "pt", i)
                if t == 0:
                    open_("dsa_y", hh, hh)
                o = PSB[bank_of("dsa_y", hh)]
                for j in range(t + 1):
                    last = mm(o[:, t * P:(t + 1) * P], A(d_VT, 2048)[:, j * T + hh * P:j * T + (hh + 1) * P],
                              A(d_PT + (i % 2) * T)[:, j * P:(j + 1) * P], j == 0, j == t)
                if t == NT - 1:
                    close(last, "dsa_y", hh)

            pairs = [(hh, t) for hh in range(4) for t in range(NT)]
            logits(*pairs[0])
            for i, (hh, t) in enumerate(pairs):
                if i + 1 < len(pairs):
                    logits(*pairs[i + 1])
                attend(hh, t)
                if i:
                    values(*pairs[i - 1])
            values(*pairs[-1])
            if stop <= 4:
                return
            ys = [AU, GR, DQ]
            for n in range(3):
                if n == 2:
                    emptied(pe, "dsa_y", 3)
                for half in range(2):
                    w = take().rearrange("p (k c) -> p k c", k=4)
                    for i in range(4):
                        m = 4 * half + i
                        o = open_(("branch", n), m, i)
                        for k in range(4):
                            last = mm(o, w[:, k, i * P:(i + 1) * P], p2(ys[n] + k), k == 0, k == 3)
                            if i == 0 and k == 0:
                                last.then_inc(sem("weights_used"), 1)
                        close(last, ("branch", n), m)
                    project(("gates", n), 2, h, 4 * half, 4)
            for m in range(KT):
                pe.wait_ge(sem("merged"), KT + m + 1)
            project("mix2", 4, lambda k: A(MG + k * T))
            sums("sum_2", [A(k * T) for k in range(KT)], "sq_2")
            pe.wait_ge(sem("h2_ready"), KT)
            o = open_("route", 0, 5)
            for t in range(NT):
                for k in range(KT):
                    last = mm(o[:, t * 20:(t + 1) * 20], xn[:, k, t * P:(t + 1) * P], M("w_route")[:, k * 20:(k + 1) * 20],
                              k == 0, k == KT - 1)
            close(last, "route")
            up("moe", "first", 0)
            pe.wait_ge(sem("combine_ready"), 1)
            o = open_("combine", 0, 6)
            for t in range(NT):
                last = tr(o[0:NE, t * P:(t + 1) * P], rt_c[:, t * NE:(t + 1) * NE])
            close(last, "combine")
            emptied(pe, "combine")
            for e in range(NE):
                close(mm(open_("weights", e, 4 + e % 4), C("sel16", NE, e * P, (e + 1) * P), A(F_CB, T, 0, NE)), "weights", e)
            gated("moe", NE)
            for t in range(NT):
                for i in range(2):
                    o = open_("out", 2 * t + i, 2 * (t % 2) + i)
                    for k in range(4):
                        pe.wait_ge(sem("out_ready"), 4 * i + k + 1)
                        last = tr(o[:, k * P:(k + 1) * P], res[:, 4 * i + k, t * P:(t + 1) * P])
                    close(last, "out", 2 * t + i)


        @block.scalar
        def _(act):
            n_rstd = [0]

            def f(o, i, func, **kw):
                return nc.scalar.activation(o, i, func, **kw)

            def rstd():
                n_rstd[0] += 1
                act.wait_ge(sem("variance_inverted"), n_rstd[0])
                f(v_rs, v_tmp, ACT.Sqrt).then_inc(sem("rstd_ready"), 1)

            def evac(what, k, o, i=None, func=ACT.Copy, **kw):
                filled(act, what, k)
                f(o, PSB[bank_of(what, k)] if i is None else i, func, **kw).then_inc(freed(what, k), 1)

            act.dma_start(fix[:, :], fixed).then_inc(sem("fixed_loaded"), 16)
            act.dma_start(A(XT, 4096).rearrange("p (t c) -> p t c", t=NT),
                          x.rearrange("(t p) c -> p t c", p=P)).then_inc(sem("x_loaded"), 16)
            for k in range(KT):
                evac("x", k, res[:, k, :])
            rstd()
            act.wait_ge(sem("fixed_loaded"), 16)
            f(csil[:, :], S("c", 0, KT), ACT.Silu).then_inc(sem("csil_ready"), 1)
            act.wait_ge(sem("pads_zeroed"), 1)
            for t in range(N_PROJ):
                evac("proj", t, proj(t))
                if 10 <= t < 18:
                    act.wait_ge(sem("conv_ready"), t - 9)
                    f(proj(XS + t - 10), proj(XS + t - 10), ACT.Silu).then_inc(sem("xbc_ready"), 1)
                if t == 18:
                    f(expA[:, :], S("a_log"), ACT.Exp).then_inc(sem("exp_a_ready"), 1)
                    act.wait_ge(sem("dt_abs_ready"), 1)
                    f(ym(4, 0, 8), ym(3, 0, 8), ACT.Exp, scale=-1.0).then_inc(sem("dt_exp_ready"), 1)
                if t == 20:
                    act.wait_ge(sem("to_end_ready"), 1)
                    f(ym(3, 0, 8), ym(3, 0, 8), ACT.Exp).then_inc(sem("to_end_exp_ready"), 1)
            act.wait_ge(sem("mixed"), 2)
            f(A(TW, T, 0, CH), proj(WA, 0, CH), ACT.Tanh).then_inc(sem("tanh_ready"), 1)
            f(proj(GL), proj(GL), ACT.Sigmoid).then_inc(sem("sigmoid_ready"), 1)
            for i in range(2):
                evac("b_tm", i, A(s_BT + i * T))
            evac("chunk_decay", 0, c_last[:, :], PSB[bank_of("chunk_decay")][:, 0:32], ACT.Exp)

            def decay_row(h):
                filled(act, "cs_row", h)
                f(xn[:, h, :], PSB[bank_of("cs_row", h)], ACT.Exp).then_inc(sem("row_decay_ready"), 1)

            for h in range(8):
                decay_row(h)
                emptied(act, "cs_row", h)
                f(A(s_HB + (h % 2) * T), A(s_HB + (h % 2) * T), ACT.Exp).then_inc(sem("pair_decay_ready"), 1)
            for m in range(4):
                f(proj(ZZ + m), proj(ZZ + m), ACT.Silu).then_inc(sem("z_ready"), 1)
            for g in range(2):
                rstd()
            act.wait_ge(sem("ssd_out_ready"), 4)
            act.wait_ge(sem("sigmoid_ready"), 1)
            f(A(SG), proj(GL), ACT.Copy).then_inc(sem("sg_ready"), 1)

            for m in range(4):
                if m:
                    filled(act, ("hh", m - 1), 3)
                evac("w_low", m, ew(e_W), None, ACT.Sigmoid, bias=S("w0", m))
                evac("a_low", m, ew(e_B), None, ACT.Sigmoid, bias=S("a0", m))
                emptied(act, "w_low", m)
                f(ew(e_W), ew(e_W), ACT.Exp, scale=-EXP_HALF).then_inc(sem("w_ready"), 1)
                rstd()
                evac("last_decay", m, pls[:, :], PSB[bank_of("last_decay", m)][0:CH, 0:2 * NC])
                for i, t in enumerate((t_A, t_BP, t_KP, t_V)):
                    evac(("tm", m), i, tm(t), four(PSB[bank_of(("tm", m), i)]))
                for lv in range(1, 6):
                    for e in range(2):
                        evac((f"U{lv}", m), e, h_buf[e][m_U])
                for e in range(2):
                    if e == 0:
                        filled(act, ("ZU5", m), 1)
                        emptied(act, ("tm", m), 0)
                    r = slice(e * CH, (e + 1) * CH)
                    f(four(h_buf[e][m_U])[:, :, 0:CH], tm(t_A)[:, :, r], ACT.Copy)
                for e in range(2):
                    evac(("wv", m), e, four(h_buf[e][m_U])[:, :, CH:P],
                         PSB[bank_of(("wv", m), e)][:, 0:256].rearrange("p (a b) -> p a b", a=4))
                for e in range(2):
                    evac(("aw", m), e, h_buf[e][m_AW])
                for e in range(2):
                    h = 2 * m + e
                    for i in range(2):
                        evac(("hh", m), 2 * e + i, h_all[:, i::2, h, :],
                             PSB[bank_of(("hh", m), 2 * e + i)][0:CH, 0:256].rearrange("p (c i) -> p c i", c=NT))
            for m in range(4):
                if m:
                    emptied(act, "gate", m - 1)
                evac("rwkv_y", m, ew(0))
                rstd()
            if stop <= 2:
                return


            for k in range(KT):
                evac("mix", k, xn[:, k, :])
            rstd()
            rstd()

            def silu_gates(j, phase, sub, it=None):
                for i in range(4):
                    k = (phase, sub, i)
                    if j != 0:
                        act.wait_ge(sem("ffn_taps_used"), at(j, 4, i - 3))
                    filled(act, "ffn_up", k, it)
                    f(A(F_UB + i * PADW + 3), PSB[i], ACT.Copy).then_inc(freed("ffn_up", k), 1)
                for i in range(2):
                    act.wait_ge(sem("ffn_taps_used"), at(j, 4, i + 1))
                    f(A(F_CB + i * T), A(F_CB + i * T), ACT.Silu).then_inc(sem("ffn_silu_ready"), 1)

            act.wait_ge(sem("ffn_zeroed"), 1)
            silu_gates(0, "first", 0)
            with act.Fori(0, (NF - 1) // 2) as it:
                silu_gates((it, 1), "loop", 1, it)
                silu_gates((it, 2), "loop", 0, it)
            rstd()
            rstd()
            if stop <= 3:
                return
            for i in range(2):
                evac("bias_row", i, A(d_BR + i * T, T, 0, 4), PSB[bank_of("bias_row", i)][0:4, :])
            emptied(act, "bias_row", 0)
            emptied(act, "bias_row", 1)
            act.dma_start(skew, A(d_BR, 2 * T, 0, 4)).then_inc(sem("bias_stored"), 16)
            for t in range(8):
                evac("p2", t, p2(t), None, ACT.Gelu_apprx_tanh)
            for t in range(8, 18):
                evac("p2", t, p2(t), None, ACT.Silu if GR <= t < GR + 4 else ACT.Copy)
            rstd()
            for t in range(18, 22):
                evac("p2", t, p2(t), None, ACT.Silu if GR <= t < GR + 4 else ACT.Copy)
            for t in range(NT):
                evac("gmlp_vt", t, A(g_VT + t * T))
            for m in range(2):
                act.wait_ge(sem("forget_abs"), m + 1)
                f(A(l_E + m * T), A(l_E + m * T), ACT.Exp).then_inc(sem("forget_exp"), 1)
            for t in range(22, 36):
                evac("p2", t, p2(t))
            act.wait_ge(sem("bias_stored"), 16)
            for t in range(NT):
                evac("gla_vt", t, A(l_VT + t * T))
            for lv in range(1, 8):
                for m in range(2):
                    act.wait_ge(sem("log_decay_ready"), 2 * (lv - 1) + m + 1)
                    f(A(l_E + m * T), A(l_E + m * T), ACT.Exp).then_inc(sem("decay_ready"), 1)
            for m in range(2):
                act.wait_ge(sem("log_decay_ready"), 14 + m + 1)
                f(A(l_QK + m * T), A(l_QK + m * T), ACT.Exp).then_inc(sem("decay_ready"), 1)
                f(A(l_E + m * T), A(l_B + m * T), ACT.Exp).then_inc(sem("decay_ready"), 1)
            for m in range(2):
                evac("khat", m, A(l_KT + m * T))
            for _ in range(4 + 8):
                rstd()
            act.wait_ge(sem("gla_out_ready"), 4)
            hankel = bass.AP(tensor=skew.tensor, offset=skew.offset, ap=[[1, P], [2 * T, 4], [1, 896]])
            act.dma_start(A(d_HK, 4 * 896).rearrange("p (h n) -> p h n", h=4), hankel).then_inc(sem("bias_loaded"), 16)
            filled(act, "iw")
            f(iw.rearrange("p (t h) -> p t h", t=NT),
              PSB[bank_of("iw")].rearrange("p (t c) -> p t c", t=NT)[:, :, 32:36], ACT.Copy).then_inc(freed("iw"), 1)
            for t in range(NT):
                evac("dsa_vt", t, A(d_VT + t * T))
            for t in range(1, NT):
                n = (t + 1) * P
                for hh in range(4):
                    i = 4 * (t - 1) + hh
                    if i >= 2:
                        act.wait_ge(sem("relu_used"), i - 1)
                    evac(("index", t), hh, A(d_RL + (i % 2) * T, n), PSB[4 + hh][:, 0:n], ACT.Relu)
            for i in range(16):
                t = i % 4
                n = (t + 1) * P
                act.wait_ge(sem("logits_ready"), i + 1)
                p_ = A(d_LG + (i % 2) * T, n)
                f(p_, p_, ACT.Exp, bias=nmax[:, i % 4:i % 4 + 1], accum_out=rsum[:, i % 4:i % 4 + 1])\
                    .then_inc(sem("exp_ready"), 1)
                evac("pt", i, A(d_PT + (i % 2) * T, n), PSB[bank_of("pt", i)][:, 0:n])
                if t == 0 and i:
                    evac("dsa_y", i // 4 - 1, p2(DQ + i // 4 - 1))
            evac("dsa_y", 3, p2(DQ + 3))
            if stop <= 4:
                return
            for n in range(3):
                for m in range(KT):
                    i = n * KT + m
                    if 4 <= i < KT + 4:
                        emptied(act, ("branch", 0), i - 4)
                    elif i >= 4:
                        act.wait_ge(sem("merged"), i - 4 - KT + 1)
                    evac(("gates", n), m, A(s_SG2 + (i % 4) * T), None, ACT.Sigmoid, bias=S("b_branch", n * KT + m))
            rstd()
            act.wait_ge(sem("route_diff"), 1)
            f(rt_w[0], rt_w[0], ACT.Exp).then_inc(sem("route_exp"), 1)
            act.wait_ge(sem("route_diff"), 2)
            f(rt_s[4], rt_s[4], ACT.Exp).then_inc(sem("route_exp"), 1)
            evac("combine", 0, A(F_CB, T, 0, NE), PSB[bank_of("combine")][0:NE, :])
            for e in range(NE):
                evac("weights", e, A(F_CMB + e * T))

            def silu_experts(j, phase, sub, it=None):
                for i in range(2):
                    k = (phase, sub, i)
                    if j != 0:
                        act.wait_ge(sem("moe_act_ready"), at(j, 2, i - 1))
                    filled(act, "moe_up", k, it)
                    f(A(F_UB + i * T), PSB[i], ACT.Silu).then_inc(freed("moe_up", k), 1)

            silu_experts(0, "first", 0)
            with act.Fori(0, (NE - 1) // 2) as it:
                silu_experts((it, 1), "loop", 1, it)
                silu_experts((it, 2), "loop", 0, it)
            silu_experts(NE - 1, "last", 1)
            for i in range(8):
                evac("out", i, A(OUT + i * T))


        @block.vector
        def _(dve):
            ch = Chain(dve, "vector_step")
            link = ch.link
            V = nc.vector
            n_rstd = [0]

            def tt(o, a, b, op):
                return V.tensor_tensor(o, a, b, op)

            def ts(o, a, s1, s2=None, op0=ALU.mult, op1=None):
                return V.tensor_scalar(o, a, s1, s2, op0) if op1 is None else V.tensor_scalar(o, a, s1, s2, op0, op1)

            def stt(o, a, s1, b, op0, op1):
                return V.scalar_tensor_tensor(o, a, s1, b, op0, op1)

            def rstd(what, scale, add, op1=ALU.add, k=0):
                n_rstd[0] += 1
                filled(dve, what, k)
                V.tensor_scalar(v_tmp, PSB[bank_of(what, k)], scale, add, ALU.mult, op1).then_inc(freed(what, k), 1)
                emptied(dve, what, k)
                V.reciprocal(v_tmp, v_tmp).then_inc(sem("variance_inverted"), 1)
                dve.wait_ge(sem("rstd_ready"), n_rstd[0])

            def log1p(o, u, t1, t2):
                link(ts(t1, u, 2.0, None, ALU.add))
                link(V.reciprocal(t1, t1))
                link(tt(t1, t1, u, ALU.mult))
                link(tt(t2, t1, t1, ALU.mult))
                link(ts(o, t2, 1.0 / (2 * LOG1P_TERMS + 1)))
                for i in range(LOG1P_TERMS - 1, 0, -1):
                    link(stt(o, o, 1.0 / (2 * i + 1), t2, ALU.add, ALU.mult))
                link(stt(o, o, 1.0, t1, ALU.add, ALU.mult))

            for k in range(KT):
                emptied(dve, "x", k)
                tt(A(SQ + k * T), res[:, k, :], res[:, k, :], ALU.mult).then_inc(sem("sq_pre_mix"), 1)
            dve.wait_ge(sem("fixed_loaded"), 16)
            rstd("sum_pre_mix", 1.0 / D, 1e-6)
            for k in range(KT):
                stt(xn[:, k, :], res[:, k, :], S("g_pre_mix", k), v_rs, ALU.mult, ALU.mult).then_inc(sem("xn_ready"), 1)

            for t in range(8):
                emptied(dve, "proj", t)
                buf = A(s_HB + (t % 2) * T)
                link(ts(buf, proj(t), S("conv_w", 3 * 8 + t), S("conv_b", t), ALU.mult, ALU.add))
                link(stt(buf, proj(t, shift=1), S("conv_w", 2 * 8 + t), buf, ALU.mult, ALU.add))
                link(stt(buf, proj(t, shift=2), S("conv_w", 1 * 8 + t), buf, ALU.mult, ALU.add))
                link(stt(buf, proj(t, shift=3), S("conv_w", t), buf, ALU.mult, ALU.add))
                V.tensor_copy(proj(t), buf).then_inc(sem("conv_ready"), 1)
            dt, cs, de, t3, t4, t5, t6, t7 = [ym(i, 0, 8) for i in range(8)]
            emptied(dve, "proj", DT)
            link(ts(dt, proj(DT, 0, 8), S("dt_bias", rows=8), None, ALU.add))
            link(ts(t3, dt, -1.0))
            tt(t3, t3, dt, ALU.max).then_inc(sem("dt_abs_ready"), 1)
            for i, t in enumerate([WA, GL] + list(range(RR, RR + 12))):
                emptied(dve, "proj", t)
                buf = A(s_HB + 2 * T + (i % 2) * T)
                link(tt(buf, proj(t, shift=1), proj(t), ALU.subtract))
                stt(proj(t), buf, S("mu", i), proj(t), ALU.mult, ALU.add).then_inc(sem("mixed"), 1)
                if i == 5:
                    dve.wait_ge(sem("dt_exp_ready"), 1)
                    log1p(t5, t4, t6, t7)
                    link(ts(dt, dt, 0.0, None, ALU.max))
                    link(stt(dt, t5, 2.0, dt, ALU.mult, ALU.add))
                    link(ts(t6, dt, expA[0:8, :], -1.0, ALU.mult, ALU.mult))
                    link(V.tensor_tensor_scan(cs, C("carry128", 8), t6, 0.0, ALU.mult, ALU.add))
                    last = four(cs)[:, :, P - 1:P].to_broadcast([8, NT, P])
                    tt(four(t3), last, four(cs), ALU.subtract).then_inc(sem("to_end_ready"), 1)
                if i == 8:
                    dve.wait_ge(sem("to_end_exp_ready"), 1)
                    tt(de, t3, dt, ALU.mult).then_inc(sem("dt_ready"), 1)
            filled(dve, "dec3")
            V.tensor_copy(dec3[:, :], PSB[bank_of("dec3")][:, 0:96]).then_inc(freed("dec3"), 1)
            emptied(dve, "dec3")
            d3 = dec3[:, :].rearrange("p (i t h) -> p i t h", i=3, t=NT)

            def per_head(i, t):
                return d3[:, i, t, :].unsqueeze(2).to_broadcast([P, 8, CH])

            for t in range(NT):
                filled(dve, "xs_tm", t)
                src = PSB[bank_of("xs_tm", t)].rearrange("p (h c) -> p h c", h=8)
                tt(A(s_XS2 + t * T).rearrange("p (h c) -> p h c", h=8), src, per_head(2, t), ALU.mult)\
                    .then_inc(sem("xs2_ready"), 1)
                tt(A(s_XD + t * T).rearrange("p (h c) -> p h c", h=8), src, per_head(0, t), ALU.mult)\
                    .then_inc(freed("xs_tm", t), 1)
            for g in range(2):
                filled(dve, "scores", g)
                tt(four(A(s_GT + g * T)), four(PSB[bank_of("scores", g)]), rep4(C("incl128")), ALU.mult)\
                    .then_inc(freed("scores", g), 1)
            emptied(dve, "chunk_decay")
            cl = c_last[:, :].rearrange("p (h t) -> p h t", h=8)
            for t in range(3):
                filled(dve, "state", t)
                o = A(s_SI + t * T)
                if t == 0:
                    V.tensor_copy(o, PSB[bank_of("state", t)]).then_inc(freed("state", t), 1)
                else:
                    v8 = lambda a: a.rearrange("p (h c) -> p h c", h=8)
                    emptied(dve, "state", t - 1)
                    link(tt(v8(o), v8(A(s_SI + (t - 1) * T)), cl[:, :, t:t + 1].to_broadcast([P, 8, CH]), ALU.mult))
                    tt(o, o, PSB[bank_of("state", t)], ALU.add).then_inc(freed("state", t), 1)
            emptied(dve, "state", 2)

            def head_free(h):
                if h % 2 == 0:
                    dve.wait_ge(sem("ssd_head_used"), h // 2 + 1)
                else:
                    filled(dve, "ssd_y", h // 2)

            def log_decays(h):
                dve.wait_ge(sem("row_decay_ready"), h + 1)
                if h >= 2:
                    head_free(h - 2)
                row = PSB[bank_of("cs_row", h)]
                for t in range(NT):
                    c = slice(t * P, (t + 1) * P)
                    last = ts(A(s_HB + (h % 2) * T)[:, c], row[:, c], d3[:, 1, t, h:h + 1], 0.0, ALU.subtract, ALU.min)
                last.then_inc(freed("cs_row", h), 1)

            log_decays(0)
            for h in range(8):
                if h + 1 < 8:
                    log_decays(h + 1)
                dve.wait_ge(sem("pair_decay_ready"), h + 1)
                tt(A(s_CE + (h % 2) * T), proj(CM + h // 4), xn[:, h, :], ALU.mult)
                tt(A(s_HB + (h % 2) * T), A(s_HB + (h % 2) * T), A(s_GT + (h // 4) * T), ALU.mult)\
                    .then_inc(sem("mt_ready"), 1)
            filled(dve, "ssd_y", 3)
            for m in range(4):
                dve.wait_ge(sem("z_ready"), m + 1)
                t = A(s_HB + m * T)
                stt(t, proj(XS + m), S("d_skip", m), PSB[bank_of("ssd_y", m)], ALU.mult, ALU.add)\
                    .then_inc(freed("ssd_y", m), 1)
                emptied(dve, "ssd_y", m)
                link(tt(t, t, proj(ZZ + m), ALU.mult))
                tt(A(s_XD + m * T), t, t, ALU.mult).then_inc(sem("sq_ssd"), 1)
            for g in range(2):
                rstd(f"sum_ssd{g}", 1.0 / 256, 1e-6)
                for i in range(2):
                    m = 2 * g + i
                    stt(ym(m), A(s_HB + m * T), S("ssd_norm", m), v_rs, ALU.mult, ALU.mult)\
                        .then_inc(sem("ssd_out_ready"), 1)

            link(ts(one_ka[:, :], S("k_a", 0, 4), -1.0, 1.0, ALU.mult, ALU.add))
            c8 = lambda a: a.rearrange("p (c t) -> p c t", c=NC)
            for m in range(4):
                kt, rt, vt = proj(KK_ + m), proj(RR + m), proj(VV + m)
                pt = ew(e_P)
                if m:
                    filled(dve, ("hh", m - 1), 3)
                link(ts(ew(e_KK), kt, S("k_k", m)))
                tt(ew(e_BP), ew(e_KK), ew(e_KK), ALU.mult).then_inc(sem("sq_kk"), 1)
                emptied(dve, "a_low", m)
                link(ts(ew(e_KP), ew(e_B), S("k_a", m), one_ka[:, m:m + 1], ALU.mult, ALU.add))
                link(tt(kt, kt, ew(e_KP), ALU.mult))
                dve.wait_ge(sem("w_ready"), m + 1)
                link(tt(ew(e_AT), ew(e_W), C("carry64"), ALU.mult))
                link(tt(ew(e_W), ew(e_W), ew(e_AT), ALU.subtract))
                link(V.tensor_tensor_scan(pt, ew(e_AT), ew(e_W), 0.0, ALU.mult, ALU.add))
                link(V.reciprocal(ew(e_INV), pt))
                rstd(f"sum_kk{m}", 1.0, 1e-24, ALU.max)
                link(tt(ew(e_KK), ew(e_KK), v_rs, ALU.mult))
                stt(ew(e_BP), rt, S("r_k", m), kt, ALU.mult, ALU.mult).then_inc(sem("bonus_in"), 1)
                link(stt(ew(e_AT)[:, 1:T], ew(e_KK)[:, 1:T], -1.0, pt[:, 0:T - 1], ALU.mult, ALU.mult))
                link(ts(ew(e_AT)[:, 0:T:CH], ew(e_KK)[:, 0:T:CH], -1.0))
                link(tt(ew(e_B), ew(e_B), ew(e_KK), ALU.mult))
                link(tt(ew(e_BH), ew(e_B), ew(e_INV), ALU.mult))
                link(tt(ew(e_KH), kt, ew(e_INV), ALU.mult))
                link(tt(rt, rt, pt, ALU.mult))
                filled(dve, f"sum_bonus{m}")
                tt(ym(4 + m), vt, PSB[bank_of(f"sum_bonus{m}")], ALU.mult).then_inc(freed(f"sum_bonus{m}"), 1)
                last = pt[:, CH - 1::CH].unsqueeze(2).to_broadcast([P, NC, CH])
                link(tt(c8(ew(e_BP)), c8(ew(e_BH)), last, ALU.mult))
                tt(c8(ew(e_KP)), c8(ew(e_KH)), last, ALU.mult).then_inc(sem("pair_ready"), 1)
                for e in range(2):
                    hb = h_buf[e]
                    filled(dve, ("abT", m), e)
                    if e == 0:
                        filled(dve, ("tm", m), 3)
                    tt(four(hb[m_AT]), four(PSB[bank_of(("abT", m), e)]), rep4(C("strict64")), ALU.mult)\
                        .then_inc(freed(("abT", m), e), 1)
                    emptied(dve, ("abT", m), e)
                    link(tt(four(hb[m_Z]), four(hb[m_AT]), rep4(C("level0")), ALU.mult))
                    link(tt(four(hb[m_Z]), four(hb[m_Z]), rep4(C("ident")), ALU.add))
                    filled(dve, ("ab", m), e)
                    tt(four(hb[m_X]), four(PSB[bank_of(("ab", m), e)]), rep4(C("level0t")), ALU.mult)\
                        .then_inc(freed(("ab", m), e), 1)
                    emptied(dve, ("ab", m), e)
                    link(tt(four(hb[m_X]), four(hb[m_X]), rep4(C("ident")), ALU.add))
                    tt(four(hb[m_LV]), four(hb[m_AT]), rep4(C("level1")), ALU.mult).then_inc(sem(f"level{e}_ready"), 1)
                for lv in range(1, 6):
                    for e in range(2):
                        hb = h_buf[e]
                        filled(dve, (f"ZU{lv}", m), e)
                        if lv < 5:
                            filled(dve, (f"XU{lv}", m), e)
                        tt(hb[m_Z], hb[m_Z], PSB[bank_of((f"ZU{lv}", m), e)], ALU.add).then_inc(freed((f"ZU{lv}", m), e), 1)
                        if lv < 5:
                            tt(hb[m_X], hb[m_X], PSB[bank_of((f"XU{lv}", m), e)], ALU.add)\
                                .then_inc(freed((f"XU{lv}", m), e), 1)
                            tt(four(hb[m_LV]), four(hb[m_AT]), rep4(C(f"level{lv + 1}")), ALU.mult)\
                                .then_inc(sem(f"level{e}_ready"), 1)
                for e in range(2):
                    hb = h_buf[e]
                    for what, dst, mask in (("akT", m_X, "strict64"), ("rbT", m_AT, "incl64"), ("rkT", m_LV, "incl64")):
                        filled(dve, (what, m), e)
                        tt(four(hb[dst]), four(PSB[bank_of((what, m), e)]), rep4(C(mask)), ALU.mult)\
                            .then_inc(freed((what, m), e), 1)
                filled(dve, ("ry", m), 1)
                for e in range(2):
                    V.tensor_copy(proj((RR, KK_)[e] + m), PSB[bank_of(("ry", m), e)]).then_inc(freed(("ry", m), e), 1)
                for e in range(2):
                    h = 2 * m + e
                    emptied(dve, "last_decay", m)
                    o = gt_all[:, :, h, :]
                    link(tt(o, C("ident", CH, 0, CH).unsqueeze(1).to_broadcast([CH, NC, CH]),
                            pls[:, e * NC:(e + 1) * NC].unsqueeze(2).to_broadcast([CH, NC, CH]), ALU.mult))
                    for i in range(2):
                        filled(dve, ("gt", m), 2 * e + i)
                        tt(o[:, i::2, :], o[:, i::2, :],
                           PSB[bank_of(("gt", m), 2 * e + i)][0:CH, 0:256].rearrange("p (c i) -> p c i", c=NT), ALU.add)\
                            .then_inc(freed(("gt", m), 2 * e + i), 1)
            for i in range(4):
                emptied(dve, ("hh", 3), i)
            for cn in range(1, NC - 1):
                filled(dve, ("s", cn))
                o = h_all[:, cn, :, :]
                tt(o, o, PSB[bank_of(("s", cn))][0:CH, :].rearrange("p (h i) -> p h i", h=8), ALU.add)\
                    .then_inc(freed(("s", cn)), 1)
            filled(dve, "mod")
            tt(mod[:, :], PSB[7][:, 0:48], S("b_mod", 0, 48), ALU.add).then_inc(freed("mod"), 1)
            for m in range(4):
                emptied(dve, "rwkv_y", m)
                y = ew(0)
                filled(dve, f"sum_y{m}")
                stt(y, PSB[bank_of(f"sum_y{m}")], -1.0 / CH, y, ALU.mult, ALU.add).then_inc(freed(f"sum_y{m}"), 1)
                emptied(dve, f"sum_y{m}")
                tt(ew(2), y, y, ALU.mult).then_inc(sem("sq_y"), 1)
                rstd(f"sum_y2{m}", 1.0 / CH, 64e-5)
                link(tt(y, y, v_rs, ALU.mult))
                link(ts(y, y, S("ln_w", m), S("ln_b", m), ALU.mult, ALU.add))
                emptied(dve, f"sum_bonus{m}")
                link(tt(y, y, ym(4 + m), ALU.add))
                filled(dve, "gate", m)
                tt(ym(4 + m), y, PSB[bank_of("gate", m)], ALU.mult).then_inc(freed("gate", m), 1)
            if stop <= 2:
                return

            def squares(src, dst, name, n=KT):
                for k in range(n):
                    tt(dst(k), src(k), src(k), ALU.mult).then_inc(sem(name), 1)

            x_ = lambda k: res[:, k, :]
            n_ = lambda k: xn[:, k, :]
            sq = lambda k: A(SQ + k * T)
            sqb = lambda k: A(F_CMB + k * T)

            def add_normed(src, gain):
                for k in range(KT):
                    link(stt(src(k), src(k), S(gain, k), v_rs, ALU.mult, ALU.mult))
                    last = tt(x_(k), x_(k), src(k), ALU.add)
                link(last)

            for k in range(KT):
                emptied(dve, "mix", k)
                tt(sq(k), n_(k), n_(k), ALU.mult).then_inc(sem("sq_post_mix"), 1)
            rstd("sum_post_mix", 1.0 / D, 1e-6)
            add_normed(n_, "g_post_mix")
            squares(x_, sq, "sq_pre_ffn")
            V.memset(A(F_UB, 4 * PADW).rearrange("p (t c) -> p t c", t=4)[:, :, 0:3], 0.0).then_inc(sem("ffn_zeroed"), 1)
            link(V.memset(A(F_ACC, 4096), 0.0))
            rstd("sum_pre_ffn", 1.0 / D, 1e-6)
            for k in range(KT):
                stt(n_(k), x_(k), S("g_pre_ffn", k), v_rs, ALU.mult, ALU.mult).then_inc(sem("ffn_in_ready"), 1)

            def conv_gate(j, phase, sub, it=None):
                fc0 = at(j, 16, S0 + SMALL["ffn_conv"][0])

                def tap(i, k):
                    return fix[:, bass.ds(fc0 + (4 * i + k), 1)] if it is not None else \
                        fix[:, fc0 + 4 * i + k:fc0 + 4 * i + k + 1]

                if j != 0:
                    dve.wait_ge(sem("ffn_act_ready"), at(j, 2, 0))
                for i in range(4):
                    emptied(dve, "ffn_up", (phase, sub, i), it)
                    u, c = lambda s_: A(F_UB + i * PADW + 3 - s_), A(F_CB + i * T)
                    link(ts(c, u(0), tap(i, 2), tap(i, 3), ALU.mult, ALU.add))
                    link(stt(c, u(1), tap(i, 1), c, ALU.mult, ALU.add))
                    stt(c, u(2), tap(i, 0), c, ALU.mult, ALU.add).then_inc(sem("ffn_taps_used"), 1)
                for i in range(2):
                    dve.wait_ge(sem("ffn_silu_ready"), at(j, 2, i + 1))
                    if i == 0:
                        dve.wait_ge(sem("ffn_taps_used"), at(j, 4, 4))
                    tt(act_buf(sub, i), A(F_CB + i * T), A(F_CB + (2 + i) * T), ALU.mult)\
                        .then_inc(sem("ffn_act_ready"), 1)

            def accumulate(kind, phase, sub, it=None):
                for m in range(KT):
                    k = (phase, sub, m)
                    filled(dve, kind + "_down", k, it)
                    o = A(F_ACC + m * T)
                    tt(o, o, PSB[4 + m % 4], ALU.add).then_inc(freed(kind + "_down", k), 1)

            conv_gate(0, "first", 0)
            times = (NF - 1) // 2
            with dve.Fori(0, times) as it:
                ch.enter(it, 16)
                conv_gate((it, 1), "loop", 1, it)
                accumulate("ffn", "loop", 0, it)
                conv_gate((it, 2), "loop", 0, it)
                accumulate("ffn", "loop", 1, it)
            ch.leave(times)
            accumulate("ffn", "last", 0)
            emptied(dve, "ffn_down", ("last", 0, 6))
            emptied(dve, "ffn_down", ("last", 0, 7))
            acc = lambda k: A(F_ACC + k * T)
            squares(acc, sqb, "sq_post_ffn")
            rstd("sum_post_ffn", 1.0 / D, 1e-6)
            add_normed(acc, "g_post_ffn")
            squares(x_, sqb, "sq_1")

            def modulated(scale_at, shift_at, gain, name):
                link(stt(gmod[:, :], mod[:, scale_at:scale_at + KT], 1.0, S(gain, 0, KT), ALU.add, ALU.mult))
                for k in range(KT):
                    link(stt(n_(k), x_(k), gmod[:, k:k + 1], v_rs, ALU.mult, ALU.mult))
                    ts(n_(k), n_(k), mod[:, shift_at + k:shift_at + k + 1], None, ALU.add).then_inc(sem(name), 1)

            rstd("sum_1", 1.0 / D, 1e-6)
            modulated(8, 0, "g1", "h_ready")
            if stop <= 3:
                return
            filled(dve, "w_s")
            tt(four(A(g_WS)), four(PSB[bank_of("w_s")]), rep4(C("incl128")), ALU.mult).then_inc(freed("w_s"), 1)
            filled(dve, "gmlp_mean")
            for k in range(4):
                v = p2(AV + k)
                last = stt(v, PSB[bank_of("gmlp_mean")], -1.0 / T, v, ALU.mult, ALU.add)
                if k == 3:
                    last.then_inc(freed("gmlp_mean"), 1)
            emptied(dve, "gmlp_mean")
            for k in range(4):
                tt(A(g_SQ + k * T), p2(AV + k), p2(AV + k), ALU.mult).then_inc(sem("sq_gmlp"), 1)
            rstd("gmlp_var", 1.0 / T, 1e-6)
            for k in range(4):
                v = p2(AV + k)
                link(stt(v, v, S("gmlp_g", k), v_rs, ALU.mult, ALU.mult))
                ts(v, v, S("gmlp_b", k), None, ALU.add).then_inc(sem("gmlp_v_ready"), 1)
            for g in range(4):
                filled(dve, "mixed", g)
                tt(p2(AU + g), p2(AU + g), PSB[bank_of("mixed", g)], ALU.mult).then_inc(freed("mixed", g), 1)
            bt, et, qk = [[A(o + m * T) for m in range(2)] for o in (l_B, l_E, l_QK)]
            for m in range(2):
                filled(dve, "forget", m)
                ts(bt[m], PSB[bank_of("forget", m)], S("b_gate", m), None, ALU.add).then_inc(freed("forget", m), 1)
                emptied(dve, "forget", m)
                link(ts(et[m], bt[m], -1.0))
                tt(et[m], et[m], bt[m], ALU.min).then_inc(sem("forget_abs"), 1)
            V.memset(A(l_AT, 2048), 0.0)
            for m in range(2):
                dve.wait_ge(sem("forget_exp"), m + 1)
                log1p(qk[0], et[m], qk[1], A(l_KT))
                link(ts(bt[m], bt[m], -1.0, 0.0, ALU.mult, ALU.max))
                link(stt(bt[m], qk[0], 2.0, bt[m], ALU.mult, ALU.add))
                link(ts(et[m], bt[m], -1.0 / 16))
                link(V.tensor_tensor_scan(bt[m], C("carry128"), et[m], 0.0, ALU.mult, ALU.add))
            for m in range(2):
                emptied(dve, "p2", GQ + m)
                ts(p2(GQ + m), p2(GQ + m), 0.125).then_inc(sem("level_ready"), 1)
            dve.wait_ge(sem("level_ready"), 2)

            def merge_level(lv):
                mask = C("ident" if lv == 0 else f"level{lv - 1}").bitcast(mybir.dt.int32)
                for hh in range(4):
                    filled(dve, ("attn", lv), hh)
                    V.copy_predicated(four(A(l_AT + hh * T)), rep4(mask), four(PSB[bank_of(("attn", lv), hh)]))\
                        .then_inc(freed(("attn", lv), hh), 1)

            def level_logs(lv):
                hw = 1 << (lv - 1)
                v4 = lambda a: a.rearrange("p (b u h) -> p b u h", u=2, h=hw)
                for m in range(2):
                    b, e = v4(bt[m]), v4(et[m])
                    mid = b[:, :, 0, hw - 1:hw].to_broadcast([P, T // (2 * hw), hw])
                    link(tt(e[:, :, 1, :], b[:, :, 1, :], mid, ALU.subtract))
                    tt(e[:, :, 0, :], mid, b[:, :, 0, :], ALU.subtract).then_inc(sem("log_decay_ready"), 1)

            for lv in range(1, 8):
                hw = 1 << (lv - 1)
                v4 = lambda a: a.rearrange("p (b u h) -> p b u h", u=2, h=hw)
                level_logs(lv)
                merge_level(lv - 1)
                for m in range(2):
                    dve.wait_ge(sem("decay_ready"), 2 * (lv - 1) + m + 1)
                    emptied(dve, "p2", GK + m)
                    e, q_, k_, o = v4(et[m]), v4(p2(GQ + m)), v4(p2(GK + m)), v4(qk[m])
                    link(tt(o[:, :, 1, :], e[:, :, 1, :], q_[:, :, 1, :], ALU.mult))
                    tt(o[:, :, 0, :], e[:, :, 0, :], k_[:, :, 0, :], ALU.mult).then_inc(sem("level_ready"), 1)
            merge_level(7)
            c4 = lambda a: a.rearrange("p (c t) -> p c t", c=NT)
            for m in range(2):
                last = c4(bt[m])[:, :, P - 1:P].to_broadcast([P, NT, P])
                tt(c4(qk[m]), last, c4(bt[m]), ALU.subtract).then_inc(sem("log_decay_ready"), 1)
            for m in range(2):
                dve.wait_ge(sem("decay_ready"), 14 + 2 * m + 2)
                tt(qk[m], qk[m], p2(GK + m), ALU.mult).then_inc(sem("khat_ready"), 1)
            for m in range(2):
                st = A(l_ST + m * 384, 384)
                filled(dve, "gla_state", m)
                pst = PSB[bank_of("gla_state", m)]
                link(V.tensor_copy(st[:, 0:P], pst[:, 0:P]))
                for t in range(1, 3):
                    last = stt(st[:, t * P:(t + 1) * P], st[:, (t - 1) * P:t * P], et[m][:, t * P + P - 1:t * P + P],
                               pst[:, t * P:(t + 1) * P], ALU.mult, ALU.add)
                    if t == 1:
                        link(last)
                    else:
                        last.then_inc(freed("gla_state", m), 1)
                        emptied(dve, "gla_state", m)
                tt(et[m], et[m], p2(GQ + m), ALU.mult).then_inc(sem("gla_states_ready"), 1)
            for hh in range(4):
                filled(dve, "gla_o", hh)
                o = A(l_AT + hh * T)
                V.tensor_copy(o, PSB[bank_of("gla_o", hh)]).then_inc(freed("gla_o", hh), 1)
                emptied(dve, "gla_o", hh)
                tt(qk[hh % 2], o, o, ALU.mult).then_inc(sem("sq_gla"), 1)
                rstd(f"sum_gla{hh}", 1.0 / P, 1e-6)
                link(stt(o, o, S("gla_g"), v_rs, ALU.mult, ALU.mult))
                tt(p2(GR + hh), o, p2(GR + hh), ALU.mult).then_inc(sem("gla_out_ready"), 1)
            link(ts(qg[:, :], S("q_g"), float(P) ** -0.5))
            for i in range(8):
                t = p2(DQ + i)
                emptied(dve, "p2", DQ + i)
                tt(qk[i % 2], t, t, ALU.mult).then_inc(sem("sq_qk"), 1)
                rstd(f"sum_qk{i}", 1.0 / P, 1e-6)
                stt(t, t, qg[:, :] if i < 4 else S("k_g"), v_rs, ALU.mult, ALU.mult).then_inc(sem("qk_ready"), 1)
            ma = [A(d_MA + P * (t * (t + 1) // 2), (t + 1) * P) for t in range(NT)]
            link(V.tensor_copy(ma[0], C("neg128")))
            sc = A(d_SC)
            emptied(dve, "iw")
            for t in range(1, NT):
                n = (t + 1) * P
                for hh in range(4):
                    i = 4 * (t - 1) + hh
                    emptied(dve, ("index", t), hh)
                    r_, w_ = A(d_RL + (i % 2) * T, n), iw[:, t * 4 + hh:t * 4 + hh + 1]
                    if hh == 0:
                        ts(sc[:, 0:n], r_, w_).then_inc(sem("relu_used"), 1)
                    else:
                        stt(sc[:, 0:n], r_, w_, sc[:, 0:n], ALU.mult, ALU.add).then_inc(sem("relu_used"), 1)
                    dve.wait_ge(sem("relu_used"), i + 1)
                link(tt(sc[:, t * P:n], sc[:, t * P:n], C("neg128"), ALU.add))
                for _ in range(16):
                    link(V.max(top8[:, :], sc[:, 0:n]))
                    link(V.match_replace(sc[:, 0:n], top8[:, :], sc[:, 0:n], -3e38))
                link(ts(ma[t], sc[:, 0:n], -3e38, -1e30, ALU.is_gt, ALU.mult))

            def masked(i):
                hh, t = i // 4, i % 4
                n = (t + 1) * P
                lg = A(d_LG + (i % 2) * T, n)
                filled(dve, ("logits", hh), t)
                if i >= 2:
                    filled(dve, "pt", i - 2)
                tt(lg, PSB[bank_of(("logits", hh), t)][:, 0:n], ma[t], ALU.add).then_inc(freed(("logits", hh), t), 1)
                emptied(dve, ("logits", hh), t)
                V.tensor_reduce(nmax[:, i % 4:i % 4 + 1], lg, AX.X, ALU.max, negate=True).then_inc(sem("logits_ready"), 1)

            masked(0)
            for i in range(16):
                t = i % 4
                if i + 1 < 16:
                    masked(i + 1)
                dve.wait_ge(sem("exp_ready"), i + 1)
                lg = A(d_LG + (i % 2) * T, (t + 1) * P)
                link(V.reciprocal(rinv[:, t:t + 1], rsum[:, t:t + 1]))
                ts(lg, lg, rinv[:, t:t + 1]).then_inc(sem("probs_ready"), 1)
            if stop <= 4:
                return
            for n in range(3):
                for m in range(KT):
                    i = n * KT + m
                    g = A(s_SG2 + (i % 4) * T)
                    emptied(dve, ("gates", n), m)
                    filled(dve, ("branch", n), m)
                    up_ = PSB[bank_of(("branch", n), m)]
                    o = A(MG + m * T)
                    if n == 0:
                        tt(o, g, up_, ALU.mult).then_inc(freed(("branch", n), m), 1)
                    else:
                        tt(g, g, up_, ALU.mult).then_inc(freed(("branch", n), m), 1)
                        emptied(dve, ("branch", n), m)
                        tt(o, o, g, ALU.add).then_inc(sem("merged"), 1)
            for m in range(KT):
                filled(dve, "mix2", m)
                stt(x_(m), PSB[bank_of("mix2", m)], mod[:, 16 + m:17 + m], x_(m), ALU.mult, ALU.add)\
                    .then_inc(freed("mix2", m), 1)
                emptied(dve, "mix2", m)
                tt(A(m * T), x_(m), x_(m), ALU.mult).then_inc(sem("sq_2"), 1)
            rstd("sum_2", 1.0 / D, 1e-6)
            modulated(32, 24, "g2", "h2_ready")

            filled(dve, "route")
            lg = rt_l.rearrange("p (t c) -> p t c", t=NT)
            tt(lg, PSB[bank_of("route")][:, 0:80].rearrange("p (t c) -> p t c", t=NT), rep4(S("b_route", 0, 20)), ALU.add)\
                .then_inc(freed("route"), 1)
            emptied(dve, "route")
            ex, oh, sel, h1, h2 = [w.rearrange("p (t c) -> p t c", t=NT) for w in rt_w]
            mx, pg, none, v1, ev, w1, w2_, tmp, v2 = rt_s
            each = lambda a: a.unsqueeze(2).to_broadcast([P, NT, 4])

            def first_of(hot, vals, top):
                link(tt(hot, vals, each(top), ALU.is_equal))
                link(ts(none, hot[:, :, 0], -1.0, 1.0, ALU.mult, ALU.add))
                for c in range(1, 4):
                    link(tt(hot[:, :, c], hot[:, :, c], none, ALU.mult))
                    link(tt(none, none, hot[:, :, c], ALU.subtract))

            link(V.tensor_reduce(mx, lg[:, :, 0:4], AX.X, ALU.max))
            tt(ex, lg[:, :, 0:4], each(mx), ALU.subtract).then_inc(sem("route_diff"), 1)
            first_of(oh, lg[:, :, 0:4], mx)
            for g in range(4):
                part = lg[:, :, 4 + 4 * g:8 + 4 * g]
                hot = oh[:, :, g:g + 1].to_broadcast([P, NT, 4])
                if g == 0:
                    link(tt(sel, part, hot, ALU.mult))
                else:
                    link(tt(h1, part, hot, ALU.mult))
                    link(tt(sel, sel, h1, ALU.add))
            link(V.tensor_reduce(v1, sel, AX.X, ALU.max))
            first_of(h1, sel, v1)
            link(stt(sel, h1, -3e38, sel, ALU.mult, ALU.add))
            link(V.tensor_reduce(v2, sel, AX.X, ALU.max))
            first_of(h2, sel, v2)
            tt(ev, v2, v1, ALU.subtract).then_inc(sem("route_diff"), 1)
            dve.wait_ge(sem("route_exp"), 1)
            link(V.tensor_reduce(pg, ex, AX.X, ALU.add))
            dve.wait_ge(sem("route_exp"), 2)
            link(ts(w1, ev, 1.0, None, ALU.add))
            link(tt(w1, w1, pg, ALU.mult))
            link(V.reciprocal(w1, w1))
            link(tt(w2_, w1, ev, ALU.mult))
            link(tt(h1, h1, each(w1), ALU.mult))
            link(tt(h2, h2, each(w2_), ALU.mult))
            link(tt(h1, h1, h2, ALU.add))
            cm = rt_c.rearrange("p (t g c) -> p t g c", t=NT, g=4)
            for g in range(4):
                last = tt(cm[:, :, g, :], h1, oh[:, :, g:g + 1].to_broadcast([P, NT, 4]), ALU.mult)
            last.then_inc(sem("combine_ready"), 1)
            link(V.memset(A(F_ACC, 4096), 0.0))

            def expert_gate(j, phase, sub, it=None):
                off = at(j, T, F_CMB)
                cw = arena[:, bass.ds(off, T)] if it is not None else A(off)
                for i in range(2):
                    g = A(F_UB + i * T)
                    emptied(dve, "moe_up", (phase, sub, i), it)
                    filled(dve, "moe_up", (phase, sub, 2 + i), it)
                    if j == 0 and i == 0:
                        for e in range(NE - 4, NE):
                            emptied(dve, "weights", e)
                    tt(g, g, PSB[2 + i], ALU.mult).then_inc(freed("moe_up", (phase, sub, 2 + i)), 1)
                    emptied(dve, "moe_up", (phase, sub, 2 + i), it)
                    tt(act_buf(sub, i), g, cw, ALU.mult).then_inc(sem("moe_act_ready"), 1)

            expert_gate(0, "first", 0)
            with dve.Fori(0, (NE - 1) // 2) as it:
                expert_gate((it, 1), "loop", 1, it)
                accumulate("moe", "loop", 0, it)
                expert_gate((it, 2), "loop", 0, it)
                accumulate("moe", "loop", 1, it)
            expert_gate(NE - 1, "last", 1)
            accumulate("moe", "last", 0)
            accumulate("moe", "last", 1)
            for m in range(4, 8):
                emptied(dve, "moe_down", ("last", 1, m))
            for k in range(KT):
                stt(x_(k), acc(k), mod[:, 40 + k:41 + k], x_(k), ALU.mult, ALU.add).then_inc(sem("out_ready"), 1)


        @block.gpsimd
        def _(pool):
            pv = A(PROJ, N_PROJ * PADW).rearrange("p (t c) -> p t c", c=PADW)
            emptied(pool, "x", KT - 1)
            nc.gpsimd.memset(pv[:, :, 0:3], 0.0).then_inc(sem("pads_zeroed"), 1)

        @block.sync
        def _(sp):
            n_units = units.shape[0]
            for u in range(RING):
                sp.dma_start(ring[:, u, :], units[u, :, :]).then_inc(sem(f"weights{u}_loaded"), 16)
            whole = n_units // RING - 1
            with sp.Fori(0, whole) as i:
                for j in range(RING):
                    sp.wait_ge(sem("weights_used"), RING * i + j + 2)
                    sp.dma_start(ring[:, j, :], units[bass.ds(RING * i + RING + j, 1), :, :].rearrange("a p n -> (a p) n"))\
                        .then_inc(sem(f"weights{j}_loaded"), 16)
            for u in range(RING * (whole + 1), n_units):
                sp.wait_ge(sem("weights_used"), u - 1)
                sp.dma_start(ring[:, u % RING, :], units[u, :, :]).then_inc(sem(f"weights{u % RING}_loaded"), 16)
            if stop <= 4:
                return
            for i in range(8):
                emptied(sp, "out", i)
                sp.dma_start(out[(i // 2) * P:(i // 2 + 1) * P, (i % 2) * T:(i % 2 + 1) * T], A(OUT + i * T))\
                    .then_inc(sem("out_stored"), 16)
            sp.wait_ge(sem("out_stored"), 8 * 16)


def _columns(v):
    v = np.asarray(v).reshape(-1)
    pad = -len(v) % P
    return np.pad(v, (0, pad)).reshape(-1, P).T


def _units_1024(w):
    return w.reshape(KT, P, -1, 256).transpose(2, 1, 0, 3).reshape(-1, P, UNIT)


def _rwkv_tiles(a):
    r, w, k, v, lo, g = np.split(a, np.cumsum([512, 64, 512, 512, 64]), axis=-1)
    return np.concatenate([w, lo, g, r, k, v], axis=-1)


def _constants():
    f = np.float32
    s, t = np.arange(P)[:, None], np.arange(P)[None, :]
    out = {"ident": s == t, "ones": np.ones((P, P)), "blk64": s // CH == t // CH, "flip": s + t == P - 1,
           "strict64": (s < t) & (s // CH == t // CH), "incl64": (s <= t) & (s // CH == t // CH),
           "incl128": s <= t, "neg128": np.where(s >= t, 0.0, -1e30)}
    for k in range(7):
        h = 1 << k
        out[f"level{k}"] = (s // (2 * h) == t // (2 * h)) & (s % (2 * h) < h) & (t % (2 * h) >= h)
    out["level0t"] = out["level0"].T
    n = np.arange(T)[None, :] + np.zeros((P, 1))
    out["carry64"], out["carry128"] = n % CH != 0, n % P != 0
    c = np.arange(NE * P)[None, :]
    out["sel16"] = (c // P == s) & (s < NE)
    m = np.arange(2 * T)
    d = 511 - m
    large = np.minimum(16 + (np.log(np.maximum(d, 16) / 16.0) / np.log(8.0) * 16 + 1e-9).astype(np.int64), 31)
    bucket = np.where(d < 16, d, large)
    out["bucket"] = (bucket[None, :] == s) & (d >= 0)[None, :]
    return np.concatenate([np.broadcast_to(out[k], (P, w)).astype(f) for k, (_, w) in CONSTS.items()], 1)


def _prepare(i):
    i = {k: np.asarray(v) for k, v in i.items()}
    z = lambda r, c: np.zeros((r, c), np.float32)
    w = i["w_in"][0]
    zc, xbc, dtc, rw = np.split(w, [512, 1536, 1544], axis=1)
    cols = np.concatenate([xbc, dtc, z(D, P - 8), _rwkv_tiles(rw), zc, z(D, P)], 1)
    order = np.concatenate
    w2 = i["w_in_2"][0]
    a_u, a_v, g_q, g_k, g_v, g_r, g_a, d_q, d_k, d_v, d_iq, d_ik, d_iw, gates = np.split(
        w2, np.cumsum([512, 512, 256, 256, 512, 512, 16, 512, 512, 512, 256, 64, 4]), axis=1)
    cols2 = order([a_u, a_v, g_q, g_k, g_v, g_r, g_a, z(D, 16), d_iw, z(D, 92), d_q, d_k, d_v, d_iq, d_ik, d_ik], 1)
    up = i["ffn_w_up"][0]
    gu, vu = _units_1024(up[:, :D_FF]), _units_1024(up[:, D_FF:])
    down = i["ffn_w_down"][0].reshape(NF, 2, P, D).transpose(0, 2, 1, 3).reshape(NF, P, UNIT)
    eg = np.concatenate([_units_1024(i["w_exp_gate_2"][0, e]) for e in range(NE)])
    eu = np.concatenate([_units_1024(i["w_exp_up_2"][0, e]) for e in range(NE)])
    ed = i["w_exp_down_2"][0].reshape(NE, 2, P, D).transpose(0, 2, 1, 3).reshape(NE, P, UNIT)

    def steps(g, v, d):
        out = [g[0], v[0]]
        for k in range(1, len(g)):
            out += [g[k], v[k], d[k - 1]]
        return np.stack(out + [d[-1]])

    branch = []
    gate_units = _units_1024(gates)
    for n in range(3):
        b = i["w_branch_2"][0, n].reshape(4, P, 2, 512).transpose(2, 1, 0, 3).reshape(2, P, UNIT)
        for h in range(2):
            branch += [b[h], gate_units[4 * n + 2 * h], gate_units[4 * n + 2 * h + 1]]
    units = order([_units_1024(cols), _units_1024(i["w_mod_2"][0]), _units_1024(i["w_out"][0]), steps(gu, vu, down),
                   _units_1024(cols2), np.stack(branch), _units_1024(i["w_out_2"][0]), steps(eg, eu, ed)])
    mu = _rwkv_tiles(i["rwkv_mu"][0])
    fc = order([i["ffn_conv_w"][0], i["ffn_conv_b"]], 0)
    fc = fc.reshape(4, 2, NF, 2, P).transpose(4, 2, 1, 3, 0).reshape(P, 16 * NF)
    small = {
        "g_pre_mix": i["pre_mix_norm"], "g_post_mix": i["post_mix_norm"], "g_pre_ffn": i["pre_ffn_norm"],
        "g_post_ffn": i["post_ffn_norm"], "conv_w": i["ssd_conv_w"][0], "conv_b": i["ssd_conv_b"],
        "dt_bias": i["ssd_dt_bias"], "a_log": i["ssd_a_log"], "d_skip": np.repeat(i["ssd_d"][0], CH),
        "ssd_norm": i["ssd_norm"], "mu": mu, "w0": i["rwkv_w0"], "a0": i["rwkv_a0"], "k_k": i["rwkv_k_k"],
        "k_a": i["rwkv_k_a"], "r_k": i["rwkv_r_k"], "ln_w": i["rwkv_ln_w"], "ln_b": i["rwkv_ln_b"],
        "c": i["c_2"], "b_mod": i["b_mod_2"], "g1": i["g_norm1_2"], "g2": i["g_norm2_2"],
        "gmlp_g": i["gmlp_ln_g_2"], "gmlp_b": i["gmlp_ln_b_2"], "b_gate": i["gla_b_gate_2"],
        "gla_g": i["gla_norm_g_2"], "q_g": i["dsa_qnorm_g_2"], "k_g": i["dsa_knorm_g_2"],
        "b_branch": i["b_branch_gate_2"]}
    small = {k: _columns(v) for k, v in small.items()}
    small["b_route"] = np.broadcast_to(order([i["b_group_2"][0], i["b_router_2"][0]])[None], (P, 20))
    small["rel_bias"] = np.pad(i["rel_bias_2"], ((0, P - 32), (0, 0)))
    small["ffn_conv"] = fc
    for k, (_, n) in SMALL.items():
        assert small[k].shape == (P, n), (k, small[k].shape)
    route = order([i["w_group_2"][0], i["w_router_2"][0]], 1)
    mats = {"wa2": order([i["rwkv_w2"][0], i["rwkv_a2"][0]]), "g2m": i["rwkv_g2"][0],
            "gate2": np.pad(i["gla_w_gate2_2"][0], ((0, P - 16), (0, 0))),
            "w_s": i["gmlp_w_s_2"][0].transpose(1, 0, 2).reshape(P, 4 * P),
            "b_s": np.pad(i["gmlp_b_s_2"][0].reshape(1, T), ((0, P - 1), (0, 0))),
            "w_route": route.reshape(KT, P, 20).transpose(1, 0, 2).reshape(P, KT * 20)}
    fixed = order([_constants()] + [small[k] for k in SMALL] + [mats[k] for k in MATS], 1)
    return {"units": np.ascontiguousarray(units), "fixed": np.ascontiguousarray(fixed, dtype=np.float32),
            "x": np.ascontiguousarray(i["x"][0])}


def kernel(**inputs):
    import concourse.bacc as bacc
    from concourse.bass_utils import run_bass_kernel_spmd

    nc = bacc.Bacc("TRN2", target_bir_lowering=False, num_devices=1)
    arrays = _prepare(inputs)
    aps = [nc.dram_tensor(k, v.shape, F32, kind="ExternalInput").ap() for k, v in arrays.items()]
    skew = nc.dram_tensor("bias_rows", (4, 2 * T), F32, kind="Internal").ap()
    out = nc.dram_tensor("out", (T, D), F32, kind="ExternalOutput").ap()
    build(nc, *aps, skew, out)
    r = run_bass_kernel_spmd(nc, [arrays], core_ids=[0])
    return r.results[0]["out"].reshape(1, T, D)
```

```python
from contextlib import ExitStack

import numpy as np
import concourse.bass as bass
from concourse import mybir

F32 = mybir.dt.float32
F32R = mybir.dt.float32r
ALU = mybir.AluOpType
ACT = mybir.ActivationFunctionType
AX = mybir.AxisListType

T = 512
P = 128
NT = T // P
D = 1024
KT = D // P
UNIT = 2048
CHUNK = UNIT // 2
RING = 2
PADW = 516
D_FF = 2816
NF = D_FF // 256
NE = 16
GATE_ROUNDS = (3, 4, 5, 7, 9, 10, 12, 14)
N_MOD = 6 * D // 256
MOD_BATCH = N_MOD // 4
CH = 64
NC = T // CH
EXP_HALF = 0.6065306597126334
LOG1P_TERMS = 7

XS, BM, CM, DT, WA, GL, RR, KK_, VV, ZZ, N_PROJ = 0, 4, 6, 8, 9, 10, 11, 15, 19, 23, 28
AU, AV, GQ, GK, GV, GR, MISC, DQ, DK, DV, IQ, IK = 0, 4, 8, 10, 12, 16, 20, 21, 25, 29, 33, 35


def layout(sizes):
    at, out = 0, {}
    for name, width in sizes:
        out[name] = (at, width)
        at += width
    return out, at


CONSTS, N_CONST = layout(
    [("ident", P), ("ones", P), ("blk64", P), ("flip", P), ("strict64", P), ("incl64", P), ("incl128", P),
     ("level0t", P)] + [(f"level{k}", P) for k in range(7)] +
    [("carry64", T), ("carry128", T), ("sel16", NE * P), ("bucket", 2 * T), ("neg128", P)])
SMALL, N_SMALL = layout(
    [("g_pre_mix", KT), ("g_post_mix", KT), ("g_pre_ffn", KT), ("g_post_ffn", KT),
     ("conv_w", 4 * 8), ("conv_b", 8), ("dt_bias", 1), ("a_log", 1), ("d_skip", 4), ("ssd_norm", 4),
     ("mu", 14), ("w0", 4), ("a0", 4), ("k_k", 4), ("k_a", 4), ("r_k", 4), ("ln_w", 4), ("ln_b", 4),
     ("c", KT), ("b_mod", 48), ("g1", KT), ("g2", KT), ("gmlp_g", 4), ("gmlp_b", 4),
     ("b_gate", 2), ("gla_g", 1), ("q_g", 1), ("k_g", 1), ("b_branch", 24),
     ("b_route", 20), ("rel_bias", 4), ("ffn_conv", 16 * NF)])
MATS, N_MATS = layout(
    [("wa2", T), ("g2m", T), ("gate2", 256), ("w_s", 4 * P), ("b_s", T), ("w_route", KT * 20 + P - 16)])
N_TINY = 560
C0, S0, M0 = 0, N_CONST, N_CONST + N_SMALL
N_FIX = N_CONST + N_SMALL + N_MATS


def build(nc, units, fixed, x, skew, out, dbg=None, stop=99):
    ctx = ExitStack()
    with ctx:
        ring = ctx.enter_context(nc.sbuf_tensor("weight_ring", [P, RING, UNIT], F32))
        fix = ctx.enter_context(nc.sbuf_tensor("fixed_data", [P, N_FIX], F32))
        res = ctx.enter_context(nc.sbuf_tensor("residual", [P, KT, T], F32))
        xn = ctx.enter_context(nc.sbuf_tensor("normed", [P, KT, T], F32))
        xn_at = nc.sbuf_base - 4 * KT * T
        tiny = ctx.enter_context(nc.sbuf_tensor("tiny", [P, 1024], F32))
        n_arena = 30176
        arena = ctx.enter_context(nc.sbuf_tensor("arena", [P, n_arena], F32))
        arena_at = nc.sbuf_base - 4 * n_arena
        ps = ctx.enter_context(nc.psum_tensor("psum", [P, 8, T], F32))

        sems = {}

        def sem(name):
            if name not in sems:
                sems[name] = ctx.enter_context(nc.semaphore(name))
            return sems[name]

        def C(name, rows=P, a=0, b=None):
            o, w = CONSTS[name]
            return fix[0:rows, C0 + o + a:C0 + o + (w if b is None else b)]

        def S(name, j=0, n=1, rows=P):
            o, _ = SMALL[name]
            return fix[0:rows, S0 + o + j:S0 + o + j + n]

        def M(name, r0=0, r1=P, a=0, b=None):
            o, w = MATS[name]
            return fix[r0:r1, M0 + o + a:M0 + o + (w if b is None else b)]

        def A(off, n=T, r0=0, r1=P):
            assert off + n <= n_arena, (off, n, n_arena)
            return arena[r0:r1, off:off + n]

        def four(ap):
            return ap.rearrange("p (a b) -> p a b", a=4)

        def rep4(ap):
            return ap.unsqueeze(1).to_broadcast([ap.shape[0], 4, ap.shape[1]])

        full = [sem(f"bank{b}_full") for b in range(8)]
        free = [sem(f"bank{b}_free") for b in range(8)]
        used = [0] * 8
        place = {}

        def bank_of(what, k=0):
            return place[what, k][0]

        def filled(eng, what, k=0, it=None):
            b, n, per = place[what, k]
            eng.wait_ge(full[b], n + 1 if it is None else it * per + (n + 1))

        def emptied(eng, what, k=0, it=None):
            b, n, per = place[what, k]
            eng.wait_ge(free[b], n + 1 if it is None else it * per + (n + 1))

        def freed(what, k=0):
            return free[place[what, k][0]]

        class Chain:

            def __init__(self, eng, name):
                self.eng, self.sem, self.n, self.it, self.per = eng, sem(name), 0, None, 0

            def link(self, ins):
                self.n += 1
                ins.then_inc(self.sem, 1)
                self.eng.wait_ge(self.sem, self.n if self.it is None else self.it * self.per + self.n)

            def enter(self, it, per):
                self.it, self.per, self.at = it, per, self.n

            def leave(self, times):
                assert self.n - self.at == self.per, (self.n - self.at, self.per)
                self.n = self.at + self.per * times
                self.it = None

        def part(name, off, cols, base=None):
            return nc.alloc_sbuf_tensor_at(name, [P, cols], F32R, offset=(arena_at if base is None else base) + 4 * off)

        class Weights:

            def __init__(self, name, off):
                self.hi, self.lo = part(name + "_hi", off, 2 * CHUNK), part(name + "_lo", off + 2 * CHUNK, 2 * CHUNK)

            def slot(self, q):
                c = slice(q % 2 * CHUNK, (q % 2 + 1) * CHUNK)
                return self.hi[:, c], self.lo[:, c]

        class Tiles:

            def __init__(self, name, n, lo_off, hi=None, hi_off=None):
                self.off = lo_off
                self.his = hi if hi is not None else part(name + "_hi", hi_off, n * T)
                self.los = part(name + "_lo", lo_off, n * T)

            def raw(self, k):
                return A(self.off + k * T)

            def hi(self, k):
                return self.his[:, k * T:(k + 1) * T]

            def lo(self, k):
                return self.los[:, k * T:(k + 1) * T]

        x_hi = part("normed_hi", 0, KT * T, xn_at)

        PROJ = 0
        YM = N_PROJ * PADW
        WK = YM + 8 * T

        def proj(t, r0=0, r1=P, shift=0):
            return A(PROJ + t * PADW + 3 - shift, T, r0, r1)

        def ym(t, r0=0, r1=P):
            return A(YM + t * T, T, r0, r1)

        XT = PROJ
        SQ = WK
        SQ1 = 8208
        in1 = Tiles("in1", KT, WK, x_hi)
        w_in1 = Weights("w_in1", WK + 4096)
        CONV = WK + 8192
        y1 = Tiles("y1", KT, YM, None, WK + 6144)
        w_out1 = Weights("w_out1", WK + 2048)
        s_XD, s_XS2, s_BT, s_SI, s_GT, s_HB, s_CE, s_TC = [
            WK + o for o in (0, 2048, 4096, 5120, -1024, 6656, 7680, 8704)]
        def ew(i, r0=0, r1=P):
            return A(WK + i * T, T, r0, r1)

        e_W, e_P, e_INV, e_B, e_KK, e_AT, e_BH, e_KH, e_BP, e_KP = range(10)

        def tm(i):
            return A(WK + 5120 + i * T).rearrange("p (t c) -> p t c", t=NT)

        t_A, t_BP, t_KP, t_V = range(4)
        h_buf = [[A(WK + 7168 + i * T) for i in range(4)] + [proj(ZZ + 1), proj(ZZ + 2)], [ew(i) for i in (e_W, e_P, e_INV, e_B, e_KK, e_KP)]]
        m_AT, m_LV, m_X, m_Z, m_U, m_AW = range(6)
        gt_all = xn[0:CH, :, :].rearrange("p a b -> p (a b)").rearrange("p (c h i) -> p c h i", c=NC, h=8)
        h_all = A(PROJ, 4096, 0, CH).rearrange("p (c h i) -> p c h i", c=NC, h=8)
        TW = PROJ + DT * PADW
        SG = PROJ + ZZ * PADW

        MOD_PARTS = (ZZ + 3, ZZ + 4, GL)

        def mod_part(i):
            return proj(MOD_PARTS[i // 2])[:, (i % 2) * 256:(i % 2 + 1) * 256]

        F_UB, F_CB, F_ACC, F_ACT, F_CMB, F_IN, F_W, F_RT = 0, 2064, 4112, 8208, 12304, 20496, 24592, 28688
        in_ff = Tiles("in_ff", KT, F_IN, x_hi)
        w_ff = Weights("w_ff", F_W)
        acts = Tiles("acts", 4, F_ACT, None, F_ACT + 2048)
        N_ROUTE = MATS["w_route"][1]
        route_hi, route_lo = part("w_route_hi", F_RT, N_ROUTE), part("w_route_lo", F_RT + N_ROUTE, N_ROUTE)

        class Pair:

            def __init__(self, sub):
                self.hi, self.lo = (lambda i: acts.hi(2 * sub + i)), (lambda i: acts.lo(2 * sub + i))

        acts_of = [Pair(0), Pair(1)]

        def at(j, m, k):
            return m * j + k if isinstance(j, int) else j[0] * (2 * m) + (m * j[1] + k)

        def p2(t, r0=0, r1=P):
            return A(t * T, T, r0, r1)

        W2 = 36 * T
        g_VT, g_WS, g_SQ = W2, W2 + 2048, W2
        l_B, l_E, l_QK, l_AT, l_KT, l_ST, l_VT = W2, W2 + 1024, W2 + 2048, W2 + 3072, W2 + 5120, W2 + 6144, GV * T
        sq_gla = [A(l_AT + i * T) for i in range(4)]
        sq_qk = [A(W2 + i * T) for i in range(6)] + [A(l_KT + i * T) for i in range(2)]
        d_MA, d_SC, d_RL, d_LG, d_PT, d_HK = [W2 + o for o in (0, 1280, 2432, 1280, 2304, 3552)]
        d_VT, d_BR = DV * T, (DV + 2) * T
        SQ2 = AU * T
        MG = GQ * T
        sig = [[t * T for t in (IQ, IQ + 1, IK, MISC)]] + [[W2 + 4096 + i * T for i in range(4)]] * 2
        in2 = Tiles("in2", KT, n_arena - 4096, x_hi)
        w_in2 = Weights("w_in2", n_arena - 8192)
        w_br = [Weights("w_br0", W2 + 3552)] + [Weights("w_br", DK * T)] * 2
        ys = [Tiles("ya", 4, AU * T, None, AV * T), Tiles("yb", 4, GR * T, None, AV * T),
              Tiles("yc", 4, DQ * T, None, AU * T)]
        merged2 = Tiles("merged2", KT, MG, None, W2)
        OUT = 0

        v_tmp = tiny[:, 0:T]
        v_rs = tiny[:, T:2 * T]

        sm_o = [0]
        smalls = ctx.enter_context(nc.sbuf_tensor("smalls", [P, N_TINY], F32))

        def small(n, rows=P):
            o = sm_o[0]
            sm_o[0] += n
            assert sm_o[0] <= N_TINY
            return smalls[0:rows, o:o + n]

        dec3 = small(96)
        expA = small(1)
        one_ka = small(4)
        pls = small(16, CH)
        csil = small(KT)
        c_last = small(32)
        mod = small(48)
        gmod = small(KT)
        qg = small(1)
        row_rs = [dec3[:, 0:16], dec3[:, 16:48]]
        iw = small(16)
        top8 = small(24)
        nmax = small(4)
        rsum = small(4)
        rinv = small(4)
        rt_l, rt_c = small(80), small(64)
        rt_w = [small(16) for _ in range(5)]
        rt_s = [small(4) for _ in range(9)]

        block = ctx.enter_context(nc.Block())
        PSB = [ps[:, b, :] for b in range(8)]


        @block.tensor
        def _(pe):
            chunk = [0]

            def mm(o, l, r, start=True, stop=True):
                return nc.tensor.matmul(o, l, r, start=start, stop=stop)

            def tr(o, i):
                k = i.shape[0]
                return nc.tensor.transpose(o, i, C("ident", k, 0, k))

            def open_(what, k, b, it=None, per=0):
                if used[b]:
                    pe.wait_ge(free[b], used[b] if it is None else it * per + used[b])
                place[what, k] = (b, used[b], per)
                used[b] += 1
                return PSB[b]

            def close(last, what, k=0):
                last.then_inc(full[place[what, k][0]], 1)

            def take(weights, it=None, per=0):
                q = chunk[0]
                chunk[0] += 1
                pe.wait_ge(sem("split_ready"), q + 1 if it is None else it * per + (q + 1))
                return weights.slot(q)

            def norm_sum(what, srcs, ones, ready, b=4):
                o = open_(what, 0, b)
                for k, src in enumerate(srcs):
                    pe.wait_ge(*ready(k))
                    last = mm(o, ones, src, k == 0, k == len(srcs) - 1)
                close(last, what)

            def tile_of(w, nk, width, col, rhs, o, first, ready=None):
                hi, lo = [part_.rearrange("p (k c) -> p k c", k=nk) for part_ in w]
                c = slice(col, col + P)
                for k in range(nk):
                    if ready:
                        pe.wait_ge(sem(ready), k + 1)
                    begun = mm(o, hi[:, k, c], rhs.hi(k), k == 0, False)
                    if first and k == 0:
                        begun.then_inc(sem("split_used"), 1)
                    mm(o, lo[:, k, c], rhs.hi(k), False, False)
                    last = mm(o, hi[:, k, c], rhs.lo(k), False, k == nk - 1)
                return last

            def project(what, n_units, weights, rhs, t0=0, b0=0, nb=4, ready=None):
                for i in range(2 * n_units):
                    w = take(weights)
                    o = open_(what, t0, b0 + t0 % nb)
                    close(tile_of(w, KT, P, 0, rhs, o, True, None if i else ready), what, t0)
                    t0 += 1

            def modulation(m):
                pe.wait_ge(sem("mod_part_ready"), MOD_BATCH * (m + 1))
                for i in range(MOD_BATCH):
                    for j in range(2):
                        c = 2 * (MOD_BATCH * m + i) + j
                        last = mm(PSB[7][:, c:c + 1], mod_part(i)[:, j * P:(j + 1) * P], C("ones", b=1))
                if m == 3:
                    close(last, "mod")
                else:
                    last.then_inc(sem("mod_parts_used"), 1)

            pe.wait_ge(sem("fixed_loaded"), 16)
            pe.wait_ge(sem("x_loaded"), 16)
            for k in range(KT):
                o = open_("x", k, k % 4)
                for t in range(NT):
                    last = tr(o[:, t * P:(t + 1) * P], A(XT + t * D + k * P, P))
                close(last, "x", k)
            norm_sum("sum_pre_mix", [A(SQ + k * T) for k in range(KT)], C("ones"), lambda k: (sem("sq_pre_mix"), k + 1))
            project("proj", 14, w_in1, in1, ready="xn_ready")

            pe.wait_ge(sem("dt_ready"), 1)
            o = open_("dec3", 0, 4)
            for i in range(3):
                for t in range(NT):
                    last = tr(o[:, (i * NT + t) * 8:(i * NT + t + 1) * 8], ym([0, 1, 2][i], 0, 8)[:, t * P:(t + 1) * P])
            close(last, "dec3")
            pe.wait_ge(sem("xbc_ready"), 8)
            for t in range(NT):
                o = open_("xs_tm", t, t)
                for k in range(4):
                    last = tr(o[:, k * P:(k + 1) * P], proj(XS + k)[:, t * P:(t + 1) * P])
                close(last, "xs_tm", t)
            for i in range(2):
                o = open_("b_tm", i, 5 + i)
                for t in range(2):
                    for g in range(2):
                        last = tr(o[:, (t * 2 + g) * P:(t * 2 + g + 1) * P],
                                  proj(BM + g)[:, (2 * i + t) * P:(2 * i + t + 1) * P])
                close(last, "b_tm", i)
            for g in range(2):
                o = open_("scores", g, 5 + g)
                for t in range(NT):
                    c = slice(t * P, (t + 1) * P)
                    last = mm(o[:, c], proj(BM + g)[:, c], proj(CM + g)[:, c])
                close(last, "scores", g)
            emptied(pe, "b_tm", 1)
            pe.wait_ge(sem("xs2_ready"), NT)
            for t in range(3):
                o = open_("state", t, t)
                for g in range(2):
                    last = mm(o[:, g * 256:(g + 1) * 256], A(s_BT, 1024)[:, (t * 2 + g) * P:(t * 2 + g + 1) * P],
                              A(s_XS2, 2048)[:, t * T + g * 256:t * T + (g + 1) * 256])
                close(last, "state", t)

            def cs_row(h):
                close(mm(open_("cs_row", h, 5 + h % 2), C("sel16", 8, h * P, (h + 1) * P), ym(1, 0, 8)), "cs_row", h)

            o = open_("chunk_decay", 0, 7)
            for h in range(8):
                last = mm(o[:, h * NT:(h + 1) * NT], C("sel16", 8, h * P, (h + 1) * P), ym(1, 0, 8)[:, P - 1::P])
            close(last, "chunk_decay")
            cs_row(0)
            cs_row(1)
            for h in range(8):
                m, e = h // 2, h % 2
                if e == 0:
                    o = open_("ssd_y", m, m)
                pe.wait_ge(sem("mt_ready"), h + 1)
                rows = o[e * CH:(e + 1) * CH, :]
                for t in range(NT):
                    c = slice(t * P, (t + 1) * P)
                    last = mm(rows[:, c], A(s_XD, 2048)[:, t * T + h * CH:t * T + (h + 1) * CH],
                              A(s_HB + (h % 2) * T)[:, c], True, t == 0)
                    if t:
                        last = mm(rows[:, c], A(s_SI + (t - 1) * T)[:, h * CH:(h + 1) * CH],
                                  A(s_CE + (h % 2) * T)[:, c], False, True)
                if e:
                    close(last, "ssd_y", m)
                else:
                    last.then_inc(sem("ssd_head_used"), 1)
                if h + 2 < 8:
                    cs_row(h + 2)
            for g in range(2):
                norm_sum(f"sum_ssd{g}", [A(s_XD + (2 * g + i) * T) for i in range(2)], C("ones"),
                         lambda i: (sem("sq_ssd"), 2 * g + i + 1))

            open_("mod", 0, 7)
            for m in range(4):
                c = slice(m * P, (m + 1) * P)
                pe.wait_ge(sem("tanh_ready"), 1)
                close(mm(open_("w_low", m, 0), M("wa2", 0, CH)[:, c], A(TW, T, 0, CH)), "w_low", m)
                close(mm(open_("a_low", m, 1), M("wa2", CH, P)[:, c], proj(WA, CH, P)), "a_low", m)
                norm_sum(f"sum_kk{m}", [ew(e_BP)], C("blk64"), lambda _: (sem("sq_kk"), m + 1))
                norm_sum(f"sum_bonus{m}", [ew(e_BP)], C("blk64"), lambda _: (sem("bonus_in"), m + 1), 5)
                pe.wait_ge(sem("pair_ready"), m + 1)
                o = open_("last_decay", m, 0)
                for e in range(2):
                    r = slice(e * CH, (e + 1) * CH)
                    last = mm(o[0:CH, e * NC:(e + 1) * NC], C("ident")[:, r], ew(e_P)[:, CH - 1::CH])
                close(last, "last_decay", m)
                for i, src in enumerate((ew(e_AT), ew(e_BP), ew(e_KP), proj(VV + m))):
                    o = open_(("tm", m), i, 1 + i)
                    for t in range(NT):
                        last = tr(o[:, t * P:(t + 1) * P], src[:, t * P:(t + 1) * P])
                    close(last, ("tm", m), i)

                def gram(what, e, b, l, r):
                    o = open_((what, m), e, b)
                    rows = slice(e * CH, (e + 1) * CH)
                    for t in range(NT):
                        c = slice(t * P, (t + 1) * P)
                        last = mm(o[:, c], l[rows, c], r[rows, c])
                    close(last, (what, m), e)

                def units4(what, e, b, l, r):
                    o = open_((what, m), e, b)
                    for t in range(NT):
                        c = slice(t * P, (t + 1) * P)
                        last = mm(o[:, c], l[:, c], r[:, c])
                    close(last, (what, m), e)

                for e in range(2):
                    gram("abT", e, 5 + e, ew(e_BH), ew(e_AT))
                for e in range(2):
                    gram("ab", e, 1 + e, ew(e_AT), ew(e_BH))
                for lv in range(1, 6):
                    if lv == 5:
                        modulation(m)
                    for e in range(2):
                        hb = h_buf[e]
                        pe.wait_ge(sem(f"level{e}_ready"), 5 * m + lv)
                        units4(f"U{lv}", e, 3 * e, hb[m_LV], hb[m_X])
                    for e in range(2):
                        hb = h_buf[e]
                        emptied(pe, (f"U{lv}", m), e)
                        units4(f"ZU{lv}", e, 3 * e + 1, hb[m_U], hb[m_Z])
                        if lv < 5:
                            units4(f"XU{lv}", e, 3 * e + 2, hb[m_Z], hb[m_U])
                for e in range(2):
                    gram("akT", e, 3 * e, ew(e_KH), ew(e_AT))
                    gram("rbT", e, 3 * e + 1, ew(e_BH), proj(RR + m))
                    gram("rkT", e, 3 * e + 2, ew(e_KH), proj(RR + m))
                for e in range(2):
                    hb, r = h_buf[e], slice(e * CH, (e + 1) * CH)
                    emptied(pe, ("akT", m), e)
                    o = open_(("wv", m), e, 3 * e)
                    for t in range(NT):
                        last = mm(o[:, t * CH:(t + 1) * CH], hb[m_X][:, t * P:(t + 1) * P], tm(t_V)[:, t, r])
                    close(last, ("wv", m), e)
                for e in range(2):
                    hb = h_buf[e]
                    emptied(pe, ("wv", m), e)
                    units4("aw", e, 3 * e, hb[m_Z], hb[m_U])
                for e in range(2):
                    hb, r = h_buf[e], slice(e * CH, (e + 1) * CH)
                    emptied(pe, ("rkT", m), e)
                    emptied(pe, ("aw", m), e)
                    o = open_(("ry", m), e, 3 * e + 1)
                    for t in range(NT):
                        c = slice(t * P, (t + 1) * P)
                        mm(o[:, c], hb[m_AW][:, c], hb[m_AT][:, c], True, False)
                        mm(o[CH:P, c], tm(t_V)[:, t, r], hb[m_LV][:, c], False, True)
                        last = mm(o[0:CH, c], C("ident")[:, r], proj(RR + m)[:, c], False, True)
                    close(last, ("ry", m), e)
                    b = ((0, 2, 3, 5), (6, 0, 2, 3))[e]
                    for i in range(2):
                        q = slice(i * CH, (i + 1) * CH)
                        a = four(hb[m_AW])
                        og = open_(("gt", m), 2 * e + i, b[i])
                        for t in range(NT):
                            last = mm(og[0:CH, t * CH:(t + 1) * CH], a[q, t, 0:CH], tm(t_BP)[q, t, r])
                        close(last, ("gt", m), 2 * e + i)
                    for i in range(2):
                        q = slice(i * CH, (i + 1) * CH)
                        oh = open_(("hh", m), 2 * e + i, b[2 + i])
                        for t in range(NT):
                            c = slice(t * CH, (t + 1) * CH)
                            mm(oh[0:CH, c], tm(t_BP)[q, t, r], a[q, t, CH:P], True, False)
                            last = mm(oh[0:CH, c], tm(t_KP)[q, t, r], tm(t_V)[q, t, r], False, True)
                        close(last, ("hh", m), 2 * e + i)
            for i in range(4):
                emptied(pe, ("hh", 3), i)
            for cn in range(1, NC - 1):
                if cn > 1:
                    emptied(pe, ("s", cn - 1))
                o = open_(("s", cn), 0, 0)
                for h in range(8):
                    last = mm(o[0:CH, h * CH:(h + 1) * CH], gt_all[:, cn, h, :], h_all[:, cn - 1, h, :])
                close(last, ("s", cn))
            emptied(pe, ("s", NC - 2))
            for m in range(4):
                o = open_("rwkv_y", m, 1 + m % 2)
                for e in range(2):
                    rows = o[e * CH:(e + 1) * CH, :]
                    ry = proj((RR, KK_)[e] + m)
                    mm(rows, C("ident")[:, CH:P], ry, True, False)
                    for cn in range(1, NC):
                        c = slice(cn * CH, (cn + 1) * CH)
                        last = mm(rows[:, c], h_all[:, cn - 1, 2 * m + e, :], ry[0:CH, c], False, cn == NC - 1)
                close(last, "rwkv_y", m)
                norm_sum(f"sum_y{m}", [ew(0)], C("blk64"), lambda _: (freed("rwkv_y", m), place["rwkv_y", m][1] + 1), 3)
                norm_sum(f"sum_y2{m}", [ew(2)], C("blk64"), lambda _: (sem("sq_y"), m + 1), 4)
                pe.wait_ge(sem("sg_ready"), 1)
                close(mm(open_("gate", m, 5), M("g2m", a=m * P, b=(m + 1) * P), A(SG)), "gate", m)
            if stop <= 2:
                return
            pe.wait_ge(sem("ssd_out_ready"), 4)
            project("mix", 4, w_out1, y1, ready="y_ready")


            def sums(what, names, ready):
                norm_sum(what, names, C("ones"), lambda k: (sem(ready), k + 1))

            sq8 = [A(SQ1 + k * T) for k in range(KT)]
            sums("sum_post_mix", sq8, "sq_post_mix")
            sums("sum_pre_ffn", sq8, "sq_pre_ffn")
            def up(kind, phase, sub, it=None, ready=None):
                for i in range(4):
                    w = take(w_ff, it, 12)
                    k = (phase, sub, i)
                    o = open_(kind + "_up", k, i, it, 2)
                    close(tile_of(w, KT, P, 0, in_ff, o, True, None if i else ready), kind + "_up", k)

            def down(kind, phase, j, it=None):
                sub = j % 2 if isinstance(j, int) else j[1] % 2
                pe.wait_ge(sem(kind + "_act_ready"), at(j, 2, 2))
                for m in range(KT):
                    if m % 4 == 0:
                        w = take(w_ff, it, 12)
                    k = (phase, sub, m)
                    o = open_(kind + "_down", k, 4 + m % 4, it, 4)
                    close(tile_of(w, 2, T, m % 4 * P, acts_of[sub], o, m % 4 == 0), kind + "_down", k)

            def gated(kind, n):
                times = (n - 1) // 2
                with pe.Fori(0, times) as it:
                    up(kind, "loop", 1, it)
                    down(kind, "loop", (it, 0), it)
                    up(kind, "loop", 0, it)
                    down(kind, "loop", (it, 1), it)
                for b in range(8):
                    used[b] += (2 if b < 4 else 4) * (times - 1)
                chunk[0] += 12 * (times - 1)
                if n % 2 == 0:
                    up(kind, "last", 1)
                    down(kind, "last", n - 2)
                down(kind, "last", n - 1)

            up("ffn", "first", 0, ready="ffn_in_ready")
            gated("ffn", NF)
            sq8b = [A(F_CMB + k * T) for k in range(KT)]
            sums("sum_post_ffn", sq8b, "sq_post_ffn")
            sums("sum_1", sq8b, "sq_1")
            if stop <= 3:
                return
            for i in range(2):
                close(mm(open_("bias_row", i, 4 + i)[0:4, :], S("rel_bias", 0, 4), C("bucket", P, i * T, (i + 1) * T)),
                      "bias_row", i)
            project("p2", 4, w_in2, in2, ready="h_ready")
            o = open_("w_s", 0, 6)
            for g in range(4):
                last = tr(o[:, g * P:(g + 1) * P], M("w_s")[:, g * P:(g + 1) * P])
            close(last, "w_s")
            project("p2", 3, w_in2, in2, 8)
            norm_sum("gmlp_mean", [p2(AV + k) for k in range(4)], C("ones"), lambda k: (free[bank_of("p2", AV + k)], place["p2", AV + k][1] + 1))
            project("p2", 2, w_in2, in2, 14)
            sums("gmlp_var", [A(g_SQ + k * T) for k in range(4)], "sq_gmlp")
            project("p2", 2, w_in2, in2, 18)
            pe.wait_ge(sem("gmlp_v_ready"), 4)
            for t in range(NT):
                o = open_("gmlp_vt", t, 4 + t)
                for k in range(4):
                    last = tr(o[:, k * P:(k + 1) * P], p2(AV + k)[:, t * P:(t + 1) * P])
                close(last, "gmlp_vt", t)
            emptied(pe, "w_s")
            for t in range(NT):
                emptied(pe, "gmlp_vt", t)
            for g in range(4):
                o = open_("mixed", g, 4 + g)
                for t in range(NT):
                    c = slice(t * P, (t + 1) * P)
                    mm(o[:, c], A(g_VT, 2048)[:, t * T + g * P:t * T + (g + 1) * P], A(g_WS)[:, g * P:(g + 1) * P], True, False)
                    last = mm(o[:, c], C("ones"), M("b_s")[:, g * P:(g + 1) * P], False, True)
                close(last, "mixed", g)
            emptied(pe, "p2", MISC)
            for m in range(2):
                close(mm(open_("forget", m, 4 + m), M("gate2")[:, m * P:(m + 1) * P], p2(MISC)), "forget", m)
            project("p2", 7, w_in2, in2, 22)
            for t in range(NT):
                o = open_("gla_vt", t, 4 + t)
                for k in range(4):
                    last = tr(o[:, k * P:(k + 1) * P], p2(GV + k)[:, t * P:(t + 1) * P])
                close(last, "gla_vt", t)
            for lv in range(8):
                for m in range(2):
                    pe.wait_ge(sem("level_ready"), 2 * lv + m + 1)
                    for e in range(2):
                        r = slice(e * CH, (e + 1) * CH)
                        o = open_(("attn", lv), 2 * m + e, 2 * m + e)
                        for t in range(NT):
                            c = slice(t * P, (t + 1) * P)
                            if lv:
                                l = rr = A(l_QK + m * T)
                            else:
                                l, rr = p2(GK + m), p2(GQ + m)
                            last = mm(o[:, c], l[r, c], rr[r, c])
                        close(last, ("attn", lv), 2 * m + e)
            pe.wait_ge(sem("khat_ready"), 2)
            for m in range(2):
                o = open_("khat", m, 4 + m)
                for t in range(NT):
                    last = tr(o[:, t * P:(t + 1) * P], A(l_QK + m * T)[:, t * P:(t + 1) * P])
                close(last, "khat", m)
            for m in range(2):
                emptied(pe, "khat", m)
                o = open_("gla_state", m, 6 + m)
                for t in range(3):
                    for e in range(2):
                        last = mm(o[e * CH:(e + 1) * CH, t * P:(t + 1) * P],
                                  A(l_KT + m * T)[:, t * P + e * CH:t * P + (e + 1) * CH],
                                  A(l_VT, 2048)[:, t * T + (2 * m + e) * P:t * T + (2 * m + e + 1) * P])
                close(last, "gla_state", m)
            pe.wait_ge(sem("gla_states_ready"), 2)
            for hh in range(4):
                emptied(pe, ("attn", 7), hh)
                m, r = hh // 2, slice((hh % 2) * CH, (hh % 2 + 1) * CH)
                o = open_("gla_o", hh, hh)
                for t in range(NT):
                    c = slice(t * P, (t + 1) * P)
                    last = mm(o[:, c], A(l_VT, 2048)[:, t * T + hh * P:t * T + (hh + 1) * P],
                              A(l_AT + hh * T)[:, c], True, t == 0)
                    if t:
                        last = mm(o[:, c], A(l_ST + m * 384)[r, (t - 1) * P:t * P], A(l_E + m * T)[r, c], False, True)
                close(last, "gla_o", hh)

            def row_sums(what, tiles, ready, b):
                o = open_(what, 0, b)
                for i, tile in enumerate(tiles):
                    pe.wait_ge(sem(ready), i + 1)
                    for t in range(NT):
                        last = mm(o[:, i * NT + t:i * NT + t + 1], tile[:, t * P:(t + 1) * P], C("ones", b=1))
                close(last, what)

            def spread(what, i, rs):
                o = open_(what, i, 4 + i % 4)
                for t in range(NT):
                    col = rs[:, i * NT + t:i * NT + t + 1].to_broadcast([P, P])
                    last = mm(o[:, t * P:(t + 1) * P], col, C("ident"))
                close(last, what, i)

            row_sums("sum_gla", sq_gla, "sq_gla", 4)
            row_sums("sum_qk", sq_qk, "sq_qk", 5)
            o = open_("iw", 0, 6)
            for t in range(NT):
                last = tr(o[:, t * P:(t + 1) * P], p2(MISC)[:, t * P:(t + 1) * P])
            close(last, "iw")
            pe.wait_ge(sem("row_rs_ready"), 1)
            for i in range(4):
                spread("gla_rs", i, row_rs[0])
            pe.wait_ge(sem("row_rs_ready"), 2)
            for i in range(8):
                spread("qk_rs", i, row_rs[1])
            def branch(n):
                for k in range(4):
                    pe.wait_ge(sem(f"y{n}_ready"), k + 1)
                for half in range(2):
                    for i in range(4):
                        if i % 2 == 0:
                            w = take(w_br[n])
                        m = 4 * half + i
                        o = open_(("branch", n), m, i)
                        close(tile_of(w, 4, 256, i % 2 * P, ys[n], o, i % 2 == 0), ("branch", n), m)
                    project(("gates", n), 2, w_br[n], in2, 4 * half, 4)

            for t in range(NT):
                o = open_("dsa_vt", t, t)
                for k in range(4):
                    last = tr(o[:, k * P:(k + 1) * P], p2(DV + k)[:, t * P:(t + 1) * P])
                close(last, "dsa_vt", t)
            for t in range(1, NT):
                n = (t + 1) * P
                for hh in range(4):
                    r = slice((hh % 2) * CH, (hh % 2 + 1) * CH)
                    close(mm(open_(("index", t), hh, 4 + hh)[:, 0:n], p2(IQ + hh // 2)[r, t * P:(t + 1) * P],
                             p2(IK)[r, 0:n]), ("index", t), hh)
            branch(0)
            pe.wait_ge(sem("bias_loaded"), 16)
            emptied(pe, "qk_rs", 7)

            def logits(hh, t):
                n = (t + 1) * P
                o = open_(("logits", hh), t, 4 + t % 2)
                mm(o[:, 0:n], p2(DQ + hh)[:, t * P:(t + 1) * P], p2(DK + hh)[:, 0:n], True, False)
                close(mm(o[:, 0:n], C("flip"), A(d_HK + hh * 896 + 384 - t * P, n), False, True), ("logits", hh), t)

            def attend(hh, t):
                i = 4 * hh + t
                pe.wait_ge(sem("probs_ready"), i + 1)
                o = open_("pt", i, 6 + i % 2)
                for j in range(t + 1):
                    last = tr(o[:, j * P:(j + 1) * P], A(d_LG + (i % 2) * T)[:, j * P:(j + 1) * P])
                close(last, "pt", i)

            def values(hh, t):
                i = 4 * hh + t
                emptied(pe, "pt", i)
                if t == 0:
                    open_("dsa_y", hh, hh)
                o = PSB[bank_of("dsa_y", hh)]
                for j in range(t + 1):
                    last = mm(o[:, t * P:(t + 1) * P], A(d_VT, 2048)[:, j * T + hh * P:j * T + (hh + 1) * P],
                              A(d_PT + (i % 2) * T)[:, j * P:(j + 1) * P], j == 0, j == t)
                if t == NT - 1:
                    close(last, "dsa_y", hh)

            pairs = [(hh, t) for hh in range(4) for t in range(NT)]
            logits(*pairs[0])
            for i, (hh, t) in enumerate(pairs):
                if i + 1 < len(pairs):
                    logits(*pairs[i + 1])
                attend(hh, t)
                if i:
                    values(*pairs[i - 1])
            values(*pairs[-1])
            if stop <= 4:
                return
            branch(1)
            branch(2)
            project("mix2", 4, w_br[2], merged2, ready="merged_split")
            sums("sum_2", [A(SQ2 + k * T) for k in range(KT)], "sq_2")
            o = open_("route_t", 0, 5)
            pe.wait_ge(sem("route_split"), 2)
            for k in range(KT):
                c = slice(k * 20, k * 20 + P)
                pe.wait_ge(sem("h2_ready"), k + 1)
                mm(o, route_hi[:, c], in_ff.hi(k), k == 0, False)
                mm(o, route_lo[:, c], in_ff.hi(k), False, False)
                last = mm(o, route_hi[:, c], in_ff.lo(k), False, k == KT - 1)
            close(last, "route_t")
            emptied(pe, "route_t")
            o = open_("route", 0, 6)
            for t in range(NT):
                last = tr(o[:, t * 20:(t + 1) * 20], A(F_CB, T, 0, 20)[:, t * P:(t + 1) * P])
            close(last, "route")
            up("moe", "first", 0)
            pe.wait_ge(sem("combine_ready"), 1)
            o = open_("combine", 0, 6)
            for t in range(NT):
                last = tr(o[0:NE, t * P:(t + 1) * P], rt_c[:, t * NE:(t + 1) * NE])
            close(last, "combine")
            emptied(pe, "combine")
            for e in range(NE):
                close(mm(open_("weights", e, 4 + e % 4), C("sel16", NE, e * P, (e + 1) * P), A(F_CB, T, 0, NE)), "weights", e)
            gated("moe", NE)
            for t in range(NT):
                for i in range(2):
                    o = open_("out", 2 * t + i, 2 * (t % 2) + i)
                    for k in range(4):
                        pe.wait_ge(sem("out_ready"), 4 * i + k + 1)
                        last = tr(o[:, k * P:(k + 1) * P], res[:, 4 * i + k, t * P:(t + 1) * P])
                    close(last, "out", 2 * t + i)


        @block.scalar
        def _(act):
            n_rstd = [0]

            def f(o, i, func, **kw):
                return nc.scalar.activation(o, i, func, **kw)

            def rstd():
                n_rstd[0] += 1
                act.wait_ge(sem("variance_inverted"), n_rstd[0])
                f(v_rs, v_tmp, ACT.Sqrt).then_inc(sem("rstd_ready"), 1)

            n_x, n_hi = [0], [0]

            def squares_of_x(dst, name, term=None):
                for k in range(KT):
                    if term:
                        emptied(act, term, k)
                    else:
                        act.wait_ge(sem("x_updated"), n_x[0] + k + 1)
                    f(dst(k), res[:, k, :], ACT.Square).then_inc(sem(name), 1)
                n_x[0] += 0 if term else KT

            def round_hi(tiles, shift=None):
                for k in range(KT):
                    act.wait_ge(sem("scaled"), n_hi[0] + k + 1)
                    if shift is None:
                        f(tiles.hi(k), tiles.raw(k), ACT.Copy).then_inc(sem("hi_rounded"), 1)
                    else:
                        f(tiles.hi(k), tiles.raw(k), ACT.Identity, bias=shift(k)).then_inc(sem("hi_rounded"), 1)
                n_hi[0] += KT

            def evac(what, k, o, i=None, func=ACT.Copy, **kw):
                filled(act, what, k)
                f(o, PSB[bank_of(what, k)] if i is None else i, func, **kw).then_inc(freed(what, k), 1)

            act.dma_start(fix[:, :], fixed).then_inc(sem("fixed_loaded"), 16)
            act.dma_start(A(XT, 4096).rearrange("p (t c) -> p t c", t=NT),
                          x.rearrange("(t p) c -> p t c", p=P)).then_inc(sem("x_loaded"), 16)
            for k in range(KT):
                evac("x", k, res[:, k, :])
            rstd()
            round_hi(in1)
            f(csil[:, :], S("c", 0, KT), ACT.Silu).then_inc(sem("csil_ready"), 1)
            act.wait_ge(sem("pads_zeroed"), 1)
            for t in range(N_PROJ):
                evac("proj", t, proj(t))
                if 10 <= t < 18:
                    act.wait_ge(sem("conv_ready"), t - 9)
                    f(proj(XS + t - 10), proj(XS + t - 10), ACT.Silu).then_inc(sem("xbc_ready"), 1)
                if t == 18:
                    f(expA[:, :], S("a_log"), ACT.Exp).then_inc(sem("exp_a_ready"), 1)
                    act.wait_ge(sem("dt_abs_ready"), 1)
                    f(ym(4, 0, 8), ym(3, 0, 8), ACT.Exp, scale=-1.0).then_inc(sem("dt_exp_ready"), 1)
                if t == 20:
                    act.wait_ge(sem("to_end_ready"), 1)
                    f(ym(3, 0, 8), ym(3, 0, 8), ACT.Exp).then_inc(sem("to_end_exp_ready"), 1)
            act.wait_ge(sem("mixed"), 2)
            f(A(TW, T, 0, CH), proj(WA, 0, CH), ACT.Tanh).then_inc(sem("tanh_ready"), 1)
            f(proj(GL), proj(GL), ACT.Sigmoid).then_inc(sem("sigmoid_ready"), 1)
            for i in range(2):
                evac("b_tm", i, A(s_BT + i * T))
            evac("chunk_decay", 0, c_last[:, :], PSB[bank_of("chunk_decay")][:, 0:32], ACT.Exp)

            def decay_row(h):
                filled(act, "cs_row", h)
                f(xn[:, h, :], PSB[bank_of("cs_row", h)], ACT.Exp).then_inc(sem("row_decay_ready"), 1)

            for h in range(8):
                decay_row(h)
                emptied(act, "cs_row", h)
                f(A(s_HB + (h % 2) * T), A(s_HB + (h % 2) * T), ACT.Exp).then_inc(sem("pair_decay_ready"), 1)
            for m in range(4):
                f(proj(ZZ + m), proj(ZZ + m), ACT.Silu).then_inc(sem("z_ready"), 1)
            for g in range(2):
                rstd()
            act.wait_ge(sem("ssd_out_ready"), 4)
            act.wait_ge(sem("sigmoid_ready"), 1)
            f(A(SG), proj(GL), ACT.Copy).then_inc(sem("sg_ready"), 1)

            for m in range(4):
                if m:
                    filled(act, ("hh", m - 1), 3)
                evac("w_low", m, ew(e_W), None, ACT.Sigmoid, bias=S("w0", m))
                evac("a_low", m, ew(e_B), None, ACT.Sigmoid, bias=S("a0", m))
                emptied(act, "w_low", m)
                f(ew(e_W), ew(e_W), ACT.Exp, scale=-EXP_HALF).then_inc(sem("w_ready"), 1)
                rstd()
                evac("last_decay", m, pls[:, :], PSB[bank_of("last_decay", m)][0:CH, 0:2 * NC])
                for i, t in enumerate((t_A, t_BP, t_KP, t_V)):
                    evac(("tm", m), i, tm(t), four(PSB[bank_of(("tm", m), i)]))
                for lv in range(1, 6):
                    for e in range(2):
                        evac((f"U{lv}", m), e, h_buf[e][m_U])
                for e in range(2):
                    if e == 0:
                        filled(act, ("ZU5", m), 1)
                        emptied(act, ("tm", m), 0)
                    r = slice(e * CH, (e + 1) * CH)
                    f(four(h_buf[e][m_U])[:, :, 0:CH], tm(t_A)[:, :, r], ACT.Copy)
                for e in range(2):
                    evac(("wv", m), e, four(h_buf[e][m_U])[:, :, CH:P],
                         PSB[bank_of(("wv", m), e)][:, 0:256].rearrange("p (a b) -> p a b", a=4))
                for e in range(2):
                    evac(("aw", m), e, h_buf[e][m_AW])
                for e in range(2):
                    h = 2 * m + e
                    for i in range(2):
                        evac(("hh", m), 2 * e + i, h_all[:, i::2, h, :],
                             PSB[bank_of(("hh", m), 2 * e + i)][0:CH, 0:256].rearrange("p (c i) -> p c i", c=NT))
            for m in range(4):
                if m:
                    emptied(act, "gate", m - 1)
                evac("rwkv_y", m, ew(0))
                rstd()
            if stop <= 2:
                return


            for k in range(KT):
                evac("mix", k, xn[:, k, :])
            rstd()
            squares_of_x(lambda k: A(SQ1 + k * T), "sq_pre_ffn")
            rstd()
            round_hi(in_ff)

            def silu_gates(j, phase, sub, it=None):
                for i in range(4):
                    k = (phase, sub, i)
                    if j != 0:
                        act.wait_ge(sem("ffn_taps_used"), at(j, 4, i - 3))
                    filled(act, "ffn_up", k, it)
                    f(A(F_UB + i * PADW + 3), PSB[i], ACT.Copy).then_inc(freed("ffn_up", k), 1)
                for i in range(2):
                    act.wait_ge(sem("ffn_taps_used"), at(j, 4, i + 1))
                    f(A(F_CB + i * T), A(F_CB + i * T), ACT.Silu).then_inc(sem("ffn_silu_ready"), 1)

            act.wait_ge(sem("ffn_zeroed"), 1)
            silu_gates(0, "first", 0)
            with act.Fori(0, (NF - 1) // 2) as it:
                silu_gates((it, 1), "loop", 1, it)
                silu_gates((it, 2), "loop", 0, it)
            for k in range(KT):
                emptied(act, "ffn_down", ("last", 0, k))
                f(A(F_CMB + k * T), A(F_ACC + k * T), ACT.Square).then_inc(sem("sq_post_ffn"), 1)
            rstd()
            squares_of_x(lambda k: A(F_CMB + k * T), "sq_1")
            rstd()
            emptied(act, "mod")
            round_hi(in2, lambda k: mod[:, k:k + 1])
            if stop <= 3:
                return
            for i in range(2):
                evac("bias_row", i, A(d_BR + i * T, T, 0, 4), PSB[bank_of("bias_row", i)][0:4, :])
            emptied(act, "bias_row", 0)
            emptied(act, "bias_row", 1)
            act.dma_start(skew, A(d_BR, 2 * T, 0, 4)).then_inc(sem("bias_stored"), 16)
            for t in range(8):
                evac("p2", t, p2(t), None, ACT.Gelu_apprx_tanh)
            for t in range(8, 18):
                evac("p2", t, p2(t), None, ACT.Silu if GR <= t < GR + 4 else ACT.Copy)
            rstd()
            for t in range(18, 22):
                evac("p2", t, p2(t), None, ACT.Silu if GR <= t < GR + 4 else ACT.Copy)
            for t in range(NT):
                evac("gmlp_vt", t, A(g_VT + t * T))
            for m in range(2):
                act.wait_ge(sem("forget_abs"), m + 1)
                f(A(l_E + m * T), A(l_E + m * T), ACT.Exp).then_inc(sem("forget_exp"), 1)
            act.wait_ge(sem("bias_stored"), 16)
            for t in range(22, 36):
                evac("p2", t, p2(t))
            filled(act, "gla_vt", 3)
            for t in range(NT):
                evac("gla_vt", t, A(l_VT + t * T))
            for lv in range(1, 8):
                for m in range(2):
                    act.wait_ge(sem("log_decay_ready"), 2 * (lv - 1) + m + 1)
                    f(A(l_E + m * T), A(l_E + m * T), ACT.Exp).then_inc(sem("decay_ready"), 1)
            for m in range(2):
                act.wait_ge(sem("log_decay_ready"), 14 + m + 1)
                f(A(l_QK + m * T), A(l_QK + m * T), ACT.Exp).then_inc(sem("decay_ready"), 1)
                f(A(l_E + m * T), A(l_B + m * T), ACT.Exp).then_inc(sem("decay_ready"), 1)
            for m in range(2):
                evac("khat", m, A(l_KT + m * T))
            for hh in range(4):
                filled(act, "gla_o", hh)
                f(sq_gla[hh], PSB[bank_of("gla_o", hh)], ACT.Square).then_inc(sem("sq_gla"), 1)
                evac("gla_o", hh, p2(GQ + hh))
            for i in range(8):
                f(sq_qk[i], p2(DQ + i), ACT.Square).then_inc(sem("sq_qk"), 1)
            for i in range(2):
                act.wait_ge(sem("row_inverted"), i + 1)
                f(row_rs[i], row_rs[i], ACT.Sqrt).then_inc(sem("row_rs_ready"), 1)
            filled(act, "iw")
            f(iw.rearrange("p (t h) -> p t h", t=NT),
              PSB[bank_of("iw")].rearrange("p (t c) -> p t c", t=NT)[:, :, 32:36], ACT.Copy).then_inc(freed("iw"), 1)
            filled(act, "dsa_vt", 3)
            for t in range(NT):
                evac("dsa_vt", t, A(d_VT + t * T))
            for t in range(1, NT):
                n = (t + 1) * P
                for hh in range(4):
                    i = 4 * (t - 1) + hh
                    if i >= 2:
                        act.wait_ge(sem("relu_used"), i - 1)
                    evac(("index", t), hh, A(d_RL + (i % 2) * T, n), PSB[4 + hh][:, 0:n], ACT.Relu)

            def gates(n):
                for m in range(KT):
                    i = n * KT + m
                    if 4 <= i < KT + 4:
                        emptied(act, ("branch", 0), i - 4)
                    elif i >= 4:
                        act.wait_ge(sem("merged"), i - 4 - KT + 1)
                    evac(("gates", n), m, A(sig[n][i % 4]), None, ACT.Sigmoid, bias=S("b_branch", n * KT + m))

            gates(0)
            hankel = bass.AP(tensor=skew.tensor, offset=skew.offset, ap=[[1, P], [2 * T, 4], [1, 896]])
            act.dma_start(A(d_HK, 4 * 896).rearrange("p (h n) -> p h n", h=4), hankel).then_inc(sem("bias_loaded"), 16)
            for i in range(16):
                t = i % 4
                n = (t + 1) * P
                act.wait_ge(sem("logits_ready"), i + 1)
                p_ = A(d_LG + (i % 2) * T, n)
                f(p_, p_, ACT.Exp, bias=nmax[:, i % 4:i % 4 + 1], accum_out=rsum[:, i % 4:i % 4 + 1])\
                    .then_inc(sem("exp_ready"), 1)
                evac("pt", i, A(d_PT + (i % 2) * T, n), PSB[bank_of("pt", i)][:, 0:n])
                if t == 0 and i:
                    evac("dsa_y", i // 4 - 1, p2(DQ + i // 4 - 1))
            evac("dsa_y", 3, p2(DQ + 3))
            if stop <= 4:
                return
            gates(1)
            gates(2)
            squares_of_x(lambda k: A(SQ2 + k * T), "sq_2", "mix2")
            rstd()
            round_hi(in_ff, lambda k: mod[:, 24 + k:25 + k])
            evac("route_t", 0, A(F_CB, T, 0, 20), PSB[bank_of("route_t")][0:20, :])
            act.wait_ge(sem("route_diff"), 1)
            f(rt_w[0], rt_w[0], ACT.Exp).then_inc(sem("route_exp"), 1)
            act.wait_ge(sem("route_diff"), 2)
            f(rt_s[4], rt_s[4], ACT.Exp).then_inc(sem("route_exp"), 1)
            evac("combine", 0, A(F_CB, T, 0, NE), PSB[bank_of("combine")][0:NE, :])
            for e in range(NE):
                evac("weights", e, A(F_CMB + e * T))

            def silu_experts(j, phase, sub, it=None):
                for i in range(2):
                    k = (phase, sub, i)
                    if j != 0:
                        act.wait_ge(sem("moe_act_ready"), at(j, 2, i - 1))
                    filled(act, "moe_up", k, it)
                    f(A(F_UB + i * T), PSB[i], ACT.Silu).then_inc(freed("moe_up", k), 1)

            silu_experts(0, "first", 0)
            with act.Fori(0, (NE - 1) // 2) as it:
                silu_experts((it, 1), "loop", 1, it)
                silu_experts((it, 2), "loop", 0, it)
            silu_experts(NE - 1, "last", 1)
            for i in range(8):
                evac("out", i, A(OUT + i * T))


        @block.vector
        def _(dve):
            ch = Chain(dve, "vector_step")
            link = ch.link
            V = nc.vector
            n_rstd = [0]

            def tt(o, a, b, op):
                return V.tensor_tensor(o, a, b, op)

            def ts(o, a, s1, s2=None, op0=ALU.mult, op1=None):
                return V.tensor_scalar(o, a, s1, s2, op0) if op1 is None else V.tensor_scalar(o, a, s1, s2, op0, op1)

            def stt(o, a, s1, b, op0, op1):
                return V.scalar_tensor_tensor(o, a, s1, b, op0, op1)

            def rstd(what, scale, add, op1=ALU.add, k=0):
                n_rstd[0] += 1
                filled(dve, what, k)
                V.tensor_scalar(v_tmp, PSB[bank_of(what, k)], scale, add, ALU.mult, op1).then_inc(freed(what, k), 1)
                emptied(dve, what, k)
                V.reciprocal(v_tmp, v_tmp).then_inc(sem("variance_inverted"), 1)
                dve.wait_ge(sem("rstd_ready"), n_rstd[0])

            n_hi = [0]

            def scaled_parts(tiles, gain, ready, shift=None):
                for k in range(KT + 2):
                    if k < KT:
                        stt(tiles.raw(k), res[:, k, :], gain(k), v_rs, ALU.mult, ALU.mult).then_inc(sem("scaled"), 1)
                    if k >= 2:
                        j = k - 2
                        dve.wait_ge(sem("hi_rounded"), n_hi[0] + j + 1)
                        raw, hi = tiles.raw(j), tiles.hi(j).bitcast(F32)
                        if shift is None:
                            tt(tiles.lo(j), raw, hi, ALU.subtract).then_inc(sem(ready), 1)
                        else:
                            stt(tiles.lo(j), raw, shift(j), hi, ALU.add, ALU.subtract).then_inc(sem(ready), 1)
                n_hi[0] += KT

            def split(tiles, k, ready):
                link(V.tensor_copy(tiles.hi(k), tiles.raw(k)))
                tt(tiles.lo(k), tiles.raw(k), tiles.hi(k).bitcast(F32), ALU.subtract).then_inc(sem(ready), 1)

            def log1p(o, u, t1, t2):
                link(ts(t1, u, 2.0, None, ALU.add))
                link(V.reciprocal(t1, t1))
                link(tt(t1, t1, u, ALU.mult))
                link(tt(t2, t1, t1, ALU.mult))
                link(ts(o, t2, 1.0 / (2 * LOG1P_TERMS + 1)))
                for i in range(LOG1P_TERMS - 1, 0, -1):
                    link(stt(o, o, 1.0 / (2 * i + 1), t2, ALU.add, ALU.mult))
                link(stt(o, o, 1.0, t1, ALU.add, ALU.mult))

            for k in range(KT):
                emptied(dve, "x", k)
                tt(A(SQ + k * T), res[:, k, :], res[:, k, :], ALU.mult).then_inc(sem("sq_pre_mix"), 1)
            dve.wait_ge(sem("fixed_loaded"), 16)
            rstd("sum_pre_mix", 1.0 / D, 1e-6)
            scaled_parts(in1, lambda k: S("g_pre_mix", k), "xn_ready")

            for t in range(8):
                emptied(dve, "proj", t)
                buf = A(CONV + (t % 2) * T)
                link(ts(buf, proj(t), S("conv_w", 3 * 8 + t), S("conv_b", t), ALU.mult, ALU.add))
                link(stt(buf, proj(t, shift=1), S("conv_w", 2 * 8 + t), buf, ALU.mult, ALU.add))
                link(stt(buf, proj(t, shift=2), S("conv_w", 1 * 8 + t), buf, ALU.mult, ALU.add))
                link(stt(buf, proj(t, shift=3), S("conv_w", t), buf, ALU.mult, ALU.add))
                V.tensor_copy(proj(t), buf).then_inc(sem("conv_ready"), 1)
            dt, cs, de, t3, t4, t5, t6, t7 = [ym(i, 0, 8) for i in range(8)]
            emptied(dve, "proj", DT)
            link(ts(dt, proj(DT, 0, 8), S("dt_bias", rows=8), None, ALU.add))
            link(ts(t3, dt, -1.0))
            tt(t3, t3, dt, ALU.max).then_inc(sem("dt_abs_ready"), 1)
            for i, t in enumerate([WA, GL] + list(range(RR, RR + 12))):
                emptied(dve, "proj", t)
                buf = A(CONV + 2 * T + (i % 2) * T)
                link(tt(buf, proj(t, shift=1), proj(t), ALU.subtract))
                stt(proj(t), buf, S("mu", i), proj(t), ALU.mult, ALU.add).then_inc(sem("mixed"), 1)
                if i == 5:
                    dve.wait_ge(sem("dt_exp_ready"), 1)
                    log1p(t5, t4, t6, t7)
                    link(ts(dt, dt, 0.0, None, ALU.max))
                    link(stt(dt, t5, 2.0, dt, ALU.mult, ALU.add))
                    link(ts(t6, dt, expA[0:8, :], -1.0, ALU.mult, ALU.mult))
                    link(V.tensor_tensor_scan(cs, C("carry128", 8), t6, 0.0, ALU.mult, ALU.add))
                    last = four(cs)[:, :, P - 1:P].to_broadcast([8, NT, P])
                    tt(four(t3), last, four(cs), ALU.subtract).then_inc(sem("to_end_ready"), 1)
                if i == 8:
                    dve.wait_ge(sem("to_end_exp_ready"), 1)
                    tt(de, t3, dt, ALU.mult).then_inc(sem("dt_ready"), 1)
            filled(dve, "dec3")
            V.tensor_copy(dec3[:, :], PSB[bank_of("dec3")][:, 0:96]).then_inc(freed("dec3"), 1)
            emptied(dve, "dec3")
            d3 = dec3[:, :].rearrange("p (i t h) -> p i t h", i=3, t=NT)

            def per_head(i, t):
                return d3[:, i, t, :].unsqueeze(2).to_broadcast([P, 8, CH])

            for t in range(NT):
                filled(dve, "xs_tm", t)
                src = PSB[bank_of("xs_tm", t)].rearrange("p (h c) -> p h c", h=8)
                tt(A(s_XS2 + t * T).rearrange("p (h c) -> p h c", h=8), src, per_head(2, t), ALU.mult)\
                    .then_inc(sem("xs2_ready"), 1)
                tt(A(s_XD + t * T).rearrange("p (h c) -> p h c", h=8), src, per_head(0, t), ALU.mult)\
                    .then_inc(freed("xs_tm", t), 1)
            for g in range(2):
                filled(dve, "scores", g)
                tt(four(A(s_GT + g * T)), four(PSB[bank_of("scores", g)]), rep4(C("incl128")), ALU.mult)\
                    .then_inc(freed("scores", g), 1)
            emptied(dve, "chunk_decay")
            cl = c_last[:, :].rearrange("p (h t) -> p h t", h=8)
            for t in range(3):
                filled(dve, "state", t)
                o = A(s_SI + t * T)
                if t == 0:
                    V.tensor_copy(o, PSB[bank_of("state", t)]).then_inc(freed("state", t), 1)
                else:
                    v8 = lambda a: a.rearrange("p (h c) -> p h c", h=8)
                    emptied(dve, "state", t - 1)
                    link(tt(v8(o), v8(A(s_SI + (t - 1) * T)), cl[:, :, t:t + 1].to_broadcast([P, 8, CH]), ALU.mult))
                    tt(o, o, PSB[bank_of("state", t)], ALU.add).then_inc(freed("state", t), 1)
            emptied(dve, "state", 2)

            def head_free(h):
                if h % 2 == 0:
                    dve.wait_ge(sem("ssd_head_used"), h // 2 + 1)
                else:
                    filled(dve, "ssd_y", h // 2)

            def log_decays(h):
                dve.wait_ge(sem("row_decay_ready"), h + 1)
                if h >= 2:
                    head_free(h - 2)
                row = PSB[bank_of("cs_row", h)]
                for t in range(NT):
                    c = slice(t * P, (t + 1) * P)
                    last = ts(A(s_HB + (h % 2) * T)[:, c], row[:, c], d3[:, 1, t, h:h + 1], 0.0, ALU.subtract, ALU.min)
                last.then_inc(freed("cs_row", h), 1)

            log_decays(0)
            for h in range(8):
                if h + 1 < 8:
                    log_decays(h + 1)
                dve.wait_ge(sem("pair_decay_ready"), h + 1)
                tt(A(s_CE + (h % 2) * T), proj(CM + h // 4), xn[:, h, :], ALU.mult)
                tt(A(s_HB + (h % 2) * T), A(s_HB + (h % 2) * T), A(s_GT + (h // 4) * T), ALU.mult)\
                    .then_inc(sem("mt_ready"), 1)
            filled(dve, "ssd_y", 3)
            for m in range(4):
                dve.wait_ge(sem("z_ready"), m + 1)
                t = A(s_HB + m * T)
                stt(t, proj(XS + m), S("d_skip", m), PSB[bank_of("ssd_y", m)], ALU.mult, ALU.add)\
                    .then_inc(freed("ssd_y", m), 1)
                emptied(dve, "ssd_y", m)
                link(tt(t, t, proj(ZZ + m), ALU.mult))
                tt(A(s_XD + m * T), t, t, ALU.mult).then_inc(sem("sq_ssd"), 1)
            for g in range(2):
                rstd(f"sum_ssd{g}", 1.0 / 256, 1e-6)
                for i in range(2):
                    m = 2 * g + i
                    stt(ym(m), A(s_HB + m * T), S("ssd_norm", m), v_rs, ALU.mult, ALU.mult)\
                        .then_inc(sem("ssd_out_ready"), 1)

            link(ts(one_ka[:, :], S("k_a", 0, 4), -1.0, 1.0, ALU.mult, ALU.add))
            c8 = lambda a: a.rearrange("p (c t) -> p c t", c=NC)
            for m in range(4):
                kt, rt, vt = proj(KK_ + m), proj(RR + m), proj(VV + m)
                pt = ew(e_P)
                if m:
                    filled(dve, ("hh", m - 1), 3)
                link(ts(ew(e_KK), kt, S("k_k", m)))
                tt(ew(e_BP), ew(e_KK), ew(e_KK), ALU.mult).then_inc(sem("sq_kk"), 1)
                emptied(dve, "a_low", m)
                link(ts(ew(e_KP), ew(e_B), S("k_a", m), one_ka[:, m:m + 1], ALU.mult, ALU.add))
                link(tt(kt, kt, ew(e_KP), ALU.mult))
                dve.wait_ge(sem("w_ready"), m + 1)
                link(tt(ew(e_AT), ew(e_W), C("carry64"), ALU.mult))
                link(tt(ew(e_W), ew(e_W), ew(e_AT), ALU.subtract))
                link(V.tensor_tensor_scan(pt, ew(e_AT), ew(e_W), 0.0, ALU.mult, ALU.add))
                link(V.reciprocal(ew(e_INV), pt))
                rstd(f"sum_kk{m}", 1.0, 1e-24, ALU.max)
                link(tt(ew(e_KK), ew(e_KK), v_rs, ALU.mult))
                stt(ew(e_BP), rt, S("r_k", m), kt, ALU.mult, ALU.mult).then_inc(sem("bonus_in"), 1)
                link(stt(ew(e_AT)[:, 1:T], ew(e_KK)[:, 1:T], -1.0, pt[:, 0:T - 1], ALU.mult, ALU.mult))
                link(ts(ew(e_AT)[:, 0:T:CH], ew(e_KK)[:, 0:T:CH], -1.0))
                link(tt(ew(e_B), ew(e_B), ew(e_KK), ALU.mult))
                link(tt(ew(e_BH), ew(e_B), ew(e_INV), ALU.mult))
                link(tt(ew(e_KH), kt, ew(e_INV), ALU.mult))
                link(tt(rt, rt, pt, ALU.mult))
                filled(dve, f"sum_bonus{m}")
                tt(ym(4 + m), vt, PSB[bank_of(f"sum_bonus{m}")], ALU.mult).then_inc(freed(f"sum_bonus{m}"), 1)
                last = pt[:, CH - 1::CH].unsqueeze(2).to_broadcast([P, NC, CH])
                link(tt(c8(ew(e_BP)), c8(ew(e_BH)), last, ALU.mult))
                tt(c8(ew(e_KP)), c8(ew(e_KH)), last, ALU.mult).then_inc(sem("pair_ready"), 1)
                for e in range(2):
                    hb = h_buf[e]
                    filled(dve, ("abT", m), e)
                    if e == 0:
                        filled(dve, ("tm", m), 3)
                    tt(four(hb[m_AT]), four(PSB[bank_of(("abT", m), e)]), rep4(C("strict64")), ALU.mult)\
                        .then_inc(freed(("abT", m), e), 1)
                    emptied(dve, ("abT", m), e)
                    link(tt(four(hb[m_Z]), four(hb[m_AT]), rep4(C("level0")), ALU.mult))
                    link(tt(four(hb[m_Z]), four(hb[m_Z]), rep4(C("ident")), ALU.add))
                    filled(dve, ("ab", m), e)
                    tt(four(hb[m_X]), four(PSB[bank_of(("ab", m), e)]), rep4(C("level0t")), ALU.mult)\
                        .then_inc(freed(("ab", m), e), 1)
                    emptied(dve, ("ab", m), e)
                    link(tt(four(hb[m_X]), four(hb[m_X]), rep4(C("ident")), ALU.add))
                    tt(four(hb[m_LV]), four(hb[m_AT]), rep4(C("level1")), ALU.mult).then_inc(sem(f"level{e}_ready"), 1)
                for lv in range(1, 6):
                    for e in range(2):
                        hb = h_buf[e]
                        filled(dve, (f"ZU{lv}", m), e)
                        if lv < 5:
                            filled(dve, (f"XU{lv}", m), e)
                        tt(hb[m_Z], hb[m_Z], PSB[bank_of((f"ZU{lv}", m), e)], ALU.add).then_inc(freed((f"ZU{lv}", m), e), 1)
                        if lv < 5:
                            tt(hb[m_X], hb[m_X], PSB[bank_of((f"XU{lv}", m), e)], ALU.add)\
                                .then_inc(freed((f"XU{lv}", m), e), 1)
                            tt(four(hb[m_LV]), four(hb[m_AT]), rep4(C(f"level{lv + 1}")), ALU.mult)\
                                .then_inc(sem(f"level{e}_ready"), 1)
                for e in range(2):
                    hb = h_buf[e]
                    for what, dst, mask in (("akT", m_X, "strict64"), ("rbT", m_AT, "incl64"), ("rkT", m_LV, "incl64")):
                        filled(dve, (what, m), e)
                        tt(four(hb[dst]), four(PSB[bank_of((what, m), e)]), rep4(C(mask)), ALU.mult)\
                            .then_inc(freed((what, m), e), 1)
                filled(dve, ("ry", m), 1)
                for e in range(2):
                    V.tensor_copy(proj((RR, KK_)[e] + m), PSB[bank_of(("ry", m), e)]).then_inc(freed(("ry", m), e), 1)
                for e in range(2):
                    h = 2 * m + e
                    emptied(dve, "last_decay", m)
                    o = gt_all[:, :, h, :]
                    link(tt(o, C("ident", CH, 0, CH).unsqueeze(1).to_broadcast([CH, NC, CH]),
                            pls[:, e * NC:(e + 1) * NC].unsqueeze(2).to_broadcast([CH, NC, CH]), ALU.mult))
                    for i in range(2):
                        filled(dve, ("gt", m), 2 * e + i)
                        tt(o[:, i::2, :], o[:, i::2, :],
                           PSB[bank_of(("gt", m), 2 * e + i)][0:CH, 0:256].rearrange("p (c i) -> p c i", c=NT), ALU.add)\
                            .then_inc(freed(("gt", m), 2 * e + i), 1)
            for i in range(4):
                emptied(dve, ("hh", 3), i)
            for k in range(4):
                split(y1, k, "y_ready")
            for cn in range(1, NC - 1):
                filled(dve, ("s", cn))
                o = h_all[:, cn, :, :]
                tt(o, o, PSB[bank_of(("s", cn))][0:CH, :].rearrange("p (h i) -> p h i", h=8), ALU.add)\
                    .then_inc(freed(("s", cn)), 1)
            filled(dve, "mod")
            tt(mod[:, :], PSB[7][:, 0:48], S("b_mod", 0, 48), ALU.add).then_inc(freed("mod"), 1)
            for m in range(4):
                emptied(dve, "rwkv_y", m)
                y = ew(0)
                filled(dve, f"sum_y{m}")
                stt(y, PSB[bank_of(f"sum_y{m}")], -1.0 / CH, y, ALU.mult, ALU.add).then_inc(freed(f"sum_y{m}"), 1)
                emptied(dve, f"sum_y{m}")
                tt(ew(2), y, y, ALU.mult).then_inc(sem("sq_y"), 1)
                rstd(f"sum_y2{m}", 1.0 / CH, 64e-5)
                link(tt(y, y, v_rs, ALU.mult))
                link(ts(y, y, S("ln_w", m), S("ln_b", m), ALU.mult, ALU.add))
                emptied(dve, f"sum_bonus{m}")
                link(tt(y, y, ym(4 + m), ALU.add))
                filled(dve, "gate", m)
                tt(ym(4 + m), y, PSB[bank_of("gate", m)], ALU.mult).then_inc(freed("gate", m), 1)
                emptied(dve, "gate", m)
                split(y1, 4 + m, "y_ready")
            if stop <= 2:
                return

            x_ = lambda k: res[:, k, :]
            n_ = lambda k: xn[:, k, :]
            sq = lambda k: A(SQ1 + k * T)

            n_add = [0]

            def add_normed(src, gain):
                for k in range(KT + 1):
                    if k < KT:
                        stt(src(k), src(k), S(gain, k), v_rs, ALU.mult, ALU.mult).then_inc(sem("term_ready"), 1)
                    if k:
                        dve.wait_ge(sem("term_ready"), n_add[0] + k)
                        tt(x_(k - 1), x_(k - 1), src(k - 1), ALU.add).then_inc(sem("x_updated"), 1)
                n_add[0] += KT

            for k in range(KT):
                emptied(dve, "mix", k)
                tt(sq(k), n_(k), n_(k), ALU.mult).then_inc(sem("sq_post_mix"), 1)
            rstd("sum_post_mix", 1.0 / D, 1e-6)
            add_normed(n_, "g_post_mix")
            V.memset(A(F_UB, 4 * PADW).rearrange("p (t c) -> p t c", t=4)[:, :, 0:3], 0.0).then_inc(sem("ffn_zeroed"), 1)
            link(V.memset(A(F_ACC, 4096), 0.0))
            rstd("sum_pre_ffn", 1.0 / D, 1e-6)
            scaled_parts(in_ff, lambda k: S("g_pre_ffn", k), "ffn_in_ready")

            def conv_gate(j, phase, sub, it=None):
                fc0 = at(j, 16, S0 + SMALL["ffn_conv"][0])

                def tap(i, k):
                    return fix[:, bass.ds(fc0 + (4 * i + k), 1)] if it is not None else \
                        fix[:, fc0 + 4 * i + k:fc0 + 4 * i + k + 1]

                if j != 0:
                    dve.wait_ge(sem("ffn_act_ready"), at(j, 2, 0))
                for i in range(4):
                    emptied(dve, "ffn_up", (phase, sub, i), it)
                    u, c = lambda s_: A(F_UB + i * PADW + 3 - s_), A(F_CB + i * T)
                    link(ts(c, u(0), tap(i, 2), tap(i, 3), ALU.mult, ALU.add))
                    link(stt(c, u(1), tap(i, 1), c, ALU.mult, ALU.add))
                    stt(c, u(2), tap(i, 0), c, ALU.mult, ALU.add).then_inc(sem("ffn_taps_used"), 1)

            def finish_gate(j, sub):
                for i in range(2):
                    dve.wait_ge(sem("ffn_silu_ready"), at(j, 2, i + 1))
                    if i == 0:
                        dve.wait_ge(sem("ffn_taps_used"), at(j, 4, 4))
                    link(tt(acts.raw(2 * sub + i), A(F_CB + i * T), A(F_CB + (2 + i) * T), ALU.mult))
                    split(acts, 2 * sub + i, "ffn_act_ready")

            def accumulate(kind, phase, sub, it=None):
                for m in range(KT):
                    k = (phase, sub, m)
                    filled(dve, kind + "_down", k, it)
                    o = A(F_ACC + m * T)
                    tt(o, o, PSB[4 + m % 4], ALU.add).then_inc(freed(kind + "_down", k), 1)

            conv_gate(0, "first", 0)
            finish_gate(0, 0)
            times = (NF - 1) // 2
            with dve.Fori(0, times) as it:
                ch.enter(it, 24)
                conv_gate((it, 1), "loop", 1, it)
                accumulate("ffn", "loop", 0, it)
                finish_gate((it, 1), 1)
                conv_gate((it, 2), "loop", 0, it)
                accumulate("ffn", "loop", 1, it)
                finish_gate((it, 2), 0)
            ch.leave(times)
            accumulate("ffn", "last", 0)
            emptied(dve, "ffn_down", ("last", 0, 6))
            emptied(dve, "ffn_down", ("last", 0, 7))
            acc = lambda k: A(F_ACC + k * T)
            rstd("sum_post_ffn", 1.0 / D, 1e-6)
            add_normed(acc, "g_post_ffn")

            def modulated(tiles, scale_at, shift_at, gain, name):
                link(stt(gmod[:, :], mod[:, scale_at:scale_at + KT], 1.0, S(gain, 0, KT), ALU.add, ALU.mult))
                scaled_parts(tiles, lambda k: gmod[:, k:k + 1], name, lambda k: mod[:, shift_at + k:shift_at + k + 1])

            rstd("sum_1", 1.0 / D, 1e-6)
            modulated(in2, 8, 0, "g1", "h_ready")
            if stop <= 3:
                return
            filled(dve, "w_s")
            tt(four(A(g_WS)), four(PSB[bank_of("w_s")]), rep4(C("incl128")), ALU.mult).then_inc(freed("w_s"), 1)
            filled(dve, "gmlp_mean")
            for k in range(4):
                v = p2(AV + k)
                last = stt(v, PSB[bank_of("gmlp_mean")], -1.0 / T, v, ALU.mult, ALU.add)
                if k == 3:
                    last.then_inc(freed("gmlp_mean"), 1)
            emptied(dve, "gmlp_mean")
            for k in range(4):
                tt(A(g_SQ + k * T), p2(AV + k), p2(AV + k), ALU.mult).then_inc(sem("sq_gmlp"), 1)
            rstd("gmlp_var", 1.0 / T, 1e-6)
            for k in range(4):
                v = p2(AV + k)
                link(stt(v, v, S("gmlp_g", k), v_rs, ALU.mult, ALU.mult))
                ts(v, v, S("gmlp_b", k), None, ALU.add).then_inc(sem("gmlp_v_ready"), 1)
            for g in range(4):
                filled(dve, "mixed", g)
                tt(p2(AU + g), p2(AU + g), PSB[bank_of("mixed", g)], ALU.mult).then_inc(freed("mixed", g), 1)
                emptied(dve, "mixed", g)
                split(ys[0], g, "y0_ready")
            bt, et, qk = [[A(o + m * T) for m in range(2)] for o in (l_B, l_E, l_QK)]
            for m in range(2):
                filled(dve, "forget", m)
                ts(bt[m], PSB[bank_of("forget", m)], S("b_gate", m), None, ALU.add).then_inc(freed("forget", m), 1)
                emptied(dve, "forget", m)
                link(ts(et[m], bt[m], -1.0))
                tt(et[m], et[m], bt[m], ALU.min).then_inc(sem("forget_abs"), 1)
            for m in range(2):
                dve.wait_ge(sem("forget_exp"), m + 1)
                log1p(qk[0], et[m], qk[1], v_tmp)
                link(ts(bt[m], bt[m], -1.0, 0.0, ALU.mult, ALU.max))
                link(stt(bt[m], qk[0], 2.0, bt[m], ALU.mult, ALU.add))
                link(ts(et[m], bt[m], -1.0 / 16))
                link(V.tensor_tensor_scan(bt[m], C("carry128"), et[m], 0.0, ALU.mult, ALU.add))
            for m in range(2):
                emptied(dve, "p2", GQ + m)
                ts(p2(GQ + m), p2(GQ + m), 0.125).then_inc(sem("level_ready"), 1)
            dve.wait_ge(sem("level_ready"), 2)

            def merge_level(lv):
                mask = C("ident" if lv == 0 else f"level{lv - 1}").bitcast(mybir.dt.int32)
                for hh in range(4):
                    filled(dve, ("attn", lv), hh)
                    V.copy_predicated(four(A(l_AT + hh * T)), rep4(mask), four(PSB[bank_of(("attn", lv), hh)]))\
                        .then_inc(freed(("attn", lv), hh), 1)

            def level_logs(lv):
                hw = 1 << (lv - 1)
                v4 = lambda a: a.rearrange("p (b u h) -> p b u h", u=2, h=hw)
                for m in range(2):
                    b, e = v4(bt[m]), v4(et[m])
                    mid = b[:, :, 0, hw - 1:hw].to_broadcast([P, T // (2 * hw), hw])
                    link(tt(e[:, :, 1, :], b[:, :, 1, :], mid, ALU.subtract))
                    tt(e[:, :, 0, :], mid, b[:, :, 0, :], ALU.subtract).then_inc(sem("log_decay_ready"), 1)

            for lv in range(1, 8):
                hw = 1 << (lv - 1)
                v4 = lambda a: a.rearrange("p (b u h) -> p b u h", u=2, h=hw)
                level_logs(lv)
                if lv == 1:
                    filled(dve, ("attn", 0), 0)
                    link(V.memset(A(l_AT, 2048), 0.0))
                merge_level(lv - 1)
                for m in range(2):
                    dve.wait_ge(sem("decay_ready"), 2 * (lv - 1) + m + 1)
                    emptied(dve, "p2", GK + m)
                    e, q_, k_, o = v4(et[m]), v4(p2(GQ + m)), v4(p2(GK + m)), v4(qk[m])
                    link(tt(o[:, :, 1, :], e[:, :, 1, :], q_[:, :, 1, :], ALU.mult))
                    tt(o[:, :, 0, :], e[:, :, 0, :], k_[:, :, 0, :], ALU.mult).then_inc(sem("level_ready"), 1)
            merge_level(7)
            c4 = lambda a: a.rearrange("p (c t) -> p c t", c=NT)
            for m in range(2):
                last = c4(bt[m])[:, :, P - 1:P].to_broadcast([P, NT, P])
                tt(c4(qk[m]), last, c4(bt[m]), ALU.subtract).then_inc(sem("log_decay_ready"), 1)
            for m in range(2):
                dve.wait_ge(sem("decay_ready"), 14 + 2 * m + 2)
                tt(qk[m], qk[m], p2(GK + m), ALU.mult).then_inc(sem("khat_ready"), 1)
            for m in range(2):
                st = A(l_ST + m * 384, 384)
                filled(dve, "gla_state", m)
                pst = PSB[bank_of("gla_state", m)]
                link(V.tensor_copy(st[:, 0:P], pst[:, 0:P]))
                for t in range(1, 3):
                    last = stt(st[:, t * P:(t + 1) * P], st[:, (t - 1) * P:t * P], et[m][:, t * P + P - 1:t * P + P],
                               pst[:, t * P:(t + 1) * P], ALU.mult, ALU.add)
                    if t == 1:
                        link(last)
                    else:
                        last.then_inc(freed("gla_state", m), 1)
                        emptied(dve, "gla_state", m)
                tt(et[m], et[m], p2(GQ + m), ALU.mult).then_inc(sem("gla_states_ready"), 1)
            for i, what in enumerate(("sum_gla", "sum_qk")):
                filled(dve, what)
                n = (4, 8)[i] * NT
                ts(row_rs[i], PSB[bank_of(what)][:, 0:n], 1.0 / P, 1e-6, ALU.mult, ALU.add).then_inc(freed(what), 1)
                emptied(dve, what)
                V.reciprocal(row_rs[i], row_rs[i]).then_inc(sem("row_inverted"), 1)
            for hh in range(4):
                filled(dve, "gla_rs", hh)
                emptied(dve, "gla_o", hh)
                o = p2(GQ + hh)
                stt(o, o, S("gla_g"), PSB[bank_of("gla_rs", hh)], ALU.mult, ALU.mult)\
                    .then_inc(freed("gla_rs", hh), 1)
                emptied(dve, "gla_rs", hh)
                tt(p2(GR + hh), o, p2(GR + hh), ALU.mult).then_inc(sem("gla_out_ready"), 1)
            link(ts(qg[:, :], S("q_g"), float(P) ** -0.5))
            for i in range(8):
                t = p2(DQ + i)
                filled(dve, "qk_rs", i)
                stt(t, t, qg[:, :] if i < 4 else S("k_g"), PSB[bank_of("qk_rs", i)], ALU.mult, ALU.mult)\
                    .then_inc(freed("qk_rs", i), 1)

            def gate_branch(n, m):
                i = n * KT + m
                g = A(sig[n][i % 4])
                emptied(dve, ("gates", n), m)
                filled(dve, ("branch", n), m)
                up_ = PSB[bank_of(("branch", n), m)]
                o = A(MG + m * T)
                if n == 0:
                    tt(o, g, up_, ALU.mult).then_inc(freed(("branch", n), m), 1)
                else:
                    tt(g, g, up_, ALU.mult).then_inc(freed(("branch", n), m), 1)
                    emptied(dve, ("branch", n), m)
                    tt(o, o, g, ALU.add).then_inc(sem("merged"), 1)
                    if n == 2:
                        dve.wait_ge(sem("merged"), KT + m + 1)
                        split(merged2, m, "merged_split")

            ma = [A(d_MA + P * (t * (t + 1) // 2), (t + 1) * P) for t in range(NT)]
            sc = [None] + [A(d_SC + (0, 256, 640)[t - 1], (t + 1) * P) for t in range(1, NT)]
            link(V.tensor_copy(ma[0], C("neg128")))
            emptied(dve, "iw")
            for t in range(1, NT):
                n = (t + 1) * P
                for hh in range(4):
                    i = 4 * (t - 1) + hh
                    emptied(dve, ("index", t), hh)
                    r_, w_ = A(d_RL + (i % 2) * T, n), iw[:, t * 4 + hh:t * 4 + hh + 1]
                    if hh == 0:
                        ts(sc[t], r_, w_).then_inc(sem("relu_used"), 1)
                    else:
                        stt(sc[t], r_, w_, sc[t], ALU.mult, ALU.add).then_inc(sem("relu_used"), 1)
                    dve.wait_ge(sem("relu_used"), i + 1)
                link(tt(sc[t][:, t * P:n], sc[t][:, t * P:n], C("neg128"), ALU.add))
            topk = sem("topk_step")
            for r in range(16):
                for t in range(1, NT):
                    if r:
                        dve.wait_ge(topk, 6 * r - 3 + t)
                    V.max(top8[:, 8 * t - 8:8 * t], sc[t]).then_inc(topk, 1)
                for t in range(1, NT):
                    dve.wait_ge(topk, 6 * r + t)
                    V.match_replace(sc[t], top8[:, 8 * t - 8:8 * t], sc[t], -3e38).then_inc(topk, 1)
                if r in GATE_ROUNDS:
                    gate_branch(0, GATE_ROUNDS.index(r))
            for t in range(1, NT):
                dve.wait_ge(topk, 6 * 15 + 3 + t)
                link(ts(ma[t], sc[t], -3e38, -1e30, ALU.is_gt, ALU.mult))

            def masked(i):
                hh, t = i // 4, i % 4
                n = (t + 1) * P
                lg = A(d_LG + (i % 2) * T, n)
                filled(dve, ("logits", hh), t)
                if i >= 2:
                    filled(dve, "pt", i - 2)
                tt(lg, PSB[bank_of(("logits", hh), t)][:, 0:n], ma[t], ALU.add).then_inc(freed(("logits", hh), t), 1)
                emptied(dve, ("logits", hh), t)
                V.tensor_reduce(nmax[:, i % 4:i % 4 + 1], lg, AX.X, ALU.max, negate=True).then_inc(sem("logits_ready"), 1)

            masked(0)
            for i in range(16):
                t = i % 4
                if i + 1 < 16:
                    masked(i + 1)
                dve.wait_ge(sem("exp_ready"), i + 1)
                lg = A(d_LG + (i % 2) * T, (t + 1) * P)
                link(V.reciprocal(rinv[:, t:t + 1], rsum[:, t:t + 1]))
                ts(lg, lg, rinv[:, t:t + 1]).then_inc(sem("probs_ready"), 1)
                if 2 <= i < 6:
                    filled(dve, ("branch", 0), KT - 1)
                    dve.wait_ge(sem("gla_out_ready"), i - 1)
                    split(ys[1], i - 2, "y1_ready")
                elif i in (10, 14):
                    emptied(dve, "dsa_y", i // 4 - 2)
                    split(ys[2], i // 4 - 2, "y2_ready")
            if stop <= 4:
                return
            emptied(dve, "dsa_y", 2)
            split(ys[2], 2, "y2_ready")
            emptied(dve, "dsa_y", 3)
            split(ys[2], 3, "y2_ready")
            for n in (1, 2):
                for m in range(KT):
                    gate_branch(n, m)
            for m in range(KT):
                filled(dve, "mix2", m)
                stt(x_(m), PSB[bank_of("mix2", m)], mod[:, 16 + m:17 + m], x_(m), ALU.mult, ALU.add)\
                    .then_inc(freed("mix2", m), 1)
            rstd("sum_2", 1.0 / D, 1e-6)
            modulated(in_ff, 32, 24, "g2", "h2_ready")

            filled(dve, "route")
            lg = rt_l.rearrange("p (t c) -> p t c", t=NT)
            tt(lg, PSB[bank_of("route")][:, 0:80].rearrange("p (t c) -> p t c", t=NT), rep4(S("b_route", 0, 20)), ALU.add)\
                .then_inc(freed("route"), 1)
            emptied(dve, "route")
            ex, oh, sel, h1, h2 = [w.rearrange("p (t c) -> p t c", t=NT) for w in rt_w]
            mx, pg, none, v1, ev, w1, w2_, tmp, v2 = rt_s
            each = lambda a: a.unsqueeze(2).to_broadcast([P, NT, 4])

            def first_of(hot, vals, top):
                link(tt(hot, vals, each(top), ALU.is_equal))
                link(ts(none, hot[:, :, 0], -1.0, 1.0, ALU.mult, ALU.add))
                for c in range(1, 4):
                    link(tt(hot[:, :, c], hot[:, :, c], none, ALU.mult))
                    link(tt(none, none, hot[:, :, c], ALU.subtract))

            link(V.tensor_reduce(mx, lg[:, :, 0:4], AX.X, ALU.max))
            tt(ex, lg[:, :, 0:4], each(mx), ALU.subtract).then_inc(sem("route_diff"), 1)
            first_of(oh, lg[:, :, 0:4], mx)
            for g in range(4):
                part = lg[:, :, 4 + 4 * g:8 + 4 * g]
                hot = oh[:, :, g:g + 1].to_broadcast([P, NT, 4])
                if g == 0:
                    link(tt(sel, part, hot, ALU.mult))
                else:
                    link(tt(h1, part, hot, ALU.mult))
                    link(tt(sel, sel, h1, ALU.add))
            link(V.tensor_reduce(v1, sel, AX.X, ALU.max))
            first_of(h1, sel, v1)
            link(stt(sel, h1, -3e38, sel, ALU.mult, ALU.add))
            link(V.tensor_reduce(v2, sel, AX.X, ALU.max))
            first_of(h2, sel, v2)
            tt(ev, v2, v1, ALU.subtract).then_inc(sem("route_diff"), 1)
            dve.wait_ge(sem("route_exp"), 1)
            link(V.tensor_reduce(pg, ex, AX.X, ALU.add))
            dve.wait_ge(sem("route_exp"), 2)
            link(ts(w1, ev, 1.0, None, ALU.add))
            link(tt(w1, w1, pg, ALU.mult))
            link(V.reciprocal(w1, w1))
            link(tt(w2_, w1, ev, ALU.mult))
            link(tt(h1, h1, each(w1), ALU.mult))
            link(tt(h2, h2, each(w2_), ALU.mult))
            link(tt(h1, h1, h2, ALU.add))
            cm = rt_c.rearrange("p (t g c) -> p t g c", t=NT, g=4)
            for g in range(4):
                last = tt(cm[:, :, g, :], h1, oh[:, :, g:g + 1].to_broadcast([P, NT, 4]), ALU.mult)
            last.then_inc(sem("combine_ready"), 1)
            link(V.memset(A(F_ACC, 4096), 0.0))

            def expert_gate(j, phase, sub, it=None):
                off = at(j, T, F_CMB)
                cw = arena[:, bass.ds(off, T)] if it is not None else A(off)
                for i in range(2):
                    g = A(F_UB + i * T)
                    emptied(dve, "moe_up", (phase, sub, i), it)
                    filled(dve, "moe_up", (phase, sub, 2 + i), it)
                    if j == 0 and i == 0:
                        for e in range(NE - 4, NE):
                            emptied(dve, "weights", e)
                    tt(g, g, PSB[2 + i], ALU.mult).then_inc(freed("moe_up", (phase, sub, 2 + i)), 1)
                    emptied(dve, "moe_up", (phase, sub, 2 + i), it)
                    link(tt(acts.raw(2 * sub + i), g, cw, ALU.mult))
                    split(acts, 2 * sub + i, "moe_act_ready")

            expert_gate(0, "first", 0)
            with dve.Fori(0, (NE - 1) // 2) as it:
                ch.enter(it, 8)
                expert_gate((it, 1), "loop", 1, it)
                accumulate("moe", "loop", 0, it)
                expert_gate((it, 2), "loop", 0, it)
                accumulate("moe", "loop", 1, it)
            ch.leave((NE - 1) // 2)
            expert_gate(NE - 1, "last", 1)
            accumulate("moe", "last", 0)
            accumulate("moe", "last", 1)
            for m in range(4, 8):
                emptied(dve, "moe_down", ("last", 1, m))
            for k in range(KT):
                stt(x_(k), acc(k), mod[:, 40 + k:41 + k], x_(k), ALU.mult, ALU.add).then_inc(sem("out_ready"), 1)


        @block.gpsimd
        def _(pool):
            ch = Chain(pool, "pool_step")
            unit, chunk = [0], [0]

            def unit_loaded(u, it=None, per=0):
                v = 16 * (u // RING + 1)
                pool.wait_ge(sem(f"weights{u % RING}_loaded"), v if it is None else it * (16 * per // RING) + v)

            def unit_begun(u, it=None, per=0):
                pool.wait_ge(sem("weights_used"), u + 1 if it is None else it * per + (u + 1))

            def split_unit(weights, i, it=None):
                u, q = unit[0] + i, chunk[0] + 2 * i
                unit_loaded(u, it, 2)
                for c in range(2):
                    if i:
                        pool.wait_ge(sem("split_used"), q + c if it is None else it * 4 + (q + c))
                    raw = ring[:, u % RING, c * CHUNK:(c + 1) * CHUNK]
                    hi, lo = weights.slot(q + c)
                    if it is not None:
                        pool.sem_inc(sem("chunk_waited"), 1)
                    first = nc.gpsimd.tensor_scalar(hi, raw, 1.0, 1.0, ALU.mult, ALU.mult)
                    if c == 0:
                        first.then_inc(sem("weights_used"), 1)
                        unit_begun(u, it, 2)
                    else:
                        ch.link(first)
                    nc.gpsimd.tensor_tensor(lo, raw, hi.bitcast(F32), ALU.subtract).then_inc(sem("split_ready"), 1)

            def split_units(weights, n):
                split_unit(weights, 0)
                times = (n - 1) // 2
                with pool.Fori(0, times) as it:
                    ch.enter(it, 2)
                    split_unit(weights, 1, it)
                    split_unit(weights, 2, it)
                ch.leave(times)
                if n % 2 == 0:
                    split_unit(weights, n - 1)
                unit[0] += n
                chunk[0] += 2 * n

            def multiply_mod(it=None):
                for i in range(MOD_BATCH):
                    u = unit[0] + i
                    unit_loaded(u, it, MOD_BATCH)
                    w = ring[:, u % RING, :].rearrange("p (k c) -> p k c", k=KT)
                    nc.gpsimd.tensor_tensor(w, w, csil[:, :].unsqueeze(2).to_broadcast([P, KT, 256]), ALU.mult)\
                        .then_inc(sem("weights_used"), 1)
                    unit_begun(u, it, MOD_BATCH)
                    ch.link(nc.gpsimd.tensor_tensor(w[:, 0:4], w[:, 0:4], w[:, 4:8], ALU.add))
                    ch.link(nc.gpsimd.tensor_tensor(w[:, 0:2], w[:, 0:2], w[:, 2:4], ALU.add))
                    nc.gpsimd.tensor_tensor(mod_part(i), w[:, 0], w[:, 1], ALU.add).then_inc(sem("mod_part_ready"), 1)

            pv = A(PROJ, N_PROJ * PADW).rearrange("p (t c) -> p t c", c=PADW)
            emptied(pool, "x", KT - 1)
            nc.gpsimd.memset(pv[:, :, 0:3], 0.0).then_inc(sem("pads_zeroed"), 1)
            split_units(w_in1, 14)

            pool.wait_ge(sem("csil_ready"), 1)
            pool.wait_ge(sem("ssd_out_ready"), 4)
            pool.wait_ge(sem("sg_ready"), 1)
            with pool.Fori(0, 3) as b:
                ch.enter(b, 2 * MOD_BATCH)
                multiply_mod(b)
                pool.wait_ge(sem("mod_parts_used"), b + 1)
            ch.leave(3)
            unit[0] += 3 * MOD_BATCH
            multiply_mod()
            unit[0] += MOD_BATCH

            filled(pool, ("hh", 3), 3)
            split_units(w_out1, 4)
            filled(pool, "mix", KT - 1)
            split_units(w_ff, 3 * NF)
            if stop <= 3:
                return
            filled(pool, "ffn_down", ("last", 0, KT - 1))
            split_units(w_in2, 18)
            pool.wait_ge(sem("gla_out_ready"), 4)
            split_units(w_br[0], 6)
            filled(pool, "dsa_y", 3)
            split_units(w_br[1], 12 + 4)
            filled(pool, "mix2", KT - 1)
            nc.gpsimd.tensor_scalar(route_hi[:, :], M("w_route"), 1.0, 1.0, ALU.mult, ALU.mult)\
                .then_inc(sem("route_split"), 1)
            pool.wait_ge(sem("route_split"), 1)
            nc.gpsimd.tensor_tensor(route_lo[:, :], M("w_route"), route_hi[:, :].bitcast(F32), ALU.subtract)\
                .then_inc(sem("route_split"), 1)
            split_units(w_ff, 3 * NE)

        @block.sync
        def _(sp):
            n_units = units.shape[0]
            for u in range(RING):
                sp.dma_start(ring[:, u, :], units[u, :, :]).then_inc(sem(f"weights{u}_loaded"), 16)
            whole = n_units // RING - 1
            with sp.Fori(0, whole) as i:
                for j in range(RING):
                    sp.wait_ge(sem("weights_used"), RING * i + j + 2)
                    sp.dma_start(ring[:, j, :], units[bass.ds(RING * i + RING + j, 1), :, :].rearrange("a p n -> (a p) n"))\
                        .then_inc(sem(f"weights{j}_loaded"), 16)
            for u in range(RING * (whole + 1), n_units):
                sp.wait_ge(sem("weights_used"), u - RING + 2)
                sp.dma_start(ring[:, u % RING, :], units[u, :, :]).then_inc(sem(f"weights{u % RING}_loaded"), 16)
            if stop <= 4:
                return
            for i in range(8):
                emptied(sp, "out", i)
                sp.dma_start(out[(i // 2) * P:(i // 2 + 1) * P, (i % 2) * T:(i % 2 + 1) * T], A(OUT + i * T))\
                    .then_inc(sem("out_stored"), 16)
            sp.wait_ge(sem("out_stored"), 8 * 16)


def _columns(v):
    v = np.asarray(v).reshape(-1)
    pad = -len(v) % P
    return np.pad(v, (0, pad)).reshape(-1, P).T


def _units_1024(w):
    return w.reshape(KT, P, -1, 2, P).transpose(2, 1, 3, 0, 4).reshape(-1, P, UNIT)


def _units_down(w):
    return w.reshape(-1, 2, P, 2, T).transpose(0, 2, 3, 1, 4).reshape(-1, P, UNIT)


def _rwkv_tiles(a):
    r, w, k, v, lo, g = np.split(a, np.cumsum([512, 64, 512, 512, 64]), axis=-1)
    return np.concatenate([w, lo, g, r, k, v], axis=-1)


def _constants():
    f = np.float32
    s, t = np.arange(P)[:, None], np.arange(P)[None, :]
    out = {"ident": s == t, "ones": np.ones((P, P)), "blk64": s // CH == t // CH, "flip": s + t == P - 1,
           "strict64": (s < t) & (s // CH == t // CH), "incl64": (s <= t) & (s // CH == t // CH),
           "incl128": s <= t, "neg128": np.where(s >= t, 0.0, -1e30)}
    for k in range(7):
        h = 1 << k
        out[f"level{k}"] = (s // (2 * h) == t // (2 * h)) & (s % (2 * h) < h) & (t % (2 * h) >= h)
    out["level0t"] = out["level0"].T
    n = np.arange(T)[None, :] + np.zeros((P, 1))
    out["carry64"], out["carry128"] = n % CH != 0, n % P != 0
    c = np.arange(NE * P)[None, :]
    out["sel16"] = (c // P == s) & (s < NE)
    m = np.arange(2 * T)
    d = 511 - m
    large = np.minimum(16 + (np.log(np.maximum(d, 16) / 16.0) / np.log(8.0) * 16 + 1e-9).astype(np.int64), 31)
    bucket = np.where(d < 16, d, large)
    out["bucket"] = (bucket[None, :] == s) & (d >= 0)[None, :]
    return np.concatenate([np.broadcast_to(out[k], (P, w)).astype(f) for k, (_, w) in CONSTS.items()], 1)


def _prepare(i):
    i = {k: np.asarray(v) for k, v in i.items()}
    z = lambda r, c: np.zeros((r, c), np.float32)
    w = i["w_in"][0]
    zc, xbc, dtc, rw = np.split(w, [512, 1536, 1544], axis=1)
    cols = np.concatenate([xbc, dtc, z(D, P - 8), _rwkv_tiles(rw), zc, z(D, P)], 1)
    order = np.concatenate
    w2 = i["w_in_2"][0]
    a_u, a_v, g_q, g_k, g_v, g_r, g_a, d_q, d_k, d_v, d_iq, d_ik, d_iw, gates = np.split(
        w2, np.cumsum([512, 512, 256, 256, 512, 512, 16, 512, 512, 512, 256, 64, 4]), axis=1)
    cols2 = order([a_u, a_v, g_q, g_k, g_v, g_r, g_a, z(D, 16), d_iw, z(D, 92), d_q, d_k, d_v, d_iq, d_ik, d_ik], 1)
    up = i["ffn_w_up"][0]
    gu, vu = _units_1024(up[:, :D_FF]), _units_1024(up[:, D_FF:])
    down = _units_down(i["ffn_w_down"][0])
    eg = np.concatenate([_units_1024(i["w_exp_gate_2"][0, e]) for e in range(NE)])
    eu = np.concatenate([_units_1024(i["w_exp_up_2"][0, e]) for e in range(NE)])
    ed = _units_down(i["w_exp_down_2"][0])

    def steps(g, v, d):
        out = [g[0], v[0]]
        for k in range(1, len(g)):
            out += [g[k], v[k], d[k - 1]]
        return np.stack(out + [d[-1]])

    w_mod = i["w_mod_2"][0].reshape(KT, P, N_MOD, 256).transpose(2, 1, 0, 3).reshape(N_MOD, P, UNIT)
    branch = []
    gate_units = _units_1024(gates)
    for n in range(3):
        b = i["w_branch_2"][0, n].reshape(4, P, 2, 2, 256).transpose(2, 1, 3, 0, 4).reshape(2, P, UNIT)
        for h in range(2):
            branch += [b[h], gate_units[4 * n + 2 * h], gate_units[4 * n + 2 * h + 1]]
    units = order([_units_1024(cols), w_mod, _units_1024(i["w_out"][0]), steps(gu, vu, down),
                   _units_1024(cols2), np.stack(branch), _units_1024(i["w_out_2"][0]), steps(eg, eu, ed)])
    mu = _rwkv_tiles(i["rwkv_mu"][0])
    fc = order([i["ffn_conv_w"][0], i["ffn_conv_b"]], 0)
    fc = fc.reshape(4, 2, NF, 2, P).transpose(4, 2, 1, 3, 0).reshape(P, 16 * NF)
    small = {
        "g_pre_mix": i["pre_mix_norm"], "g_post_mix": i["post_mix_norm"], "g_pre_ffn": i["pre_ffn_norm"],
        "g_post_ffn": i["post_ffn_norm"], "conv_w": i["ssd_conv_w"][0], "conv_b": i["ssd_conv_b"],
        "dt_bias": i["ssd_dt_bias"], "a_log": i["ssd_a_log"], "d_skip": np.repeat(i["ssd_d"][0], CH),
        "ssd_norm": i["ssd_norm"], "mu": mu, "w0": i["rwkv_w0"], "a0": i["rwkv_a0"], "k_k": i["rwkv_k_k"],
        "k_a": i["rwkv_k_a"], "r_k": i["rwkv_r_k"], "ln_w": i["rwkv_ln_w"], "ln_b": i["rwkv_ln_b"],
        "c": i["c_2"], "b_mod": i["b_mod_2"], "g1": i["g_norm1_2"], "g2": i["g_norm2_2"],
        "gmlp_g": i["gmlp_ln_g_2"], "gmlp_b": i["gmlp_ln_b_2"], "b_gate": i["gla_b_gate_2"],
        "gla_g": i["gla_norm_g_2"], "q_g": i["dsa_qnorm_g_2"], "k_g": i["dsa_knorm_g_2"],
        "b_branch": i["b_branch_gate_2"]}
    small = {k: _columns(v) for k, v in small.items()}
    small["b_route"] = np.broadcast_to(order([i["b_group_2"][0], i["b_router_2"][0]])[None], (P, 20))
    small["rel_bias"] = np.pad(i["rel_bias_2"], ((0, P - 32), (0, 0)))
    small["ffn_conv"] = fc
    for k, (_, n) in SMALL.items():
        assert small[k].shape == (P, n), (k, small[k].shape)
    route = order([i["w_group_2"][0], i["w_router_2"][0]], 1)
    mats = {"wa2": order([i["rwkv_w2"][0], i["rwkv_a2"][0]]), "g2m": i["rwkv_g2"][0],
            "gate2": np.pad(i["gla_w_gate2_2"][0], ((0, P - 16), (0, 0))),
            "w_s": i["gmlp_w_s_2"][0].transpose(1, 0, 2).reshape(P, 4 * P),
            "b_s": np.pad(i["gmlp_b_s_2"][0].reshape(1, T), ((0, P - 1), (0, 0))),
            "w_route": np.pad(route.reshape(KT, P, 20).transpose(1, 0, 2).reshape(P, KT * 20), ((0, 0), (0, P - 16)))}
    fixed = order([_constants()] + [small[k] for k in SMALL] + [mats[k] for k in MATS], 1)
    return {"units": np.ascontiguousarray(units), "fixed": np.ascontiguousarray(fixed, dtype=np.float32),
            "x": np.ascontiguousarray(i["x"][0])}


def kernel(**inputs):
    import concourse.bacc as bacc
    from concourse.bass_utils import run_bass_kernel_spmd

    nc = bacc.Bacc("TRN2", target_bir_lowering=False, num_devices=1)
    arrays = _prepare(inputs)
    aps = [nc.dram_tensor(k, v.shape, F32, kind="ExternalInput").ap() for k, v in arrays.items()]
    skew = nc.dram_tensor("bias_rows", (4, 2 * T), F32, kind="Internal").ap()
    out = nc.dram_tensor("out", (T, D), F32, kind="ExternalOutput").ap()
    build(nc, *aps, skew, out)
    r = run_bass_kernel_spmd(nc, [arrays], core_ids=[0])
    return r.results[0]["out"].reshape(1, T, D)
```

```python
from contextlib import ExitStack

import numpy as np
import concourse.bass as bass
from concourse import mybir

F32 = mybir.dt.float32
F32R = mybir.dt.float32r
ALU = mybir.AluOpType
ACT = mybir.ActivationFunctionType
AX = mybir.AxisListType

T = 512
P = 128
NT = T // P
D = 1024
KT = D // P
UNIT = 2048
CHUNK = UNIT // 2
RING = 2
PADW = 516
D_FF = 2816
NF = D_FF // 256
NE = 16
GATE_ROUNDS = (3, 4, 6, 7, 9, 10, 13, 14)
N_MOD = 6 * D // 256
MOD_BATCH = N_MOD // 4
CH = 64
NC = T // CH
EXP_HALF = 0.6065306597126334
LOG1P_TERMS = 7

XS, BM, CM, DT, WA, GL, RR, KK_, VV, ZZ, N_PROJ = 0, 4, 6, 8, 9, 10, 11, 15, 19, 23, 28
AU, AV, GQ, GK, GV, GR, MISC, DQ, DK, DV, IQ, IK = 0, 4, 8, 10, 12, 16, 20, 21, 25, 29, 33, 35


def layout(sizes):
    at, out = 0, {}
    for name, width in sizes:
        out[name] = (at, width)
        at += width
    return out, at


CONSTS, N_CONST = layout(
    [("ident", P), ("ones", P), ("blk64", P), ("flip", P), ("strict64", P), ("incl64", P), ("incl128", P),
     ("level0t", P)] + [(f"level{k}", P) for k in range(7)] +
    [("carry64", T), ("carry128", T), ("sel16", NE * P), ("bucket", 2 * T), ("neg128", P)])
SMALL, N_SMALL = layout(
    [("g_pre_mix", KT), ("g_post_mix", KT), ("g_pre_ffn", KT), ("g_post_ffn", KT),
     ("conv_w", 4 * 8), ("conv_b", 8), ("dt_bias", 1), ("a_log", 1), ("d_skip", 4), ("ssd_norm", 4),
     ("mu", 14), ("w0", 4), ("a0", 4), ("k_k", 4), ("k_a", 4), ("r_k", 4), ("ln_w", 4), ("ln_b", 4),
     ("c", KT), ("b_mod", 48), ("g1", KT), ("g2", KT), ("gmlp_g", 4), ("gmlp_b", 4),
     ("b_gate", 2), ("gla_g", 1), ("q_g", 1), ("k_g", 1), ("b_branch", 24),
     ("b_route", 20), ("rel_bias", 4), ("ffn_conv", 16 * NF)])
MATS, N_MATS = layout(
    [("wa2", T), ("g2m", T), ("gate2", 256), ("w_s", 4 * P), ("b_s", T), ("w_route", KT * 20 + P - 16)])
N_SMALLS = 560
C0, S0, M0 = 0, N_CONST, N_CONST + N_SMALL
N_FIX = N_CONST + N_SMALL + N_MATS


def build(nc, units, fixed, x, skew, out):
    ctx = ExitStack()
    with ctx:
        ring = ctx.enter_context(nc.sbuf_tensor("weight_ring", [P, RING, UNIT], F32))
        fix = ctx.enter_context(nc.sbuf_tensor("fixed_data", [P, N_FIX], F32))
        res = ctx.enter_context(nc.sbuf_tensor("residual", [P, KT, T], F32))
        xn = ctx.enter_context(nc.sbuf_tensor("normed", [P, KT, T], F32))
        xn_at = nc.sbuf_base - 4 * KT * T
        tiny = ctx.enter_context(nc.sbuf_tensor("tiny", [P, 1024], F32))
        n_arena = 30176
        arena = ctx.enter_context(nc.sbuf_tensor("arena", [P, n_arena], F32))
        arena_at = nc.sbuf_base - 4 * n_arena
        ps = ctx.enter_context(nc.psum_tensor("psum", [P, 8, T], F32))

        sems = {}

        def sem(name):
            if name not in sems:
                sems[name] = ctx.enter_context(nc.semaphore(name))
            return sems[name]

        def C(name, rows=P, a=0, b=None):
            o, w = CONSTS[name]
            return fix[0:rows, C0 + o + a:C0 + o + (w if b is None else b)]

        def S(name, j=0, n=1, rows=P):
            o, _ = SMALL[name]
            return fix[0:rows, S0 + o + j:S0 + o + j + n]

        def M(name, r0=0, r1=P, a=0, b=None):
            o, w = MATS[name]
            return fix[r0:r1, M0 + o + a:M0 + o + (w if b is None else b)]

        def A(off, n=T, r0=0, r1=P):
            assert off + n <= n_arena, (off, n, n_arena)
            return arena[r0:r1, off:off + n]

        def four(ap):
            return ap.rearrange("p (a b) -> p a b", a=4)

        def rep4(ap):
            return ap.unsqueeze(1).to_broadcast([ap.shape[0], 4, ap.shape[1]])

        full = [sem(f"bank{b}_full") for b in range(8)]
        free = [sem(f"bank{b}_free") for b in range(8)]
        used = [0] * 8
        place = {}

        def bank_of(what, k=0):
            return place[what, k][0]

        def filled(eng, what, k=0, it=None):
            b, n, per = place[what, k]
            eng.wait_ge(full[b], n + 1 if it is None else it * per + (n + 1))

        def emptied(eng, what, k=0, it=None):
            b, n, per = place[what, k]
            eng.wait_ge(free[b], n + 1 if it is None else it * per + (n + 1))

        def freed(what, k=0):
            return free[place[what, k][0]]

        class Chain:

            def __init__(self, eng, name):
                self.eng, self.sem, self.n, self.it, self.per = eng, sem(name), 0, None, 0

            def link(self, ins):
                self.n += 1
                ins.then_inc(self.sem, 1)
                self.eng.wait_ge(self.sem, self.n if self.it is None else self.it * self.per + self.n)

            def enter(self, it, per):
                self.it, self.per, self.at = it, per, self.n

            def leave(self, times):
                assert self.n - self.at == self.per, (self.n - self.at, self.per)
                self.n = self.at + self.per * times
                self.it = None

        def part(name, off, cols, base=None):
            return nc.alloc_sbuf_tensor_at(name, [P, cols], F32R, offset=(arena_at if base is None else base) + 4 * off)

        class Weights:

            def __init__(self, name, off):
                self.hi, self.lo = part(name + "_hi", off, 2 * CHUNK), part(name + "_lo", off + 2 * CHUNK, 2 * CHUNK)

            def slot(self, q):
                c = slice(q % 2 * CHUNK, (q % 2 + 1) * CHUNK)
                return self.hi[:, c], self.lo[:, c]

        class Tiles:

            def __init__(self, name, n, lo_off, hi=None, hi_off=None):
                self.off = lo_off
                self.his = hi if hi is not None else part(name + "_hi", hi_off, n * T)
                self.los = part(name + "_lo", lo_off, n * T)

            def raw(self, k):
                return A(self.off + k * T)

            def hi(self, k):
                return self.his[:, k * T:(k + 1) * T]

            def lo(self, k):
                return self.los[:, k * T:(k + 1) * T]

        x_hi = part("normed_hi", 0, KT * T, xn_at)

        PROJ = 0
        YM = N_PROJ * PADW
        WK = YM + 8 * T

        def proj(t, r0=0, r1=P, shift=0):
            return A(PROJ + t * PADW + 3 - shift, T, r0, r1)

        def ym(t, r0=0, r1=P):
            return A(YM + t * T, T, r0, r1)

        XT = PROJ
        SQ = WK
        SQ1 = 8208
        in1 = Tiles("in1", KT, WK, x_hi)
        w_in1 = Weights("w_in1", WK + 4096)
        CONV = WK + 8192
        y1 = Tiles("y1", KT, YM, None, WK + 6144)
        w_out1 = Weights("w_out1", WK + 2048)
        s_XD, s_XS2, s_BT, s_SI, s_GT, s_HB, s_CE = [
            WK + o for o in (0, 2048, 4096, 5120, -1024, 6656, 7680)]
        def ew(i, r0=0, r1=P):
            return A(WK + i * T, T, r0, r1)

        e_AT, e_BH, e_KH, e_BP, e_KP = range(5, 10)
        pr_W, pr_P, pr_INV, pr_B = [A(WK + 9216 + i * T) for i in range(4)]
        pr_KK = ew(e_BP)

        def tm(i):
            return A(WK + 5120 + i * T).rearrange("p (t c) -> p t c", t=NT)

        t_A, t_BP, t_KP, t_V = range(4)
        h_buf = [[A(WK + 7168 + i * T) for i in range(4)] + [proj(ZZ + 1), proj(ZZ + 2)],
                 [ew(i) for i in (0, 1, 2, 3, 4, e_KP)]]
        m_AT, m_LV, m_X, m_Z, m_U, m_AW = range(6)
        gt_all = xn[0:CH, :, :].rearrange("p a b -> p (a b)").rearrange("p (c h i) -> p c h i", c=NC, h=8)
        h_all = A(PROJ, 4096, 0, CH).rearrange("p (c h i) -> p c h i", c=NC, h=8)
        TW = PROJ + DT * PADW
        SG = PROJ + ZZ * PADW

        MOD_PARTS = (ZZ + 3, ZZ + 4, GL)

        def mod_part(i):
            return proj(MOD_PARTS[i // 2])[:, (i % 2) * 256:(i % 2 + 1) * 256]

        F_UB, F_CB, F_ACC, F_ACT, F_CMB, F_IN, F_W, F_RT = 0, 2064, 4112, 8208, 12304, 20496, 24592, 28688
        in_ff = Tiles("in_ff", KT, F_IN, x_hi)
        w_ff = Weights("w_ff", F_W)
        acts = Tiles("acts", 4, F_ACT, None, F_ACT + 2048)
        N_ROUTE = MATS["w_route"][1]
        route_hi, route_lo = part("w_route_hi", F_RT, N_ROUTE), part("w_route_lo", F_RT + N_ROUTE, N_ROUTE)

        class Pair:

            def __init__(self, sub):
                self.hi, self.lo = (lambda i: acts.hi(2 * sub + i)), (lambda i: acts.lo(2 * sub + i))

        acts_of = [Pair(0), Pair(1)]

        def at(j, m, k):
            return m * j + k if isinstance(j, int) else j[0] * (2 * m) + (m * j[1] + k)

        def p2(t, r0=0, r1=P):
            return A(t * T, T, r0, r1)

        W2 = 36 * T
        g_VT, g_WS, g_SQ = W2, W2 + 2048, W2
        l_B, l_E, l_QK, l_AT, l_KT, l_ST, l_VT = W2, W2 + 1024, W2 + 2048, W2 + 3072, W2 + 5120, W2 + 6144, GV * T
        sq_gla = [A(l_AT + i * T) for i in range(4)]
        sq_qk = A(W2 + 6912)
        d_MA, d_SC, d_LG = W2 + 256, W2 + 1536, W2 + 1536
        d_RL, d_PT = (MISC * T, W2 + 2688), (W2 + 2560, MISC * T)
        d_HK = (AU * T, AU * T + 896, IQ * T, IQ * T + 896)
        d_VT, d_BR = DV * T, (DV + 2) * T
        SQ2 = AU * T
        MG = GQ * T
        sig = [[p2(t) for t in (IQ, IQ + 1, IK, MISC)], [tiny[:, 0:T], tiny[:, T:2 * T]],
               [A(W2 + 4096 + i * T) for i in range(4)]]
        in2 = Tiles("in2", KT, n_arena - 4096, x_hi)
        w_in2 = Weights("w_in2", n_arena - 8192)
        w_br = [Weights("w_br0", W2 + 3552)] * 2 + [Weights("w_br", DK * T)]
        ys = [Tiles("ya", 4, AU * T, None, AV * T), Tiles("yb", 4, GR * T, None, AV * T),
              Tiles("yc", 4, DQ * T, None, AU * T)]
        merged2 = Tiles("merged2", KT, MG, None, W2)
        OUT = 0

        v_tmp = tiny[:, 0:T]
        v_rs = tiny[:, T:2 * T]

        sm_o = [0]
        smalls = ctx.enter_context(nc.sbuf_tensor("smalls", [P, N_SMALLS], F32))

        def small(n, rows=P):
            o = sm_o[0]
            sm_o[0] += n
            assert sm_o[0] <= N_SMALLS
            return smalls[0:rows, o:o + n]

        dec3 = small(96)
        expA = small(1)
        one_ka = small(4)
        pls = small(16, CH)
        csil = small(KT)
        c_last = small(32)
        mod = small(48)
        gmod = small(KT)
        qg = small(1)
        row_rs = [dec3[:, 0:16], dec3[:, 16:48]]
        head_rs = dec3[:, 48:80]
        iw = small(16)
        top8 = small(24)
        nmax = small(4)
        rsum = small(4)
        rinv = small(4)
        rt_l, rt_c = small(80), small(64)
        rt_w = [small(16) for _ in range(5)]
        rt_s = [small(4) for _ in range(8)]

        block = ctx.enter_context(nc.Block())
        PSB = [ps[:, b, :] for b in range(8)]


        @block.tensor
        def _(pe):
            chunk = [0]

            def mm(o, l, r, start=True, stop=True):
                return nc.tensor.matmul(o, l, r, start=start, stop=stop)

            def tr(o, i):
                k = i.shape[0]
                return nc.tensor.transpose(o, i, C("ident", k, 0, k))

            def open_(what, k, b, it=None, per=0):
                if used[b]:
                    pe.wait_ge(free[b], used[b] if it is None else it * per + used[b])
                place[what, k] = (b, used[b], per)
                used[b] += 1
                return PSB[b]

            def close(last, what, k=0):
                last.then_inc(full[place[what, k][0]], 1)

            def take(weights, it=None, per=0):
                q = chunk[0]
                chunk[0] += 1
                pe.wait_ge(sem("split_ready"), q + 1 if it is None else it * per + (q + 1))
                return weights.slot(q)

            def norm_sum(what, srcs, ones, ready, b=4):
                o = open_(what, 0, b)
                for k, src in enumerate(srcs):
                    pe.wait_ge(*ready(k))
                    last = mm(o, ones, src, k == 0, k == len(srcs) - 1)
                close(last, what)

            def tile_of(w, nk, width, col, rhs, o, first, ready=None):
                hi, lo = [part_.rearrange("p (k c) -> p k c", k=nk) for part_ in w]
                c = slice(col, col + P)
                for k in range(nk):
                    if ready:
                        pe.wait_ge(sem(ready), k + 1)
                    begun = mm(o, hi[:, k, c], rhs.hi(k), k == 0, False)
                    if first and k == 0:
                        begun.then_inc(sem("split_used"), 1)
                    mm(o, lo[:, k, c], rhs.hi(k), False, False)
                    last = mm(o, hi[:, k, c], rhs.lo(k), False, k == nk - 1)
                return last

            def project(what, n_units, weights, rhs, t0=0, b0=0, nb=4, ready=None):
                for i in range(2 * n_units):
                    w = take(weights)
                    o = open_(what, t0, b0 + t0 % nb)
                    close(tile_of(w, KT, P, 0, rhs, o, True, None if i else ready), what, t0)
                    t0 += 1

            def modulation(m):
                pe.wait_ge(sem("mod_part_ready"), MOD_BATCH * (m + 1))
                for i in range(MOD_BATCH):
                    for j in range(2):
                        c = 2 * (MOD_BATCH * m + i) + j
                        last = mm(PSB[7][:, c:c + 1], mod_part(i)[:, j * P:(j + 1) * P], C("ones", b=1))
                if m == 3:
                    close(last, "mod")
                else:
                    last.then_inc(sem("mod_parts_used"), 1)

            pe.wait_ge(sem("ident_loaded"), 16)
            pe.wait_ge(sem("x_loaded"), 16 * NT)
            for k in range(KT):
                o = open_("x", k, k % 4)
                for t in range(NT):
                    last = tr(o[:, t * P:(t + 1) * P], A(XT + t * D + k * P, P))
                close(last, "x", k)
            norm_sum("sum_pre_mix", [A(SQ + k * T) for k in range(KT)], C("ones"), lambda k: (sem("sq_pre_mix"), k + 1))
            project("proj", 14, w_in1, in1, ready="xn_ready")

            pe.wait_ge(sem("fixed_loaded"), 32)
            pe.wait_ge(sem("dt_ready"), 1)
            o = open_("dec3", 0, 4)
            for i in range(3):
                for t in range(NT):
                    last = tr(o[:, (i * NT + t) * 8:(i * NT + t + 1) * 8], ym([0, 1, 2][i], 0, 8)[:, t * P:(t + 1) * P])
            close(last, "dec3")
            pe.wait_ge(sem("xbc_ready"), 8)
            for t in range(NT):
                o = open_("xs_tm", t, t)
                for k in range(4):
                    last = tr(o[:, k * P:(k + 1) * P], proj(XS + k)[:, t * P:(t + 1) * P])
                close(last, "xs_tm", t)
            for i in range(2):
                o = open_("b_tm", i, 5 + i)
                for t in range(2):
                    for g in range(2):
                        last = tr(o[:, (t * 2 + g) * P:(t * 2 + g + 1) * P],
                                  proj(BM + g)[:, (2 * i + t) * P:(2 * i + t + 1) * P])
                close(last, "b_tm", i)
            for g in range(2):
                o = open_("scores", g, 5 + g)
                for t in range(NT):
                    c = slice(t * P, (t + 1) * P)
                    last = mm(o[:, c], proj(BM + g)[:, c], proj(CM + g)[:, c])
                close(last, "scores", g)
            emptied(pe, "b_tm", 1)
            pe.wait_ge(sem("xs2_ready"), NT)
            for t in range(3):
                o = open_("state", t, t)
                for g in range(2):
                    last = mm(o[:, g * 256:(g + 1) * 256], A(s_BT, 1024)[:, (t * 2 + g) * P:(t * 2 + g + 1) * P],
                              A(s_XS2, 2048)[:, t * T + g * 256:t * T + (g + 1) * 256])
                close(last, "state", t)

            def cs_row(h):
                close(mm(open_("cs_row", h, 5 + h % 2), C("sel16", 8, h * P, (h + 1) * P), ym(1, 0, 8)), "cs_row", h)

            def prepare(m, step, b):
                c = slice(m * P, (m + 1) * P)
                if step == 1:
                    pe.wait_ge(sem("tanh_ready"), 1)
                    close(mm(open_("a_low", m, b), M("wa2", CH, P)[:, c], proj(WA, CH, P)), "a_low", m)
                if step == 2:
                    close(mm(open_("w_low", m, b), M("wa2", 0, CH)[:, c], A(TW, T, 0, CH)), "w_low", m)
                if step == 3:
                    norm_sum(f"sum_kk{m}", [pr_P], C("blk64"), lambda _: (sem("sq_kk"), m + 1), b)
                if step == 4:
                    norm_sum(f"sum_bonus{m}", [pr_INV], C("blk64"), lambda _: (sem("bonus_in"), m + 1), b)

            o = open_("chunk_decay", 0, 7)
            for h in range(8):
                last = mm(o[:, h * NT:(h + 1) * NT], C("sel16", 8, h * P, (h + 1) * P), ym(1, 0, 8)[:, P - 1::P])
            close(last, "chunk_decay")
            cs_row(0)
            cs_row(1)
            for h in range(8):
                m, e = h // 2, h % 2
                if e == 0:
                    o = open_("ssd_y", m, m)
                pe.wait_ge(sem("mt_ready"), h + 1)
                rows = o[e * CH:(e + 1) * CH, :]
                for t in range(NT):
                    c = slice(t * P, (t + 1) * P)
                    last = mm(rows[:, c], A(s_XD, 2048)[:, t * T + h * CH:t * T + (h + 1) * CH],
                              A(s_HB + (h % 2) * T)[:, c], True, t == 0)
                    if t:
                        last = mm(rows[:, c], A(s_SI + (t - 1) * T)[:, h * CH:(h + 1) * CH],
                                  A(s_CE + (h % 2) * T)[:, c], False, True)
                if e:
                    close(last, "ssd_y", m)
                else:
                    last.then_inc(sem("ssd_head_used"), 1)
                if h + 2 < 8:
                    cs_row(h + 2)
                if 1 <= h < 5:
                    prepare(0, h, 4)
            for g in range(2):
                norm_sum(f"sum_ssd{g}", [A(s_XD + (2 * g + i) * T) for i in range(2)], C("ones"),
                         lambda i: (sem("sq_ssd"), 2 * g + i + 1))

            open_("mod", 0, 7)
            for m in range(4):
                if m:
                    modulation(m - 1)
                pe.wait_ge(sem("pair_ready"), m + 1)
                o = open_("last_decay", m, 0)
                for e in range(2):
                    r = slice(e * CH, (e + 1) * CH)
                    last = mm(o[0:CH, e * NC:(e + 1) * NC], C("ident")[:, r], pr_P[:, CH - 1::CH])
                close(last, "last_decay", m)
                for i, src in enumerate((ew(e_AT), ew(e_BP), ew(e_KP), proj(VV + m))):
                    o = open_(("tm", m), i, 1 + i)
                    for t in range(NT):
                        last = tr(o[:, t * P:(t + 1) * P], src[:, t * P:(t + 1) * P])
                    close(last, ("tm", m), i)

                def gram(what, e, b, l, r):
                    o = open_((what, m), e, b)
                    rows = slice(e * CH, (e + 1) * CH)
                    for t in range(NT):
                        c = slice(t * P, (t + 1) * P)
                        last = mm(o[:, c], l[rows, c], r[rows, c])
                    close(last, (what, m), e)

                def units4(what, e, b, l, r):
                    o = open_((what, m), e, b)
                    for t in range(NT):
                        c = slice(t * P, (t + 1) * P)
                        last = mm(o[:, c], l[:, c], r[:, c])
                    close(last, (what, m), e)

                for e in range(2):
                    gram("abT", e, 5 + e, ew(e_BH), ew(e_AT))
                for e in range(2):
                    gram("ab", e, 1 + e, ew(e_AT), ew(e_BH))
                for lv in range(1, 6):
                    for e in range(2):
                        hb = h_buf[e]
                        if lv == 1:
                            pe.wait_ge(sem(f"level{e}_ready"), m + 1)
                        else:
                            emptied(pe, (f"XU{lv - 1}", m), e)
                        units4(f"U{lv}", e, 3 * e, hb[m_LV], hb[m_X])
                    for e in range(2):
                        hb = h_buf[e]
                        emptied(pe, (f"U{lv}", m), e)
                        units4(f"ZU{lv}", e, 3 * e + 1, hb[m_U], hb[m_Z])
                        if lv < 5:
                            units4(f"XU{lv}", e, 3 * e + 2, hb[m_Z], hb[m_U])
                    if m < 3:
                        prepare(m + 1, lv, 6)
                for e in range(2):
                    gram("akT", e, 3 * e, ew(e_KH), ew(e_AT))
                    gram("rbT", e, 3 * e + 1, ew(e_BH), proj(RR + m))
                    gram("rkT", e, 3 * e + 2, ew(e_KH), proj(RR + m))
                for e in range(2):
                    hb, r = h_buf[e], slice(e * CH, (e + 1) * CH)
                    emptied(pe, ("akT", m), e)
                    o = open_(("wv", m), e, 3 * e)
                    for t in range(NT):
                        last = mm(o[:, t * CH:(t + 1) * CH], hb[m_X][:, t * P:(t + 1) * P], tm(t_V)[:, t, r])
                    close(last, ("wv", m), e)
                for e in range(2):
                    hb = h_buf[e]
                    emptied(pe, ("wv", m), e)
                    units4("aw", e, 3 * e, hb[m_Z], hb[m_U])
                for e in range(2):
                    hb, r = h_buf[e], slice(e * CH, (e + 1) * CH)
                    emptied(pe, ("rkT", m), e)
                    emptied(pe, ("aw", m), e)
                    o = open_(("ry", m), e, 3 * e + 1)
                    for t in range(NT):
                        c = slice(t * P, (t + 1) * P)
                        mm(o[:, c], hb[m_AW][:, c], hb[m_AT][:, c], True, False)
                        mm(o[CH:P, c], tm(t_V)[:, t, r], hb[m_LV][:, c], False, True)
                        last = mm(o[0:CH, c], C("ident")[:, r], proj(RR + m)[:, c], False, True)
                    close(last, ("ry", m), e)
                    b = ((0, 2, 3, 5), (6, 0, 2, 3))[e]
                    for i in range(2):
                        q = slice(i * CH, (i + 1) * CH)
                        a = four(hb[m_AW])
                        og = open_(("gt", m), 2 * e + i, b[i])
                        for t in range(NT):
                            last = mm(og[0:CH, t * CH:(t + 1) * CH], a[q, t, 0:CH], tm(t_BP)[q, t, r])
                        close(last, ("gt", m), 2 * e + i)
                    for i in range(2):
                        q = slice(i * CH, (i + 1) * CH)
                        oh = open_(("hh", m), 2 * e + i, b[2 + i])
                        for t in range(NT):
                            c = slice(t * CH, (t + 1) * CH)
                            mm(oh[0:CH, c], tm(t_BP)[q, t, r], a[q, t, CH:P], True, False)
                            last = mm(oh[0:CH, c], tm(t_KP)[q, t, r], tm(t_V)[q, t, r], False, True)
                        close(last, ("hh", m), 2 * e + i)
            modulation(3)
            for i in range(4):
                emptied(pe, ("hh", 3), i)
            for cn in range(1, NC - 1):
                if cn > 1:
                    emptied(pe, ("s", cn - 1))
                o = open_(("s", cn), 0, 0)
                for h in range(8):
                    last = mm(o[0:CH, h * CH:(h + 1) * CH], gt_all[:, cn, h, :], h_all[:, cn - 1, h, :])
                close(last, ("s", cn))
            emptied(pe, ("s", NC - 2))
            def sum_y(m):
                norm_sum(f"sum_y{m}", [ew(m)], C("blk64"),
                         lambda _: (freed("rwkv_y", m), place["rwkv_y", m][1] + 1), 4 + m % 2)

            for m in range(4):
                o = open_("rwkv_y", m, m)
                for e in range(2):
                    rows = o[e * CH:(e + 1) * CH, :]
                    ry = proj((RR, KK_)[e] + m)
                    mm(rows, C("ident")[:, CH:P], ry, True, False)
                    for cn in range(1, NC):
                        c = slice(cn * CH, (cn + 1) * CH)
                        last = mm(rows[:, c], h_all[:, cn - 1, 2 * m + e, :], ry[0:CH, c], False, cn == NC - 1)
                close(last, "rwkv_y", m)
                if m:
                    sum_y(m - 1)
            sum_y(3)
            pe.wait_ge(sem("sg_ready"), 1)
            for m in range(4):
                close(mm(open_("gate", m, 4 + m), M("g2m", a=m * P, b=(m + 1) * P), A(SG)), "gate", m)
            o = open_("head_squares", 0, 0)
            for m in range(4):
                pe.wait_ge(sem("sq_y"), m + 1)
                for t in range(NT):
                    c = 2 * (m * NT + t)
                    last = mm(o[:, c:c + 2], proj(VV + m)[:, t * P:(t + 1) * P], C("blk64")[:, 0::CH])
            close(last, "head_squares")
            pe.wait_ge(sem("head_rs_ready"), 1)
            for m in range(4):
                o = open_("y_rs", m, m)
                for t in range(NT):
                    for e in range(2):
                        c = 2 * (m * NT + t) + e
                        last = mm(o[e * CH:(e + 1) * CH, t * P:(t + 1) * P],
                                  head_rs[:, c:c + 1].to_broadcast([P, CH]), C("ident"))
                close(last, "y_rs", m)
            pe.wait_ge(sem("ssd_out_ready"), 4)
            project("mix", 4, w_out1, y1, ready="y_ready")


            def sums(what, names, ready):
                norm_sum(what, names, C("ones"), lambda k: (sem(ready), k + 1))

            sq8 = [A(SQ1 + k * T) for k in range(KT)]
            sums("sum_post_mix", sq8, "sq_post_mix")
            sums("sum_pre_ffn", sq8, "sq_pre_ffn")
            def up(kind, phase, sub, it=None, ready=None):
                for i in range(4):
                    w = take(w_ff, it, 12)
                    k = (phase, sub, i)
                    o = open_(kind + "_up", k, i, it, 2)
                    close(tile_of(w, KT, P, 0, in_ff, o, True, None if i else ready), kind + "_up", k)

            def down(kind, phase, j, it=None):
                sub = j % 2 if isinstance(j, int) else j[1] % 2
                pe.wait_ge(sem(kind + "_act_ready"), at(j, 2, 2))
                for m in range(KT):
                    if m % 4 == 0:
                        w = take(w_ff, it, 12)
                    k = (phase, sub, m)
                    o = open_(kind + "_down", k, 4 + m % 4, it, 4)
                    close(tile_of(w, 2, T, m % 4 * P, acts_of[sub], o, m % 4 == 0), kind + "_down", k)

            def gated(kind, n):
                times = (n - 1) // 2
                with pe.Fori(0, times) as it:
                    up(kind, "loop", 1, it)
                    down(kind, "loop", (it, 0), it)
                    up(kind, "loop", 0, it)
                    down(kind, "loop", (it, 1), it)
                for b in range(8):
                    used[b] += (2 if b < 4 else 4) * (times - 1)
                chunk[0] += 12 * (times - 1)
                if n % 2 == 0:
                    up(kind, "last", 1)
                    down(kind, "last", n - 2)
                down(kind, "last", n - 1)

            up("ffn", "first", 0, ready="ffn_in_ready")
            gated("ffn", NF)
            sq8b = [A(F_CMB + k * T) for k in range(KT)]
            sums("sum_post_ffn", sq8b, "sq_post_ffn")
            sums("sum_1", sq8b, "sq_1")
            for i in range(2):
                close(mm(open_("bias_row", i, 4 + i)[0:4, :], S("rel_bias", 0, 4), C("bucket", P, i * T, (i + 1) * T)),
                      "bias_row", i)
            project("p2", 4, w_in2, in2, ready="h_ready")
            o = open_("w_s", 0, 6)
            for g in range(4):
                last = tr(o[:, g * P:(g + 1) * P], M("w_s")[:, g * P:(g + 1) * P])
            close(last, "w_s")
            project("p2", 3, w_in2, in2, 8)
            norm_sum("gmlp_mean", [p2(AV + k) for k in range(4)], C("ones"), lambda k: (free[bank_of("p2", AV + k)], place["p2", AV + k][1] + 1))
            project("p2", 2, w_in2, in2, 14)
            sums("gmlp_var", [A(g_SQ + k * T) for k in range(4)], "sq_gmlp")
            project("p2", 2, w_in2, in2, 18)
            pe.wait_ge(sem("gmlp_v_ready"), 4)
            for t in range(NT):
                o = open_("gmlp_vt", t, 4 + t)
                for k in range(4):
                    last = tr(o[:, k * P:(k + 1) * P], p2(AV + k)[:, t * P:(t + 1) * P])
                close(last, "gmlp_vt", t)
            emptied(pe, "w_s")
            for t in range(NT):
                emptied(pe, "gmlp_vt", t)
            for g in range(4):
                o = open_("mixed", g, 4 + g)
                for t in range(NT):
                    c = slice(t * P, (t + 1) * P)
                    mm(o[:, c], A(g_VT, 2048)[:, t * T + g * P:t * T + (g + 1) * P], A(g_WS)[:, g * P:(g + 1) * P], True, False)
                    last = mm(o[:, c], C("ones"), M("b_s")[:, g * P:(g + 1) * P], False, True)
                close(last, "mixed", g)
            emptied(pe, "p2", MISC)
            for m in range(2):
                close(mm(open_("forget", m, 4 + m), M("gate2")[:, m * P:(m + 1) * P], p2(MISC)), "forget", m)
            project("p2", 7, w_in2, in2, 22)
            for t in range(NT):
                o = open_("gla_vt", t, 4 + t)
                for k in range(4):
                    last = tr(o[:, k * P:(k + 1) * P], p2(GV + k)[:, t * P:(t + 1) * P])
                close(last, "gla_vt", t)
            def row_sums(o, i, tile):
                for t in range(NT):
                    last = mm(o[:, i * NT + t:i * NT + t + 1], tile[:, t * P:(t + 1) * P], C("ones", b=1))
                return last

            sum_qk = open_("sum_qk", 0, 7)
            for lv in range(8):
                for m in range(2):
                    pe.wait_ge(sem("level_ready"), 2 * lv + m + 1)
                    for e in range(2):
                        r = slice(e * CH, (e + 1) * CH)
                        o = open_(("attn", lv), 2 * m + e, 2 * m + e)
                        for t in range(NT):
                            c = slice(t * P, (t + 1) * P)
                            if lv:
                                l = rr = A(l_QK + m * T)
                            else:
                                l, rr = p2(GK + m), p2(GQ + m)
                            last = mm(o[:, c], l[r, c], rr[r, c])
                        close(last, ("attn", lv), 2 * m + e)
                pe.wait_ge(sem("sq_qk"), lv + 1)
                last = row_sums(sum_qk, lv, sq_qk)
                if lv < 7:
                    last.then_inc(sem("sq_qk_used"), 1)
                else:
                    close(last, "sum_qk")
            pe.wait_ge(sem("khat_ready"), 2)
            for m in range(2):
                o = open_("khat", m, 4 + m)
                for t in range(NT):
                    last = tr(o[:, t * P:(t + 1) * P], A(l_QK + m * T)[:, t * P:(t + 1) * P])
                close(last, "khat", m)
            for m in range(2):
                emptied(pe, "khat", m)
                o = open_("gla_state", m, 6 - m)
                for t in range(3):
                    for e in range(2):
                        last = mm(o[e * CH:(e + 1) * CH, t * P:(t + 1) * P],
                                  A(l_KT + m * T)[:, t * P + e * CH:t * P + (e + 1) * CH],
                                  A(l_VT, 2048)[:, t * T + (2 * m + e) * P:t * T + (2 * m + e + 1) * P])
                close(last, "gla_state", m)
            pe.wait_ge(sem("gla_states_ready"), 2)
            for hh in range(4):
                emptied(pe, ("attn", 7), hh)
                m, r = hh // 2, slice((hh % 2) * CH, (hh % 2 + 1) * CH)
                o = open_("gla_o", hh, hh)
                for t in range(NT):
                    c = slice(t * P, (t + 1) * P)
                    last = mm(o[:, c], A(l_VT, 2048)[:, t * T + hh * P:t * T + (hh + 1) * P],
                              A(l_AT + hh * T)[:, c], True, t == 0)
                    if t:
                        last = mm(o[:, c], A(l_ST + m * 384)[r, (t - 1) * P:t * P], A(l_E + m * T)[r, c], False, True)
                close(last, "gla_o", hh)

            def spread(what, i, rs):
                o = open_(what, i, 4 + i % 4)
                for t in range(NT):
                    col = rs[:, i * NT + t:i * NT + t + 1].to_broadcast([P, P])
                    last = mm(o[:, t * P:(t + 1) * P], col, C("ident"))
                close(last, what, i)

            o = open_("sum_gla", 0, 4)
            for i in range(4):
                pe.wait_ge(sem("sq_gla"), i + 1)
                last = row_sums(o, i, sq_gla[i])
            close(last, "sum_gla")
            pe.wait_ge(sem("row_rs_ready"), 1)
            for i in range(8):
                spread("qk_rs", i, row_rs[1])
            o = open_("iw", 0, 6)
            for t in range(NT):
                last = tr(o[:, t * P:(t + 1) * P], p2(MISC)[:, t * P:(t + 1) * P])
            close(last, "iw")
            pe.wait_ge(sem("row_rs_ready"), 2)
            for i in range(4):
                spread("gla_rs", i, row_rs[0])
            part_w = [None]

            def branch_part(n, i, banks):
                m, bank = i // 4 * 2 + i % 2, banks[i % 8]
                if i == 0:
                    for k in range(4):
                        pe.wait_ge(sem(f"y{n}_ready"), k + 1)
                if i % 4 < 2:
                    if i % 4 == 0:
                        part_w[0] = take(w_br[n])
                    o = open_(("branch", n), m, bank)
                    close(tile_of(part_w[0], 4, 256, i % 2 * P, ys[n], o, i % 4 == 0), ("branch", n), m)
                else:
                    o = open_(("gates", n), m, bank)
                    close(tile_of(take(w_br[n]), KT, P, 0, in2, o, True), ("gates", n), m)

            def branch(n):
                for i in range(16):
                    branch_part(n, i, (0, 1, 4, 5, 2, 3, 6, 7))

            for t in range(NT):
                o = open_("dsa_vt", t, t)
                for k in range(4):
                    last = tr(o[:, k * P:(k + 1) * P], p2(DV + k)[:, t * P:(t + 1) * P])
                close(last, "dsa_vt", t)
            for t in range(1, NT):
                n = (t + 1) * P
                for hh in range(4):
                    r = slice((hh % 2) * CH, (hh % 2 + 1) * CH)
                    close(mm(open_(("index", t), hh, 4 + hh)[:, 0:n], p2(IQ + hh // 2)[r, t * P:(t + 1) * P],
                             p2(IK)[r, 0:n]), ("index", t), hh)
            branch(0)
            pe.wait_ge(sem("bias0_loaded"), 16)
            emptied(pe, "qk_rs", 7)

            def logits(hh, t):
                n = (t + 1) * P
                if hh == 2 and t == 0:
                    pe.wait_ge(sem("bias1_loaded"), 16)
                o = open_(("logits", hh), t, 4 + t % 2)
                mm(o[:, 0:n], p2(DQ + hh)[:, t * P:(t + 1) * P], p2(DK + hh)[:, 0:n], True, False)
                close(mm(o[:, 0:n], C("flip"), A(d_HK[hh] + 384 - t * P, n), False, True), ("logits", hh), t)

            def attend(hh, t):
                i = 4 * hh + t
                pe.wait_ge(sem("probs_ready"), i + 1)
                o = open_("pt", i, 6)
                for j in range(t + 1):
                    last = tr(o[:, j * P:(j + 1) * P], A(d_LG + (i % 2) * T)[:, j * P:(j + 1) * P])
                close(last, "pt", i)

            def values(hh, t):
                i = 4 * hh + t
                emptied(pe, "pt", i)
                if t == 0:
                    open_("dsa_y", hh, 0)
                o = PSB[bank_of("dsa_y", hh)]
                for j in range(t + 1):
                    last = mm(o[:, t * P:(t + 1) * P], A(d_VT, 2048)[:, j * T + hh * P:j * T + (hh + 1) * P],
                              A(d_PT[i % 2])[:, j * P:(j + 1) * P], j == 0, j == t)
                if t == NT - 1:
                    close(last, "dsa_y", hh)

            pairs = [(hh, t) for hh in range(4) for t in range(NT)]
            logits(*pairs[0])
            logits(*pairs[1])
            for i, (hh, t) in enumerate(pairs):
                attend(hh, t)
                if i:
                    values(*pairs[i - 1])
                if i + 2 < len(pairs):
                    logits(*pairs[i + 2])
                branch_part(1, i, (1, 2, 3, 7) * 2)
            values(*pairs[-1])
            branch(2)
            project("mix2", 4, w_br[2], merged2, ready="merged_split")
            sums("sum_2", [A(SQ2 + k * T) for k in range(KT)], "sq_2")
            o = open_("route_t", 0, 5)
            pe.wait_ge(sem("route_split"), 2)
            for k in range(KT):
                c = slice(k * 20, k * 20 + P)
                pe.wait_ge(sem("h2_ready"), k + 1)
                mm(o, route_hi[:, c], in_ff.hi(k), k == 0, False)
                mm(o, route_lo[:, c], in_ff.hi(k), False, False)
                last = mm(o, route_hi[:, c], in_ff.lo(k), False, k == KT - 1)
            close(last, "route_t")
            emptied(pe, "route_t")
            o = open_("route", 0, 6)
            for t in range(NT):
                last = tr(o[:, t * 20:(t + 1) * 20], A(F_CB, T, 0, 20)[:, t * P:(t + 1) * P])
            close(last, "route")
            up("moe", "first", 0)
            pe.wait_ge(sem("combine_ready"), 1)
            o = open_("combine", 0, 6)
            for t in range(NT):
                last = tr(o[0:NE, t * P:(t + 1) * P], rt_c[:, t * NE:(t + 1) * NE])
            close(last, "combine")
            emptied(pe, "combine")
            for e in range(NE):
                close(mm(open_("weights", e, 4 + e % 4), C("sel16", NE, e * P, (e + 1) * P), A(F_CB, T, 0, NE)), "weights", e)
            gated("moe", NE)
            for t in range(NT):
                for i in range(2):
                    o = open_("out", 2 * t + i, 2 * (t % 2) + i)
                    for k in range(4):
                        pe.wait_ge(sem("out_ready"), 4 * i + k + 1)
                        last = tr(o[:, k * P:(k + 1) * P], res[:, 4 * i + k, t * P:(t + 1) * P])
                    close(last, "out", 2 * t + i)


        @block.scalar
        def _(act):
            n_rstd = [0]

            def f(o, i, func, **kw):
                return nc.scalar.activation(o, i, func, **kw)

            def rstd():
                n_rstd[0] += 1
                act.wait_ge(sem("variance_inverted"), n_rstd[0])
                f(v_rs, v_tmp, ACT.Sqrt).then_inc(sem("rstd_ready"), 1)

            n_x, n_hi = [0], [0]

            def squares_of_x(dst, name, term=None):
                for k in range(KT):
                    if term:
                        emptied(act, term, k)
                    else:
                        act.wait_ge(sem("x_updated"), n_x[0] + k + 1)
                    f(dst(k), res[:, k, :], ACT.Square).then_inc(sem(name), 1)
                n_x[0] += 0 if term else KT

            def round_hi(tiles, shift=None):
                for k in range(KT):
                    act.wait_ge(sem("scaled"), n_hi[0] + k + 1)
                    if shift is None:
                        f(tiles.hi(k), tiles.raw(k), ACT.Copy).then_inc(sem("hi_rounded"), 1)
                    else:
                        f(tiles.hi(k), tiles.raw(k), ACT.Identity, bias=shift(k)).then_inc(sem("hi_rounded"), 1)
                n_hi[0] += KT

            def evac(what, k, o, i=None, func=ACT.Copy, **kw):
                filled(act, what, k)
                f(o, PSB[bank_of(what, k)] if i is None else i, func, **kw).then_inc(freed(what, k), 1)

            act.dma_start(fix[:, 0:2 * P], fixed[:, 0:2 * P]).then_inc(sem("ident_loaded"), 16)
            act.dma_start(fix[:, S0:M0], fixed[:, S0:M0]).then_inc(sem("params_loaded"), 16)
            act.wait_ge(sem("x_loaded"), 16 * NT)
            act.dma_start(fix[:, 2 * P:S0], fixed[:, 2 * P:S0]).then_inc(sem("fixed_loaded"), 16)
            act.dma_start(fix[:, M0:N_FIX], fixed[:, M0:N_FIX]).then_inc(sem("fixed_loaded"), 16)
            for k in range(KT):
                evac("x", k, res[:, k, :])
            rstd()
            act.wait_ge(sem("params_loaded"), 16)
            round_hi(in1)
            f(csil[:, :], S("c", 0, KT), ACT.Silu).then_inc(sem("csil_ready"), 1)
            act.wait_ge(sem("pads_zeroed"), 1)
            for t in range(N_PROJ):
                evac("proj", t, proj(t))
                if 10 <= t < 18:
                    act.wait_ge(sem("conv_ready"), t - 9)
                    f(proj(XS + t - 10), proj(XS + t - 10), ACT.Silu).then_inc(sem("xbc_ready"), 1)
                if t == 18:
                    f(expA[:, :], S("a_log"), ACT.Exp).then_inc(sem("exp_a_ready"), 1)
                    act.wait_ge(sem("dt_abs_ready"), 1)
                    f(ym(4, 0, 8), ym(3, 0, 8), ACT.Exp, scale=-1.0).then_inc(sem("dt_exp_ready"), 1)
                if t == 20:
                    act.wait_ge(sem("to_end_ready"), 1)
                    f(ym(3, 0, 8), ym(3, 0, 8), ACT.Exp).then_inc(sem("to_end_exp_ready"), 1)
            act.wait_ge(sem("mixed"), 2)
            f(A(TW, T, 0, CH), proj(WA, 0, CH), ACT.Tanh).then_inc(sem("tanh_ready"), 1)
            f(proj(GL), proj(GL), ACT.Sigmoid).then_inc(sem("sigmoid_ready"), 1)
            for i in range(2):
                evac("b_tm", i, A(s_BT + i * T))
            evac("chunk_decay", 0, c_last[:, :], PSB[bank_of("chunk_decay")][:, 0:32], ACT.Exp)

            def prepare(m, step):
                if step == 1:
                    evac("a_low", m, pr_B, None, ACT.Sigmoid, bias=S("a0", m))
                if step == 2:
                    if m:
                        filled(act, f"sum_bonus{m - 1}")
                    evac("w_low", m, pr_W, None, ACT.Sigmoid, bias=S("w0", m))
                if step == 3:
                    emptied(act, "w_low", m)
                    f(pr_W, pr_W, ACT.Exp, scale=-EXP_HALF).then_inc(sem("w_ready"), 1)
                if step == 4:
                    rstd()

            def decay_row(h):
                filled(act, "cs_row", h)
                f(xn[:, h, :], PSB[bank_of("cs_row", h)], ACT.Exp).then_inc(sem("row_decay_ready"), 1)

            for h in range(8):
                decay_row(h)
                emptied(act, "cs_row", h)
                f(A(s_HB + (h % 2) * T), A(s_HB + (h % 2) * T), ACT.Exp).then_inc(sem("pair_decay_ready"), 1)
                if 2 <= h < 6:
                    prepare(0, h - 1)
            for m in range(4):
                f(proj(ZZ + m), proj(ZZ + m), ACT.Silu).then_inc(sem("z_ready"), 1)
            for g in range(2):
                rstd()
            act.wait_ge(sem("ssd_out_ready"), 4)
            act.wait_ge(sem("sigmoid_ready"), 1)
            f(A(SG), proj(GL), ACT.Copy).then_inc(sem("sg_ready"), 1)

            for m in range(4):
                evac("last_decay", m, pls[:, :], PSB[bank_of("last_decay", m)][0:CH, 0:2 * NC])
                for i, t in enumerate((t_A, t_BP, t_KP, t_V)):
                    evac(("tm", m), i, tm(t), four(PSB[bank_of(("tm", m), i)]))
                for lv in range(1, 6):
                    for e in range(2):
                        evac((f"U{lv}", m), e, h_buf[e][m_U])
                    if m < 3:
                        prepare(m + 1, lv)
                for e in range(2):
                    if e == 0:
                        filled(act, ("ZU5", m), 1)
                        emptied(act, ("tm", m), 0)
                    r = slice(e * CH, (e + 1) * CH)
                    f(four(h_buf[e][m_U])[:, :, 0:CH], tm(t_A)[:, :, r], ACT.Copy)
                for e in range(2):
                    evac(("wv", m), e, four(h_buf[e][m_U])[:, :, CH:P],
                         PSB[bank_of(("wv", m), e)][:, 0:256].rearrange("p (a b) -> p a b", a=4))
                for e in range(2):
                    evac(("aw", m), e, h_buf[e][m_AW])
                for e in range(2):
                    h = 2 * m + e
                    for i in range(2):
                        evac(("hh", m), 2 * e + i, h_all[:, i::2, h, :],
                             PSB[bank_of(("hh", m), 2 * e + i)][0:CH, 0:256].rearrange("p (c i) -> p c i", c=NT))
            for m in range(4):
                evac("rwkv_y", m, ew(m))
            for m in range(4):
                emptied(act, f"sum_y{m}")
                f(proj(VV + m), ew(m), ACT.Square).then_inc(sem("sq_y"), 1)
            act.wait_ge(sem("head_inverted"), 1)
            f(head_rs, head_rs, ACT.Sqrt).then_inc(sem("head_rs_ready"), 1)


            for k in range(KT):
                evac("mix", k, xn[:, k, :])
            rstd()
            squares_of_x(lambda k: A(SQ1 + k * T), "sq_pre_ffn")
            rstd()
            round_hi(in_ff)

            def silu_gates(j, phase, sub, it=None):
                for i in range(4):
                    k = (phase, sub, i)
                    if j != 0:
                        act.wait_ge(sem("ffn_taps_used"), at(j, 4, i - 3))
                    filled(act, "ffn_up", k, it)
                    f(A(F_UB + i * PADW + 3), PSB[i], ACT.Copy).then_inc(freed("ffn_up", k), 1)
                for i in range(2):
                    act.wait_ge(sem("ffn_taps_used"), at(j, 4, i + 1))
                    f(A(F_CB + i * T), A(F_CB + i * T), ACT.Silu).then_inc(sem("ffn_silu_ready"), 1)

            act.wait_ge(sem("ffn_zeroed"), 1)
            silu_gates(0, "first", 0)
            with act.Fori(0, (NF - 1) // 2) as it:
                silu_gates((it, 1), "loop", 1, it)
                silu_gates((it, 2), "loop", 0, it)
            for k in range(KT):
                emptied(act, "ffn_down", ("last", 0, k))
                f(A(F_CMB + k * T), A(F_ACC + k * T), ACT.Square).then_inc(sem("sq_post_ffn"), 1)
            rstd()
            squares_of_x(lambda k: A(F_CMB + k * T), "sq_1")
            rstd()
            emptied(act, "mod")
            round_hi(in2, lambda k: mod[:, k:k + 1])
            for i in range(2):
                evac("bias_row", i, A(d_BR + i * T, T, 0, 4), PSB[bank_of("bias_row", i)][0:4, :])
            emptied(act, "bias_row", 0)
            emptied(act, "bias_row", 1)
            act.dma_start(skew, A(d_BR, 2 * T, 0, 4)).then_inc(sem("bias_stored"), 16)
            for t in range(8):
                evac("p2", t, p2(t), None, ACT.Gelu_apprx_tanh)
            for t in range(8, 18):
                evac("p2", t, p2(t), None, ACT.Silu if GR <= t < GR + 4 else ACT.Copy)
            rstd()
            for t in range(18, 22):
                evac("p2", t, p2(t), None, ACT.Silu if GR <= t < GR + 4 else ACT.Copy)
            for t in range(NT):
                evac("gmlp_vt", t, A(g_VT + t * T))
            for m in range(2):
                act.wait_ge(sem("forget_abs"), m + 1)
                f(A(l_E + m * T), A(l_E + m * T), ACT.Exp).then_inc(sem("forget_exp"), 1)
            act.wait_ge(sem("bias_stored"), 16)
            for t in range(22, 36):
                evac("p2", t, p2(t))
            filled(act, "gla_vt", 3)
            for t in range(NT):
                evac("gla_vt", t, A(l_VT + t * T))
            f(sq_qk, p2(DQ), ACT.Square).then_inc(sem("sq_qk"), 1)
            for lv in range(1, 8):
                for m in range(2):
                    act.wait_ge(sem("log_decay_ready"), 2 * (lv - 1) + m + 1)
                    f(A(l_E + m * T), A(l_E + m * T), ACT.Exp).then_inc(sem("decay_ready"), 1)
                act.wait_ge(sem("sq_qk_used"), lv)
                f(sq_qk, p2(DQ + lv), ACT.Square).then_inc(sem("sq_qk"), 1)
            for m in range(2):
                act.wait_ge(sem("log_decay_ready"), 14 + m + 1)
                f(A(l_QK + m * T), A(l_QK + m * T), ACT.Exp).then_inc(sem("decay_ready"), 1)
                f(A(l_E + m * T), A(l_B + m * T), ACT.Exp).then_inc(sem("decay_ready"), 1)
            for m in range(2):
                evac("khat", m, A(l_KT + m * T))
            act.wait_ge(sem("row_inverted"), 1)
            f(row_rs[1], row_rs[1], ACT.Sqrt).then_inc(sem("row_rs_ready"), 1)
            for hh in range(4):
                filled(act, "gla_o", hh)
                f(sq_gla[hh], PSB[bank_of("gla_o", hh)], ACT.Square).then_inc(sem("sq_gla"), 1)
                evac("gla_o", hh, p2(GQ + hh))
            act.wait_ge(sem("row_inverted"), 2)
            f(row_rs[0], row_rs[0], ACT.Sqrt).then_inc(sem("row_rs_ready"), 1)
            filled(act, "iw")
            f(iw.rearrange("p (t h) -> p t h", t=NT),
              PSB[bank_of("iw")].rearrange("p (t c) -> p t c", t=NT)[:, :, 32:36], ACT.Copy).then_inc(freed("iw"), 1)
            filled(act, "dsa_vt", 3)
            for t in range(NT):
                evac("dsa_vt", t, A(d_VT + t * T))
            for t in range(1, NT):
                n = (t + 1) * P
                for hh in range(4):
                    i = 4 * (t - 1) + hh
                    if i >= 2:
                        act.wait_ge(sem("relu_used"), i - 1)
                    evac(("index", t), hh, A(d_RL[i % 2], n), PSB[4 + hh][:, 0:n], ACT.Relu)

            def gate(n, m):
                b = len(sig[n])
                if m >= b:
                    if n == 0:
                        emptied(act, ("branch", 0), m - b)
                    else:
                        act.wait_ge(sem("merged"), (n - 1) * KT + m - b + 1)
                if n == 0 and m == 3:
                    act.wait_ge(sem("relu_used"), 12)
                evac(("gates", n), m, sig[n][m % b], None, ACT.Sigmoid, bias=S("b_branch", n * KT + m))

            for m in range(KT):
                gate(0, m)
            filled(act, ("gates", 0), KT - 1)
            for i in range(2):
                if i:
                    emptied(act, ("branch", 0), KT - 1)
                hankel = bass.AP(tensor=skew.tensor, offset=skew.offset + 4 * T * i, ap=[[1, P], [2 * T, 2], [1, 896]])
                act.dma_start(A(d_HK[2 * i], 2 * 896).rearrange("p (h n) -> p h n", h=2), hankel)\
                    .then_inc(sem(f"bias{i}_loaded"), 16)
            for i in range(16):
                t = i % 4
                n = (t + 1) * P
                act.wait_ge(sem("logits_ready"), i + 1)
                p_ = A(d_LG + (i % 2) * T, n)
                f(p_, p_, ACT.Exp, bias=nmax[:, i % 4:i % 4 + 1], accum_out=rsum[:, i % 4:i % 4 + 1])\
                    .then_inc(sem("exp_ready"), 1)
                evac("pt", i, A(d_PT[i % 2], n), PSB[bank_of("pt", i)][:, 0:n])
                if t == 0 and i:
                    evac("dsa_y", i // 4 - 1, p2(DQ + i // 4 - 1))
                if t == 3:
                    gate(1, i // 4 * 2)
                elif t == 0 and i:
                    gate(1, i // 4 * 2 - 1)
            gate(1, KT - 1)
            evac("dsa_y", 3, p2(DQ + 3))
            for m in range(KT):
                gate(2, m)
            squares_of_x(lambda k: A(SQ2 + k * T), "sq_2", "mix2")
            rstd()
            round_hi(in_ff, lambda k: mod[:, 24 + k:25 + k])
            evac("route_t", 0, A(F_CB, T, 0, 20), PSB[bank_of("route_t")][0:20, :])
            act.wait_ge(sem("route_diff"), 1)
            f(rt_w[0], rt_w[0], ACT.Exp).then_inc(sem("route_exp"), 1)
            act.wait_ge(sem("route_diff"), 2)
            f(rt_s[4], rt_s[4], ACT.Exp).then_inc(sem("route_exp"), 1)
            evac("combine", 0, A(F_CB, T, 0, NE), PSB[bank_of("combine")][0:NE, :])
            for e in range(NE):
                evac("weights", e, A(F_CMB + e * T))

            def silu_experts(j, phase, sub, it=None):
                for i in range(2):
                    k = (phase, sub, i)
                    if j != 0:
                        act.wait_ge(sem("moe_act_ready"), at(j, 2, i - 1))
                    filled(act, "moe_up", k, it)
                    f(A(F_UB + i * T), PSB[i], ACT.Silu).then_inc(freed("moe_up", k), 1)

            silu_experts(0, "first", 0)
            with act.Fori(0, (NE - 1) // 2) as it:
                silu_experts((it, 1), "loop", 1, it)
                silu_experts((it, 2), "loop", 0, it)
            silu_experts(NE - 1, "last", 1)
            for i in range(8):
                evac("out", i, A(OUT + i * T))


        @block.vector
        def _(dve):
            ch = Chain(dve, "vector_step")
            link = ch.link
            V = nc.vector
            n_rstd = [0]

            def tt(o, a, b, op):
                return V.tensor_tensor(o, a, b, op)

            def ts(o, a, s1, s2=None, op0=ALU.mult, op1=None):
                return V.tensor_scalar(o, a, s1, s2, op0) if op1 is None else V.tensor_scalar(o, a, s1, s2, op0, op1)

            def stt(o, a, s1, b, op0, op1):
                return V.scalar_tensor_tensor(o, a, s1, b, op0, op1)

            def invert_variance(what, scale, add, op1=ALU.add, k=0):
                n_rstd[0] += 1
                filled(dve, what, k)
                V.tensor_scalar(v_tmp, PSB[bank_of(what, k)], scale, add, ALU.mult, op1).then_inc(freed(what, k), 1)
                emptied(dve, what, k)
                V.reciprocal(v_tmp, v_tmp).then_inc(sem("variance_inverted"), 1)

            def rstd(what, scale, add, op1=ALU.add, k=0):
                invert_variance(what, scale, add, op1, k)
                dve.wait_ge(sem("rstd_ready"), n_rstd[0])

            n_hi = [0]

            def scaled_parts(tiles, gain, ready, shift=None):
                for k in range(KT + 2):
                    if k < KT:
                        stt(tiles.raw(k), res[:, k, :], gain(k), v_rs, ALU.mult, ALU.mult).then_inc(sem("scaled"), 1)
                    if k >= 2:
                        j = k - 2
                        dve.wait_ge(sem("hi_rounded"), n_hi[0] + j + 1)
                        raw, hi = tiles.raw(j), tiles.hi(j).bitcast(F32)
                        if shift is None:
                            tt(tiles.lo(j), raw, hi, ALU.subtract).then_inc(sem(ready), 1)
                        else:
                            stt(tiles.lo(j), raw, shift(j), hi, ALU.add, ALU.subtract).then_inc(sem(ready), 1)
                n_hi[0] += KT

            def split(tiles, k, ready):
                link(V.tensor_copy(tiles.hi(k), tiles.raw(k)))
                tt(tiles.lo(k), tiles.raw(k), tiles.hi(k).bitcast(F32), ALU.subtract).then_inc(sem(ready), 1)

            def log1p(o, u, t1, t2):
                link(ts(t1, u, 2.0, None, ALU.add))
                link(V.reciprocal(t1, t1))
                link(tt(t1, t1, u, ALU.mult))
                link(tt(t2, t1, t1, ALU.mult))
                link(ts(o, t2, 1.0 / (2 * LOG1P_TERMS + 1)))
                for i in range(LOG1P_TERMS - 1, 0, -1):
                    link(stt(o, o, 1.0 / (2 * i + 1), t2, ALU.add, ALU.mult))
                link(stt(o, o, 1.0, t1, ALU.add, ALU.mult))

            for k in range(KT):
                emptied(dve, "x", k)
                tt(A(SQ + k * T), res[:, k, :], res[:, k, :], ALU.mult).then_inc(sem("sq_pre_mix"), 1)
            pv = A(PROJ, N_PROJ * PADW).rearrange("p (t c) -> p t c", c=PADW)
            V.memset(pv[:, :, 0:3], 0.0).then_inc(sem("pads_zeroed"), 1)
            dve.wait_ge(sem("params_loaded"), 16)
            rstd("sum_pre_mix", 1.0 / D, 1e-6)
            scaled_parts(in1, lambda k: S("g_pre_mix", k), "xn_ready")

            dve.wait_ge(sem("fixed_loaded"), 32)
            for t in range(8):
                emptied(dve, "proj", t)
                buf = A(CONV + (t % 2) * T)
                link(ts(buf, proj(t), S("conv_w", 3 * 8 + t), S("conv_b", t), ALU.mult, ALU.add))
                link(stt(buf, proj(t, shift=1), S("conv_w", 2 * 8 + t), buf, ALU.mult, ALU.add))
                link(stt(buf, proj(t, shift=2), S("conv_w", 1 * 8 + t), buf, ALU.mult, ALU.add))
                link(stt(buf, proj(t, shift=3), S("conv_w", t), buf, ALU.mult, ALU.add))
                V.tensor_copy(proj(t), buf).then_inc(sem("conv_ready"), 1)
            dt, cs, de, t3, t4, t5, t6, t7 = [ym(i, 0, 8) for i in range(8)]
            emptied(dve, "proj", DT)
            link(ts(dt, proj(DT, 0, 8), S("dt_bias", rows=8), None, ALU.add))
            link(ts(t3, dt, -1.0))
            tt(t3, t3, dt, ALU.max).then_inc(sem("dt_abs_ready"), 1)
            for i, t in enumerate([WA, GL] + list(range(RR, RR + 12))):
                emptied(dve, "proj", t)
                buf = A(CONV + 2 * T + (i % 2) * T)
                link(tt(buf, proj(t, shift=1), proj(t), ALU.subtract))
                stt(proj(t), buf, S("mu", i), proj(t), ALU.mult, ALU.add).then_inc(sem("mixed"), 1)
                if i == 5:
                    dve.wait_ge(sem("dt_exp_ready"), 1)
                    log1p(t5, t4, t6, t7)
                    link(ts(dt, dt, 0.0, None, ALU.max))
                    link(stt(dt, t5, 2.0, dt, ALU.mult, ALU.add))
                    link(ts(t6, dt, expA[0:8, :], -1.0, ALU.mult, ALU.mult))
                    link(V.tensor_tensor_scan(cs, C("carry128", 8), t6, 0.0, ALU.mult, ALU.add))
                    last = four(cs)[:, :, P - 1:P].to_broadcast([8, NT, P])
                    tt(four(t3), last, four(cs), ALU.subtract).then_inc(sem("to_end_ready"), 1)
                if i == 8:
                    dve.wait_ge(sem("to_end_exp_ready"), 1)
                    tt(de, t3, dt, ALU.mult).then_inc(sem("dt_ready"), 1)
            filled(dve, "dec3")
            V.tensor_copy(dec3[:, :], PSB[bank_of("dec3")][:, 0:96]).then_inc(freed("dec3"), 1)
            emptied(dve, "dec3")
            d3 = dec3[:, :].rearrange("p (i t h) -> p i t h", i=3, t=NT)

            def per_head(i, t):
                return d3[:, i, t, :].unsqueeze(2).to_broadcast([P, 8, CH])

            for t in range(NT):
                filled(dve, "xs_tm", t)
                src = PSB[bank_of("xs_tm", t)].rearrange("p (h c) -> p h c", h=8)
                tt(A(s_XS2 + t * T).rearrange("p (h c) -> p h c", h=8), src, per_head(2, t), ALU.mult)\
                    .then_inc(sem("xs2_ready"), 1)
                tt(A(s_XD + t * T).rearrange("p (h c) -> p h c", h=8), src, per_head(0, t), ALU.mult)\
                    .then_inc(freed("xs_tm", t), 1)
            for g in range(2):
                filled(dve, "scores", g)
                tt(four(A(s_GT + g * T)), four(PSB[bank_of("scores", g)]), rep4(C("incl128")), ALU.mult)\
                    .then_inc(freed("scores", g), 1)
            emptied(dve, "chunk_decay")
            cl = c_last[:, :].rearrange("p (h t) -> p h t", h=8)
            for t in range(3):
                filled(dve, "state", t)
                o = A(s_SI + t * T)
                if t == 0:
                    V.tensor_copy(o, PSB[bank_of("state", t)]).then_inc(freed("state", t), 1)
                else:
                    v8 = lambda a: a.rearrange("p (h c) -> p h c", h=8)
                    emptied(dve, "state", t - 1)
                    link(tt(v8(o), v8(A(s_SI + (t - 1) * T)), cl[:, :, t:t + 1].to_broadcast([P, 8, CH]), ALU.mult))
                    tt(o, o, PSB[bank_of("state", t)], ALU.add).then_inc(freed("state", t), 1)
            emptied(dve, "state", 2)

            def head_free(h):
                if h % 2 == 0:
                    dve.wait_ge(sem("ssd_head_used"), h // 2 + 1)
                else:
                    filled(dve, "ssd_y", h // 2)

            def log_decays(h):
                dve.wait_ge(sem("row_decay_ready"), h + 1)
                if h >= 2:
                    head_free(h - 2)
                row = PSB[bank_of("cs_row", h)]
                for t in range(NT):
                    c = slice(t * P, (t + 1) * P)
                    last = ts(A(s_HB + (h % 2) * T)[:, c], row[:, c], d3[:, 1, t, h:h + 1], 0.0, ALU.subtract, ALU.min)
                last.then_inc(freed("cs_row", h), 1)

            link(ts(one_ka[:, :], S("k_a", 0, 4), -1.0, 1.0, ALU.mult, ALU.add))

            def prepare(m, step):
                kt, rt, vt = proj(KK_ + m), proj(RR + m), proj(VV + m)
                if step == 1:
                    if m:
                        filled(dve, ("tm", m - 1), 3)
                    link(ts(pr_KK, kt, S("k_k", m)))
                    tt(pr_P, pr_KK, pr_KK, ALU.mult).then_inc(sem("sq_kk"), 1)
                if step == 2:
                    emptied(dve, "a_low", m)
                    link(ts(pr_INV, pr_B, S("k_a", m), one_ka[:, m:m + 1], ALU.mult, ALU.add))
                    link(tt(kt, kt, pr_INV, ALU.mult))
                    stt(pr_INV, rt, S("r_k", m), kt, ALU.mult, ALU.mult).then_inc(sem("bonus_in"), 1)
                if step == 3:
                    invert_variance(f"sum_kk{m}", 1.0, 1e-24, ALU.max)
                if step == 4:
                    dve.wait_ge(sem("rstd_ready"), n_rstd[0])
                    link(tt(pr_KK, pr_KK, v_rs, ALU.mult))
                    link(tt(pr_B, pr_B, pr_KK, ALU.mult))
                    filled(dve, f"sum_bonus{m}")
                    tt(ym(4 + m), vt, PSB[bank_of(f"sum_bonus{m}")], ALU.mult).then_inc(freed(f"sum_bonus{m}"), 1)
                if step == 5:
                    dve.wait_ge(sem("w_ready"), m + 1)
                    link(tt(pr_INV, pr_W, C("carry64"), ALU.mult))
                    link(tt(pr_W, pr_W, pr_INV, ALU.subtract))
                    link(V.tensor_tensor_scan(pr_P, pr_INV, pr_W, 0.0, ALU.mult, ALU.add))
                if step == 6:
                    link(V.reciprocal(pr_INV, pr_P))
                    link(tt(rt, rt, pr_P, ALU.mult))

            log_decays(0)
            for h in range(8):
                if h + 1 < 8:
                    log_decays(h + 1)
                dve.wait_ge(sem("pair_decay_ready"), h + 1)
                tt(A(s_CE + (h % 2) * T), proj(CM + h // 4), xn[:, h, :], ALU.mult)
                tt(A(s_HB + (h % 2) * T), A(s_HB + (h % 2) * T), A(s_GT + (h // 4) * T), ALU.mult)\
                    .then_inc(sem("mt_ready"), 1)
                if h >= 2:
                    prepare(0, h - 1)
            filled(dve, "ssd_y", 3)
            for m in range(4):
                dve.wait_ge(sem("z_ready"), m + 1)
                t = A(s_HB + m * T)
                stt(t, proj(XS + m), S("d_skip", m), PSB[bank_of("ssd_y", m)], ALU.mult, ALU.add)\
                    .then_inc(freed("ssd_y", m), 1)
                emptied(dve, "ssd_y", m)
                link(tt(t, t, proj(ZZ + m), ALU.mult))
                tt(A(s_XD + m * T), t, t, ALU.mult).then_inc(sem("sq_ssd"), 1)
            for g in range(2):
                rstd(f"sum_ssd{g}", 1.0 / 256, 1e-6)
                for i in range(2):
                    m = 2 * g + i
                    stt(ym(m), A(s_HB + m * T), S("ssd_norm", m), v_rs, ALU.mult, ALU.mult)\
                        .then_inc(sem("ssd_out_ready"), 1)

            c8 = lambda a: a.rearrange("p (c t) -> p c t", c=NC)
            for m in range(4):
                kt, pt = proj(KK_ + m), pr_P
                if m:
                    filled(dve, ("hh", m - 1), 3)
                link(stt(ew(e_AT)[:, 1:T], pr_KK[:, 1:T], -1.0, pt[:, 0:T - 1], ALU.mult, ALU.mult))
                link(ts(ew(e_AT)[:, 0:T:CH], pr_KK[:, 0:T:CH], -1.0))
                link(tt(ew(e_BH), pr_B, pr_INV, ALU.mult))
                link(tt(ew(e_KH), kt, pr_INV, ALU.mult))
                last = pt[:, CH - 1::CH].unsqueeze(2).to_broadcast([P, NC, CH])
                link(tt(c8(ew(e_BP)), c8(ew(e_BH)), last, ALU.mult))
                tt(c8(ew(e_KP)), c8(ew(e_KH)), last, ALU.mult).then_inc(sem("pair_ready"), 1)
                for e in range(2):
                    hb = h_buf[e]
                    filled(dve, ("abT", m), e)
                    if e == 0:
                        filled(dve, ("tm", m), 3)
                    tt(four(hb[m_AT]), four(PSB[bank_of(("abT", m), e)]), rep4(C("strict64")), ALU.mult)\
                        .then_inc(freed(("abT", m), e), 1)
                    emptied(dve, ("abT", m), e)
                    link(tt(four(hb[m_Z]), four(hb[m_AT]), rep4(C("level0")), ALU.mult))
                    link(tt(four(hb[m_Z]), four(hb[m_Z]), rep4(C("ident")), ALU.add))
                    filled(dve, ("ab", m), e)
                    tt(four(hb[m_X]), four(PSB[bank_of(("ab", m), e)]), rep4(C("level0t")), ALU.mult)\
                        .then_inc(freed(("ab", m), e), 1)
                    emptied(dve, ("ab", m), e)
                    link(tt(four(hb[m_X]), four(hb[m_X]), rep4(C("ident")), ALU.add))
                    tt(four(hb[m_LV]), four(hb[m_AT]), rep4(C("level1")), ALU.mult).then_inc(sem(f"level{e}_ready"), 1)
                for lv in range(1, 6):
                    for e in range(2):
                        hb = h_buf[e]
                        if lv < 5:
                            filled(dve, (f"U{lv}", m), e)
                            tt(four(hb[m_LV]), four(hb[m_AT]), rep4(C(f"level{lv + 1}")), ALU.mult)
                        filled(dve, (f"ZU{lv}", m), e)
                        if lv < 5:
                            filled(dve, (f"XU{lv}", m), e)
                        tt(hb[m_Z], hb[m_Z], PSB[bank_of((f"ZU{lv}", m), e)], ALU.add).then_inc(freed((f"ZU{lv}", m), e), 1)
                        if lv < 5:
                            tt(hb[m_X], hb[m_X], PSB[bank_of((f"XU{lv}", m), e)], ALU.add)\
                                .then_inc(freed((f"XU{lv}", m), e), 1)
                    if m < 3:
                        prepare(m + 1, lv)
                for e in range(2):
                    hb = h_buf[e]
                    for what, dst, mask in (("akT", m_X, "strict64"), ("rbT", m_AT, "incl64"), ("rkT", m_LV, "incl64")):
                        filled(dve, (what, m), e)
                        tt(four(hb[dst]), four(PSB[bank_of((what, m), e)]), rep4(C(mask)), ALU.mult)\
                            .then_inc(freed((what, m), e), 1)
                if m < 3:
                    prepare(m + 1, 6)
                filled(dve, ("ry", m), 1)
                for e in range(2):
                    V.tensor_copy(proj((RR, KK_)[e] + m), PSB[bank_of(("ry", m), e)]).then_inc(freed(("ry", m), e), 1)
                for e in range(2):
                    h = 2 * m + e
                    emptied(dve, "last_decay", m)
                    o = gt_all[:, :, h, :]
                    link(tt(o, C("ident", CH, 0, CH).unsqueeze(1).to_broadcast([CH, NC, CH]),
                            pls[:, e * NC:(e + 1) * NC].unsqueeze(2).to_broadcast([CH, NC, CH]), ALU.mult))
                    for i in range(2):
                        filled(dve, ("gt", m), 2 * e + i)
                        tt(o[:, i::2, :], o[:, i::2, :],
                           PSB[bank_of(("gt", m), 2 * e + i)][0:CH, 0:256].rearrange("p (c i) -> p c i", c=NT), ALU.add)\
                            .then_inc(freed(("gt", m), 2 * e + i), 1)
            for i in range(4):
                emptied(dve, ("hh", 3), i)
            for k in range(4):
                split(y1, k, "y_ready")
            for cn in range(1, NC - 1):
                filled(dve, ("s", cn))
                o = h_all[:, cn, :, :]
                tt(o, o, PSB[bank_of(("s", cn))][0:CH, :].rearrange("p (h i) -> p h i", h=8), ALU.add)\
                    .then_inc(freed(("s", cn)), 1)
            filled(dve, "mod")
            tt(mod[:, :], PSB[7][:, 0:48], S("b_mod", 0, 48), ALU.add).then_inc(freed("mod"), 1)
            for m in range(4):
                emptied(dve, "rwkv_y", m)
                filled(dve, f"sum_y{m}")
                stt(ew(m), PSB[bank_of(f"sum_y{m}")], -1.0 / CH, ew(m), ALU.mult, ALU.add).then_inc(freed(f"sum_y{m}"), 1)
            filled(dve, "head_squares")
            ts(head_rs, PSB[bank_of("head_squares")][:, 0:32], 1.0 / CH, 64e-5, ALU.mult, ALU.add).then_inc(freed("head_squares"), 1)
            emptied(dve, "head_squares")
            V.reciprocal(head_rs, head_rs).then_inc(sem("head_inverted"), 1)
            for m in range(4):
                y = ew(m)
                filled(dve, "y_rs", m)
                stt(y, y, S("ln_w", m), PSB[bank_of("y_rs", m)], ALU.mult, ALU.mult).then_inc(freed("y_rs", m), 1)
                emptied(dve, "y_rs", m)
                emptied(dve, f"sum_bonus{m}")
                link(stt(y, y, S("ln_b", m), ym(4 + m), ALU.add, ALU.add))
                filled(dve, "gate", m)
                tt(ym(4 + m), y, PSB[bank_of("gate", m)], ALU.mult).then_inc(freed("gate", m), 1)
                emptied(dve, "gate", m)
                split(y1, 4 + m, "y_ready")

            x_ = lambda k: res[:, k, :]
            n_ = lambda k: xn[:, k, :]
            sq = lambda k: A(SQ1 + k * T)

            n_add = [0]

            def add_normed(src, gain):
                for k in range(KT + 1):
                    if k < KT:
                        stt(src(k), src(k), S(gain, k), v_rs, ALU.mult, ALU.mult).then_inc(sem("term_ready"), 1)
                    if k:
                        dve.wait_ge(sem("term_ready"), n_add[0] + k)
                        tt(x_(k - 1), x_(k - 1), src(k - 1), ALU.add).then_inc(sem("x_updated"), 1)
                n_add[0] += KT

            for k in range(KT):
                emptied(dve, "mix", k)
                tt(sq(k), n_(k), n_(k), ALU.mult).then_inc(sem("sq_post_mix"), 1)
            rstd("sum_post_mix", 1.0 / D, 1e-6)
            add_normed(n_, "g_post_mix")
            V.memset(A(F_UB, 4 * PADW).rearrange("p (t c) -> p t c", t=4)[:, :, 0:3], 0.0).then_inc(sem("ffn_zeroed"), 1)
            link(V.memset(A(F_ACC, 4096), 0.0))
            rstd("sum_pre_ffn", 1.0 / D, 1e-6)
            scaled_parts(in_ff, lambda k: S("g_pre_ffn", k), "ffn_in_ready")

            def conv_gate(j, phase, sub, it=None):
                fc0 = at(j, 16, S0 + SMALL["ffn_conv"][0])

                def tap(i, k):
                    return fix[:, bass.ds(fc0 + (4 * i + k), 1)] if it is not None else \
                        fix[:, fc0 + 4 * i + k:fc0 + 4 * i + k + 1]

                if j != 0:
                    dve.wait_ge(sem("ffn_act_ready"), at(j, 2, 0))
                for i in range(4):
                    emptied(dve, "ffn_up", (phase, sub, i), it)
                    u, c = lambda s_: A(F_UB + i * PADW + 3 - s_), A(F_CB + i * T)
                    link(ts(c, u(0), tap(i, 2), tap(i, 3), ALU.mult, ALU.add))
                    link(stt(c, u(1), tap(i, 1), c, ALU.mult, ALU.add))
                    stt(c, u(2), tap(i, 0), c, ALU.mult, ALU.add).then_inc(sem("ffn_taps_used"), 1)

            def finish_gate(j, sub):
                for i in range(2):
                    dve.wait_ge(sem("ffn_silu_ready"), at(j, 2, i + 1))
                    if i == 0:
                        dve.wait_ge(sem("ffn_taps_used"), at(j, 4, 4))
                    link(tt(acts.raw(2 * sub + i), A(F_CB + i * T), A(F_CB + (2 + i) * T), ALU.mult))
                    split(acts, 2 * sub + i, "ffn_act_ready")

            def accumulate(kind, phase, sub, it=None):
                for m in range(KT):
                    k = (phase, sub, m)
                    filled(dve, kind + "_down", k, it)
                    o = A(F_ACC + m * T)
                    tt(o, o, PSB[4 + m % 4], ALU.add).then_inc(freed(kind + "_down", k), 1)

            conv_gate(0, "first", 0)
            finish_gate(0, 0)
            times = (NF - 1) // 2
            with dve.Fori(0, times) as it:
                ch.enter(it, 24)
                conv_gate((it, 1), "loop", 1, it)
                accumulate("ffn", "loop", 0, it)
                finish_gate((it, 1), 1)
                conv_gate((it, 2), "loop", 0, it)
                accumulate("ffn", "loop", 1, it)
                finish_gate((it, 2), 0)
            ch.leave(times)
            accumulate("ffn", "last", 0)
            emptied(dve, "ffn_down", ("last", 0, 6))
            emptied(dve, "ffn_down", ("last", 0, 7))
            acc = lambda k: A(F_ACC + k * T)
            rstd("sum_post_ffn", 1.0 / D, 1e-6)
            add_normed(acc, "g_post_ffn")

            def modulated(tiles, scale_at, shift_at, gain, name):
                link(stt(gmod[:, :], mod[:, scale_at:scale_at + KT], 1.0, S(gain, 0, KT), ALU.add, ALU.mult))
                scaled_parts(tiles, lambda k: gmod[:, k:k + 1], name, lambda k: mod[:, shift_at + k:shift_at + k + 1])

            rstd("sum_1", 1.0 / D, 1e-6)
            modulated(in2, 8, 0, "g1", "h_ready")
            filled(dve, "w_s")
            tt(four(A(g_WS)), four(PSB[bank_of("w_s")]), rep4(C("incl128")), ALU.mult).then_inc(freed("w_s"), 1)
            filled(dve, "gmlp_mean")
            for k in range(4):
                v = p2(AV + k)
                last = stt(v, PSB[bank_of("gmlp_mean")], -1.0 / T, v, ALU.mult, ALU.add)
                if k == 3:
                    last.then_inc(freed("gmlp_mean"), 1)
            emptied(dve, "gmlp_mean")
            for k in range(4):
                tt(A(g_SQ + k * T), p2(AV + k), p2(AV + k), ALU.mult).then_inc(sem("sq_gmlp"), 1)
            rstd("gmlp_var", 1.0 / T, 1e-6)
            for k in range(4):
                v = p2(AV + k)
                link(stt(v, v, S("gmlp_g", k), v_rs, ALU.mult, ALU.mult))
                ts(v, v, S("gmlp_b", k), None, ALU.add).then_inc(sem("gmlp_v_ready"), 1)
            for g in range(4):
                filled(dve, "mixed", g)
                tt(p2(AU + g), p2(AU + g), PSB[bank_of("mixed", g)], ALU.mult).then_inc(freed("mixed", g), 1)
                emptied(dve, "mixed", g)
                split(ys[0], g, "y0_ready")
            bt, et, qk = [[A(o + m * T) for m in range(2)] for o in (l_B, l_E, l_QK)]
            for m in range(2):
                filled(dve, "forget", m)
                ts(bt[m], PSB[bank_of("forget", m)], S("b_gate", m), None, ALU.add).then_inc(freed("forget", m), 1)
                emptied(dve, "forget", m)
                link(ts(et[m], bt[m], -1.0))
                tt(et[m], et[m], bt[m], ALU.min).then_inc(sem("forget_abs"), 1)
            for m in range(2):
                dve.wait_ge(sem("forget_exp"), m + 1)
                log1p(qk[0], et[m], qk[1], v_tmp)
                link(ts(bt[m], bt[m], -1.0, 0.0, ALU.mult, ALU.max))
                link(stt(bt[m], qk[0], 2.0, bt[m], ALU.mult, ALU.add))
                link(ts(et[m], bt[m], -1.0 / 16))
                link(V.tensor_tensor_scan(bt[m], C("carry128"), et[m], 0.0, ALU.mult, ALU.add))
            for m in range(2):
                emptied(dve, "p2", GQ + m)
                ts(p2(GQ + m), p2(GQ + m), 0.125).then_inc(sem("level_ready"), 1)
            dve.wait_ge(sem("level_ready"), 2)

            def merge_level(lv):
                mask = C("ident" if lv == 0 else f"level{lv - 1}").bitcast(mybir.dt.int32)
                for hh in range(4):
                    filled(dve, ("attn", lv), hh)
                    V.copy_predicated(four(A(l_AT + hh * T)), rep4(mask), four(PSB[bank_of(("attn", lv), hh)]))\
                        .then_inc(freed(("attn", lv), hh), 1)

            def level_logs(lv):
                hw = 1 << (lv - 1)
                v4 = lambda a: a.rearrange("p (b u h) -> p b u h", u=2, h=hw)
                for m in range(2):
                    b, e = v4(bt[m]), v4(et[m])
                    mid = b[:, :, 0, hw - 1:hw].to_broadcast([P, T // (2 * hw), hw])
                    link(tt(e[:, :, 1, :], b[:, :, 1, :], mid, ALU.subtract))
                    tt(e[:, :, 0, :], mid, b[:, :, 0, :], ALU.subtract).then_inc(sem("log_decay_ready"), 1)

            for lv in range(1, 8):
                hw = 1 << (lv - 1)
                v4 = lambda a: a.rearrange("p (b u h) -> p b u h", u=2, h=hw)
                level_logs(lv)
                if lv == 1:
                    filled(dve, ("attn", 0), 0)
                    link(V.memset(A(l_AT, 2048), 0.0))
                merge_level(lv - 1)
                for m in range(2):
                    dve.wait_ge(sem("decay_ready"), 2 * (lv - 1) + m + 1)
                    emptied(dve, "p2", GK + m)
                    e, q_, k_, o = v4(et[m]), v4(p2(GQ + m)), v4(p2(GK + m)), v4(qk[m])
                    link(tt(o[:, :, 1, :], e[:, :, 1, :], q_[:, :, 1, :], ALU.mult))
                    tt(o[:, :, 0, :], e[:, :, 0, :], k_[:, :, 0, :], ALU.mult).then_inc(sem("level_ready"), 1)
            merge_level(7)

            def invert_rows(what, rs):
                filled(dve, what)
                ts(rs, PSB[bank_of(what)][:, 0:rs.shape[1]], 1.0 / P, 1e-6, ALU.mult, ALU.add).then_inc(freed(what), 1)
                emptied(dve, what)
                V.reciprocal(rs, rs).then_inc(sem("row_inverted"), 1)

            c4 = lambda a: a.rearrange("p (c t) -> p c t", c=NT)
            for m in range(2):
                last = c4(bt[m])[:, :, P - 1:P].to_broadcast([P, NT, P])
                tt(c4(qk[m]), last, c4(bt[m]), ALU.subtract).then_inc(sem("log_decay_ready"), 1)
            for m in range(2):
                dve.wait_ge(sem("decay_ready"), 14 + 2 * m + 2)
                tt(qk[m], qk[m], p2(GK + m), ALU.mult).then_inc(sem("khat_ready"), 1)
            for m in range(2):
                st = A(l_ST + m * 384, 384)
                filled(dve, "gla_state", m)
                pst = PSB[bank_of("gla_state", m)]
                link(V.tensor_copy(st[:, 0:P], pst[:, 0:P]))
                for t in range(1, 3):
                    last = stt(st[:, t * P:(t + 1) * P], st[:, (t - 1) * P:t * P], et[m][:, t * P + P - 1:t * P + P],
                               pst[:, t * P:(t + 1) * P], ALU.mult, ALU.add)
                    if t == 1:
                        link(last)
                    else:
                        last.then_inc(freed("gla_state", m), 1)
                        emptied(dve, "gla_state", m)
                tt(et[m], et[m], p2(GQ + m), ALU.mult).then_inc(sem("gla_states_ready"), 1)
            invert_rows("sum_qk", row_rs[1])
            invert_rows("sum_gla", row_rs[0])
            link(ts(qg[:, :], S("q_g"), float(P) ** -0.5))
            for i in range(8):
                t = p2(DQ + i)
                filled(dve, "qk_rs", i)
                stt(t, t, qg[:, :] if i < 4 else S("k_g"), PSB[bank_of("qk_rs", i)], ALU.mult, ALU.mult)\
                    .then_inc(freed("qk_rs", i), 1)
            for hh in range(4):
                filled(dve, "gla_rs", hh)
                emptied(dve, "gla_o", hh)
                o = p2(GQ + hh)
                stt(o, o, S("gla_g"), PSB[bank_of("gla_rs", hh)], ALU.mult, ALU.mult)\
                    .then_inc(freed("gla_rs", hh), 1)
                emptied(dve, "gla_rs", hh)
                tt(p2(GR + hh), o, p2(GR + hh), ALU.mult).then_inc(sem("gla_out_ready"), 1)

            def gate_branch(n, m):
                g = sig[n][m % len(sig[n])]
                emptied(dve, ("gates", n), m)
                filled(dve, ("branch", n), m)
                up_ = PSB[bank_of(("branch", n), m)]
                o = A(MG + m * T)
                if n == 0:
                    tt(o, g, up_, ALU.mult).then_inc(freed(("branch", n), m), 1)
                else:
                    tt(g, g, up_, ALU.mult).then_inc(freed(("branch", n), m), 1)
                    emptied(dve, ("branch", n), m)
                    tt(o, o, g, ALU.add).then_inc(sem("merged"), 1)
                    if n == 2:
                        dve.wait_ge(sem("merged"), KT + m + 1)
                        split(merged2, m, "merged_split")

            ma = [A(d_MA + P * (t * (t + 1) // 2), (t + 1) * P) for t in range(NT)]
            sc = [None] + [A(d_SC + (0, 256, 640)[t - 1], (t + 1) * P) for t in range(1, NT)]
            link(V.tensor_copy(ma[0], C("neg128")))
            emptied(dve, "iw")
            for t in range(1, NT):
                n = (t + 1) * P
                for hh in range(4):
                    i = 4 * (t - 1) + hh
                    emptied(dve, ("index", t), hh)
                    r_, w_ = A(d_RL[i % 2], n), iw[:, t * 4 + hh:t * 4 + hh + 1]
                    if hh == 0:
                        ts(sc[t], r_, w_).then_inc(sem("relu_used"), 1)
                    else:
                        stt(sc[t], r_, w_, sc[t], ALU.mult, ALU.add).then_inc(sem("relu_used"), 1)
                    dve.wait_ge(sem("relu_used"), i + 1)
                link(tt(sc[t][:, t * P:n], sc[t][:, t * P:n], C("neg128"), ALU.add))
            topk = sem("topk_step")
            for r in range(16):
                for t in range(1, NT):
                    if r:
                        dve.wait_ge(topk, 6 * r - 3 + t)
                    V.max(top8[:, 8 * t - 8:8 * t], sc[t]).then_inc(topk, 1)
                for t in range(1, NT):
                    dve.wait_ge(topk, 6 * r + t)
                    V.match_replace(sc[t], top8[:, 8 * t - 8:8 * t], sc[t], -3e38).then_inc(topk, 1)
                if r in GATE_ROUNDS:
                    gate_branch(0, GATE_ROUNDS.index(r))
            for t in range(1, NT):
                dve.wait_ge(topk, 6 * 15 + 3 + t)
                link(ts(ma[t], sc[t], -3e38, -1e30, ALU.is_gt, ALU.mult))

            def masked(i):
                hh, t = i // 4, i % 4
                n = (t + 1) * P
                lg = A(d_LG + (i % 2) * T, n)
                filled(dve, ("logits", hh), t)
                if i >= 2:
                    filled(dve, "pt", i - 2)
                tt(lg, PSB[bank_of(("logits", hh), t)][:, 0:n], ma[t], ALU.add).then_inc(freed(("logits", hh), t), 1)
                emptied(dve, ("logits", hh), t)
                V.tensor_reduce(nmax[:, i % 4:i % 4 + 1], lg, AX.X, ALU.max, negate=True).then_inc(sem("logits_ready"), 1)

            filled(dve, ("branch", 0), KT - 1)
            for k in range(4):
                dve.wait_ge(sem("gla_out_ready"), k + 1)
                split(ys[1], k, "y1_ready")
            masked(0)
            for i in range(16):
                t = i % 4
                if i + 1 < 16:
                    masked(i + 1)
                dve.wait_ge(sem("exp_ready"), i + 1)
                lg = A(d_LG + (i % 2) * T, (t + 1) * P)
                link(V.reciprocal(rinv[:, t:t + 1], rsum[:, t:t + 1]))
                ts(lg, lg, rinv[:, t:t + 1]).then_inc(sem("probs_ready"), 1)
                if t == 3:
                    gate_branch(1, i // 4 * 2)
                elif t == 0 and i:
                    gate_branch(1, i // 4 * 2 - 1)
                if i in (10, 14):
                    emptied(dve, "dsa_y", i // 4 - 2)
                    split(ys[2], i // 4 - 2, "y2_ready")
            emptied(dve, "dsa_y", 2)
            split(ys[2], 2, "y2_ready")
            emptied(dve, "dsa_y", 3)
            split(ys[2], 3, "y2_ready")
            gate_branch(1, KT - 1)
            for m in range(KT):
                gate_branch(2, m)
            for m in range(KT):
                filled(dve, "mix2", m)
                stt(x_(m), PSB[bank_of("mix2", m)], mod[:, 16 + m:17 + m], x_(m), ALU.mult, ALU.add)\
                    .then_inc(freed("mix2", m), 1)
            rstd("sum_2", 1.0 / D, 1e-6)
            modulated(in_ff, 32, 24, "g2", "h2_ready")

            filled(dve, "route")
            lg = rt_l.rearrange("p (t c) -> p t c", t=NT)
            tt(lg, PSB[bank_of("route")][:, 0:80].rearrange("p (t c) -> p t c", t=NT), rep4(S("b_route", 0, 20)), ALU.add)\
                .then_inc(freed("route"), 1)
            emptied(dve, "route")
            ex, oh, sel, h1, h2 = [w.rearrange("p (t c) -> p t c", t=NT) for w in rt_w]
            mx, pg, none, v1, ev, w1, w2_, v2 = rt_s
            each = lambda a: a.unsqueeze(2).to_broadcast([P, NT, 4])

            def first_of(hot, vals, top):
                link(tt(hot, vals, each(top), ALU.is_equal))
                link(ts(none, hot[:, :, 0], -1.0, 1.0, ALU.mult, ALU.add))
                for c in range(1, 4):
                    link(tt(hot[:, :, c], hot[:, :, c], none, ALU.mult))
                    link(tt(none, none, hot[:, :, c], ALU.subtract))

            link(V.tensor_reduce(mx, lg[:, :, 0:4], AX.X, ALU.max))
            tt(ex, lg[:, :, 0:4], each(mx), ALU.subtract).then_inc(sem("route_diff"), 1)
            first_of(oh, lg[:, :, 0:4], mx)
            for g in range(4):
                part = lg[:, :, 4 + 4 * g:8 + 4 * g]
                hot = oh[:, :, g:g + 1].to_broadcast([P, NT, 4])
                if g == 0:
                    link(tt(sel, part, hot, ALU.mult))
                else:
                    link(tt(h1, part, hot, ALU.mult))
                    link(tt(sel, sel, h1, ALU.add))
            link(V.tensor_reduce(v1, sel, AX.X, ALU.max))
            first_of(h1, sel, v1)
            link(stt(sel, h1, -3e38, sel, ALU.mult, ALU.add))
            link(V.tensor_reduce(v2, sel, AX.X, ALU.max))
            first_of(h2, sel, v2)
            tt(ev, v2, v1, ALU.subtract).then_inc(sem("route_diff"), 1)
            dve.wait_ge(sem("route_exp"), 1)
            link(V.tensor_reduce(pg, ex, AX.X, ALU.add))
            dve.wait_ge(sem("route_exp"), 2)
            link(ts(w1, ev, 1.0, None, ALU.add))
            link(tt(w1, w1, pg, ALU.mult))
            link(V.reciprocal(w1, w1))
            link(tt(w2_, w1, ev, ALU.mult))
            link(tt(h1, h1, each(w1), ALU.mult))
            link(tt(h2, h2, each(w2_), ALU.mult))
            link(tt(h1, h1, h2, ALU.add))
            cm = rt_c.rearrange("p (t g c) -> p t g c", t=NT, g=4)
            for g in range(4):
                last = tt(cm[:, :, g, :], h1, oh[:, :, g:g + 1].to_broadcast([P, NT, 4]), ALU.mult)
            last.then_inc(sem("combine_ready"), 1)
            link(V.memset(A(F_ACC, 4096), 0.0))

            def expert_gate(j, phase, sub, it=None):
                off = at(j, T, F_CMB)
                cw = arena[:, bass.ds(off, T)] if it is not None else A(off)
                for i in range(2):
                    g = A(F_UB + i * T)
                    emptied(dve, "moe_up", (phase, sub, i), it)
                    filled(dve, "moe_up", (phase, sub, 2 + i), it)
                    if j == 0 and i == 0:
                        for e in range(NE - 4, NE):
                            emptied(dve, "weights", e)
                    tt(g, g, PSB[2 + i], ALU.mult).then_inc(freed("moe_up", (phase, sub, 2 + i)), 1)
                    emptied(dve, "moe_up", (phase, sub, 2 + i), it)
                    link(tt(acts.raw(2 * sub + i), g, cw, ALU.mult))
                    split(acts, 2 * sub + i, "moe_act_ready")

            expert_gate(0, "first", 0)
            with dve.Fori(0, (NE - 1) // 2) as it:
                ch.enter(it, 8)
                expert_gate((it, 1), "loop", 1, it)
                accumulate("moe", "loop", 0, it)
                expert_gate((it, 2), "loop", 0, it)
                accumulate("moe", "loop", 1, it)
            ch.leave((NE - 1) // 2)
            expert_gate(NE - 1, "last", 1)
            accumulate("moe", "last", 0)
            accumulate("moe", "last", 1)
            for m in range(4, 8):
                emptied(dve, "moe_down", ("last", 1, m))
            for k in range(KT):
                stt(x_(k), acc(k), mod[:, 40 + k:41 + k], x_(k), ALU.mult, ALU.add).then_inc(sem("out_ready"), 1)


        @block.gpsimd
        def _(pool):
            ch = Chain(pool, "pool_step")
            unit, chunk = [0], [0]

            def unit_loaded(u, it=None, per=0):
                v = 16 * (u // RING + 1)
                pool.wait_ge(sem(f"weights{u % RING}_loaded"), v if it is None else it * (16 * per // RING) + v)

            def unit_begun(u, it=None, per=0):
                pool.wait_ge(sem("weights_used"), u + 1 if it is None else it * per + (u + 1))

            def split_unit(weights, i, it=None):
                u, q = unit[0] + i, chunk[0] + 2 * i
                unit_loaded(u, it, 2)
                for c in range(2):
                    if i:
                        pool.wait_ge(sem("split_used"), q + c if it is None else it * 4 + (q + c))
                    raw = ring[:, u % RING, c * CHUNK:(c + 1) * CHUNK]
                    hi, lo = weights.slot(q + c)
                    if it is not None:
                        pool.sem_inc(sem("chunk_waited"), 1)
                    first = nc.gpsimd.tensor_scalar(hi, raw, 1.0, 1.0, ALU.mult, ALU.mult)
                    if c == 0:
                        first.then_inc(sem("weights_used"), 1)
                        unit_begun(u, it, 2)
                    else:
                        ch.link(first)
                    nc.gpsimd.tensor_tensor(lo, raw, hi.bitcast(F32), ALU.subtract).then_inc(sem("split_ready"), 1)

            def split_units(weights, n):
                split_unit(weights, 0)
                times = (n - 1) // 2
                with pool.Fori(0, times) as it:
                    ch.enter(it, 2)
                    split_unit(weights, 1, it)
                    split_unit(weights, 2, it)
                ch.leave(times)
                if n % 2 == 0:
                    split_unit(weights, n - 1)
                unit[0] += n
                chunk[0] += 2 * n

            def multiply_mod(it=None):
                for i in range(MOD_BATCH):
                    u = unit[0] + i
                    unit_loaded(u, it, MOD_BATCH)
                    w = ring[:, u % RING, :].rearrange("p (k c) -> p k c", k=KT)
                    nc.gpsimd.tensor_tensor(w, w, csil[:, :].unsqueeze(2).to_broadcast([P, KT, 256]), ALU.mult)\
                        .then_inc(sem("weights_used"), 1)
                    unit_begun(u, it, MOD_BATCH)
                    ch.link(nc.gpsimd.tensor_tensor(w[:, 0:4], w[:, 0:4], w[:, 4:8], ALU.add))
                    ch.link(nc.gpsimd.tensor_tensor(w[:, 0:2], w[:, 0:2], w[:, 2:4], ALU.add))
                    nc.gpsimd.tensor_tensor(mod_part(i), w[:, 0], w[:, 1], ALU.add).then_inc(sem("mod_part_ready"), 1)

            split_units(w_in1, 14)

            pool.wait_ge(sem("csil_ready"), 1)
            pool.wait_ge(sem("ssd_out_ready"), 4)
            pool.wait_ge(sem("sg_ready"), 1)
            with pool.Fori(0, 3) as b:
                ch.enter(b, 2 * MOD_BATCH)
                multiply_mod(b)
                pool.wait_ge(sem("mod_parts_used"), b + 1)
            ch.leave(3)
            unit[0] += 3 * MOD_BATCH
            multiply_mod()
            unit[0] += MOD_BATCH

            filled(pool, ("hh", 3), 3)
            split_units(w_out1, 4)
            filled(pool, "mix", KT - 1)
            split_units(w_ff, 3 * NF)
            filled(pool, "ffn_down", ("last", 0, KT - 1))
            split_units(w_in2, 18)
            pool.wait_ge(sem("gla_out_ready"), 4)
            split_units(w_br[0], 2 * 6)
            filled(pool, "dsa_y", 3)
            split_units(w_br[2], 6 + 4)
            filled(pool, "mix2", KT - 1)
            nc.gpsimd.tensor_scalar(route_hi[:, :], M("w_route"), 1.0, 1.0, ALU.mult, ALU.mult)\
                .then_inc(sem("route_split"), 1)
            pool.wait_ge(sem("route_split"), 1)
            nc.gpsimd.tensor_tensor(route_lo[:, :], M("w_route"), route_hi[:, :].bitcast(F32), ALU.subtract)\
                .then_inc(sem("route_split"), 1)
            split_units(w_ff, 3 * NE)

        @block.sync
        def _(sp):
            n_units = units.shape[0]
            for t in range(NT):
                sp.dma_start(A(XT + t * D, D), x[t * P:(t + 1) * P, :]).then_inc(sem("x_loaded"), 16)
            for u in range(RING):
                sp.dma_start(ring[:, u, :], units[u, :, :]).then_inc(sem(f"weights{u}_loaded"), 16)
            whole = n_units // RING - 1
            with sp.Fori(0, whole) as i:
                for j in range(RING):
                    sp.wait_ge(sem("weights_used"), RING * i + j + 2)
                    sp.dma_start(ring[:, j, :], units[bass.ds(RING * i + RING + j, 1), :, :].rearrange("a p n -> (a p) n"))\
                        .then_inc(sem(f"weights{j}_loaded"), 16)
            for u in range(RING * (whole + 1), n_units):
                sp.wait_ge(sem("weights_used"), u - RING + 2)
                sp.dma_start(ring[:, u % RING, :], units[u, :, :]).then_inc(sem(f"weights{u % RING}_loaded"), 16)
            for i in range(8):
                emptied(sp, "out", i)
                sp.dma_start(out[(i // 2) * P:(i // 2 + 1) * P, (i % 2) * T:(i % 2 + 1) * T], A(OUT + i * T))\
                    .then_inc(sem("out_stored"), 16)
            sp.wait_ge(sem("out_stored"), 8 * 16)


def _columns(v):
    v = np.asarray(v).reshape(-1)
    pad = -len(v) % P
    return np.pad(v, (0, pad)).reshape(-1, P).T


def _units_1024(w):
    return w.reshape(KT, P, -1, 2, P).transpose(2, 1, 3, 0, 4).reshape(-1, P, UNIT)


def _units_down(w):
    return w.reshape(-1, 2, P, 2, T).transpose(0, 2, 3, 1, 4).reshape(-1, P, UNIT)


def _rwkv_tiles(a):
    r, w, k, v, lo, g = np.split(a, np.cumsum([512, 64, 512, 512, 64]), axis=-1)
    return np.concatenate([w, lo, g, r, k, v], axis=-1)


def _constants():
    f = np.float32
    s, t = np.arange(P)[:, None], np.arange(P)[None, :]
    out = {"ident": s == t, "ones": np.ones((P, P)), "blk64": s // CH == t // CH, "flip": s + t == P - 1,
           "strict64": (s < t) & (s // CH == t // CH), "incl64": (s <= t) & (s // CH == t // CH),
           "incl128": s <= t, "neg128": np.where(s >= t, 0.0, -1e30)}
    for k in range(7):
        h = 1 << k
        out[f"level{k}"] = (s // (2 * h) == t // (2 * h)) & (s % (2 * h) < h) & (t % (2 * h) >= h)
    out["level0t"] = out["level0"].T
    n = np.arange(T)[None, :] + np.zeros((P, 1))
    out["carry64"], out["carry128"] = n % CH != 0, n % P != 0
    c = np.arange(NE * P)[None, :]
    out["sel16"] = (c // P == s) & (s < NE)
    m = np.arange(2 * T)
    d = 511 - m
    large = np.minimum(16 + (np.log(np.maximum(d, 16) / 16.0) / np.log(8.0) * 16 + 1e-9).astype(np.int64), 31)
    bucket = np.where(d < 16, d, large)
    out["bucket"] = (bucket[None, :] == s) & (d >= 0)[None, :]
    return np.concatenate([np.broadcast_to(out[k], (P, w)).astype(f) for k, (_, w) in CONSTS.items()], 1)


def _prepare(i):
    i = {k: np.asarray(v) for k, v in i.items()}
    z = lambda r, c: np.zeros((r, c), np.float32)
    w = i["w_in"][0]
    zc, xbc, dtc, rw = np.split(w, [512, 1536, 1544], axis=1)
    cols = np.concatenate([xbc, dtc, z(D, P - 8), _rwkv_tiles(rw), zc, z(D, P)], 1)
    order = np.concatenate
    w2 = i["w_in_2"][0]
    a_u, a_v, g_q, g_k, g_v, g_r, g_a, d_q, d_k, d_v, d_iq, d_ik, d_iw, gates = np.split(
        w2, np.cumsum([512, 512, 256, 256, 512, 512, 16, 512, 512, 512, 256, 64, 4]), axis=1)
    cols2 = order([a_u, a_v, g_q, g_k, g_v, g_r, g_a, z(D, 16), d_iw, z(D, 92), d_q, d_k, d_v, d_iq, d_ik, d_ik], 1)
    up = i["ffn_w_up"][0]
    gu, vu = _units_1024(up[:, :D_FF]), _units_1024(up[:, D_FF:])
    down = _units_down(i["ffn_w_down"][0])
    eg = np.concatenate([_units_1024(i["w_exp_gate_2"][0, e]) for e in range(NE)])
    eu = np.concatenate([_units_1024(i["w_exp_up_2"][0, e]) for e in range(NE)])
    ed = _units_down(i["w_exp_down_2"][0])

    def steps(g, v, d):
        out = [g[0], v[0]]
        for k in range(1, len(g)):
            out += [g[k], v[k], d[k - 1]]
        return np.stack(out + [d[-1]])

    w_mod = i["w_mod_2"][0].reshape(KT, P, N_MOD, 256).transpose(2, 1, 0, 3).reshape(N_MOD, P, UNIT)
    branch = []
    gate_chunks = _units_1024(gates).reshape(-1, P, 2, CHUNK).transpose(0, 2, 1, 3).reshape(24, P, CHUNK)
    for n in range(3):
        b = i["w_branch_2"][0, n].reshape(4, P, 4, 256).transpose(2, 1, 0, 3).reshape(4, P, CHUNK)
        for q in range(4):
            branch += [b[q], gate_chunks[8 * n + 2 * q], gate_chunks[8 * n + 2 * q + 1]]
    branch = np.stack(branch).reshape(-1, 2, P, CHUNK).transpose(0, 2, 1, 3).reshape(-1, P, UNIT)
    units = order([_units_1024(cols), w_mod, _units_1024(i["w_out"][0]), steps(gu, vu, down),
                   _units_1024(cols2), branch, _units_1024(i["w_out_2"][0]), steps(eg, eu, ed)])
    mu = _rwkv_tiles(i["rwkv_mu"][0])
    fc = order([i["ffn_conv_w"][0], i["ffn_conv_b"]], 0)
    fc = fc.reshape(4, 2, NF, 2, P).transpose(4, 2, 1, 3, 0).reshape(P, 16 * NF)
    small = {
        "g_pre_mix": i["pre_mix_norm"], "g_post_mix": i["post_mix_norm"], "g_pre_ffn": i["pre_ffn_norm"],
        "g_post_ffn": i["post_ffn_norm"], "conv_w": i["ssd_conv_w"][0], "conv_b": i["ssd_conv_b"],
        "dt_bias": i["ssd_dt_bias"], "a_log": i["ssd_a_log"], "d_skip": np.repeat(i["ssd_d"][0], CH),
        "ssd_norm": i["ssd_norm"], "mu": mu, "w0": i["rwkv_w0"], "a0": i["rwkv_a0"], "k_k": i["rwkv_k_k"],
        "k_a": i["rwkv_k_a"], "r_k": i["rwkv_r_k"], "ln_w": i["rwkv_ln_w"], "ln_b": i["rwkv_ln_b"],
        "c": i["c_2"], "b_mod": i["b_mod_2"], "g1": i["g_norm1_2"], "g2": i["g_norm2_2"],
        "gmlp_g": i["gmlp_ln_g_2"], "gmlp_b": i["gmlp_ln_b_2"], "b_gate": i["gla_b_gate_2"],
        "gla_g": i["gla_norm_g_2"], "q_g": i["dsa_qnorm_g_2"], "k_g": i["dsa_knorm_g_2"],
        "b_branch": i["b_branch_gate_2"]}
    small = {k: _columns(v) for k, v in small.items()}
    small["b_route"] = np.broadcast_to(order([i["b_group_2"][0], i["b_router_2"][0]])[None], (P, 20))
    small["rel_bias"] = np.pad(i["rel_bias_2"], ((0, P - 32), (0, 0)))
    small["ffn_conv"] = fc
    for k, (_, n) in SMALL.items():
        assert small[k].shape == (P, n), (k, small[k].shape)
    route = order([i["w_group_2"][0], i["w_router_2"][0]], 1)
    mats = {"wa2": order([i["rwkv_w2"][0], i["rwkv_a2"][0]]), "g2m": i["rwkv_g2"][0],
            "gate2": np.pad(i["gla_w_gate2_2"][0], ((0, P - 16), (0, 0))),
            "w_s": i["gmlp_w_s_2"][0].transpose(1, 0, 2).reshape(P, 4 * P),
            "b_s": np.pad(i["gmlp_b_s_2"][0].reshape(1, T), ((0, P - 1), (0, 0))),
            "w_route": np.pad(route.reshape(KT, P, 20).transpose(1, 0, 2).reshape(P, KT * 20), ((0, 0), (0, P - 16)))}
    fixed = order([_constants()] + [small[k] for k in SMALL] + [mats[k] for k in MATS], 1)
    return {"units": np.ascontiguousarray(units), "fixed": np.ascontiguousarray(fixed, dtype=np.float32),
            "x": np.ascontiguousarray(i["x"][0])}


def kernel(**inputs):
    import concourse.bacc as bacc
    from concourse.bass_utils import run_bass_kernel_spmd

    nc = bacc.Bacc("TRN2", target_bir_lowering=False, num_devices=1)
    arrays = _prepare(inputs)
    aps = [nc.dram_tensor(k, v.shape, F32, kind="ExternalInput").ap() for k, v in arrays.items()]
    skew = nc.dram_tensor("bias_rows", (4, 2 * T), F32, kind="Internal").ap()
    out = nc.dram_tensor("out", (T, D), F32, kind="ExternalOutput").ap()
    build(nc, *aps, skew, out)
    r = run_bass_kernel_spmd(nc, [arrays], core_ids=[0])
    return r.results[0]["out"].reshape(1, T, D)
```
